# Optimizing a Trainium2 kernel written in Bass

```python
import math
import jax, jax.numpy as jnp
from jax import lax
import numpy as np

D_MODEL = 2048
BATCH = 1
SEQ = 256
DEPTH = 2
DEC_BATCH = 8
DEC_SEQ = 8
PAST_LEN = 2048
PAGE_SIZE = 128

N_MIXERS = 2
N_RET_LAYERS = (DEPTH + 1) // 2
N_CONV_LAYERS = DEPTH // 2
N_META = 16
RET_HEADS = 8
RET_DK = D_MODEL // RET_HEADS
RET_DV = 2 * RET_DK
RET_QK = RET_HEADS * RET_DK
RET_V = RET_HEADS * RET_DV
CHUNK = 128
CONV_WIDTH = 3
CONV_E = D_MODEL
ROPE_BASE = 10000.0
LN_EPS = 1e-5
GN_EPS = 1e-6
DEEPNORM_ALPHA = (2.0 * DEPTH) ** 0.25
DEEPNORM_BETA = (8.0 * DEPTH) ** -0.25

kernel_name = "retnet_shortconv_hybrid_step"

def _decay_log():
    return jnp.log1p(-jnp.exp2(-5.0 - jnp.arange(RET_HEADS, dtype=jnp.float32)))

def layer_norm(x, g, b):
    xf = x.astype(jnp.float32)
    mu = jnp.mean(xf, axis=-1, keepdims=True)
    var = jnp.mean(jnp.square(xf - mu), axis=-1, keepdims=True)
    y = (xf - mu) * lax.rsqrt(var + LN_EPS)
    return (y * g.astype(jnp.float32) + b.astype(jnp.float32)).astype(x.dtype)

def rotary(t, pos):
    half = t.shape[-1] // 2
    freqs = ROPE_BASE ** (-jnp.arange(half, dtype=jnp.float32) * 2.0 / t.shape[-1])
    ang = pos.astype(jnp.float32)[:, None] * freqs[None, :]
    cos = jnp.cos(ang).astype(t.dtype)
    sin = jnp.sin(ang).astype(t.dtype)
    t1, t2 = t[..., :half], t[..., half:]
    return jnp.concatenate([t1 * cos - t2 * sin, t1 * sin + t2 * cos], axis=-1)

def retention_chunk(q, k, v, S):
    dt = q.dtype
    L = q.shape[2]
    lg = _decay_log()
    idx = jnp.arange(L, dtype=jnp.float32)
    diff = idx[:, None] - idx[None, :]
    dmask = jnp.exp(jnp.where(diff[None] >= 0, diff[None] * lg[:, None, None], -jnp.inf)).astype(dt)
    q_decay = jnp.exp((idx + 1.0)[None, :] * lg[:, None]).astype(dt)
    k_decay = jnp.exp((L - 1.0 - idx)[None, :] * lg[:, None]).astype(dt)
    s_decay = jnp.exp(L * lg).astype(dt)
    scores = jnp.einsum('bhld,bhmd->bhlm', q, k) * dmask
    out = (jnp.einsum('bhlm,bhmv->bhlv', scores, v)
           + jnp.einsum('bhld,bhdv->bhlv', q, S) * q_decay[:, :, None])
    S_new = S * s_decay[:, None, None] + jnp.einsum('bhmd,bhmv->bhdv', k * k_decay[:, :, None], v)
    return out, S_new

def retention_prompt(q, k, v):
    B = q.shape[0]
    S0 = jnp.zeros((B, RET_HEADS, RET_DK, RET_DV), q.dtype)
    out_meta, S = retention_chunk(q[:, :, :N_META], k[:, :, :N_META], v[:, :, :N_META], S0)

    def to_chunks(t):
        t = t[:, :, N_META:]
        b, h, l, d = t.shape
        return t.reshape(b, h, l // CHUNK, CHUNK, d).transpose(2, 0, 1, 3, 4)

    def step(S, qkv):
        qc, kc, vc = qkv
        o, S = retention_chunk(qc, kc, vc, S)
        return S, o

    S, outs = lax.scan(step, S, (to_chunks(q), to_chunks(k), to_chunks(v)))
    outs = outs.transpose(1, 2, 0, 3, 4).reshape(B, RET_HEADS, -1, RET_DV)
    return jnp.concatenate([out_meta, outs], axis=2), S

def retention_layer(h, pos, w_in, w_out, state):
    B, L, _ = h.shape
    proj = h @ w_in
    q, k, v, g = jnp.split(proj, [RET_QK, 2 * RET_QK, 2 * RET_QK + RET_V], axis=-1)
    q = q.reshape(B, L, RET_HEADS, RET_DK).transpose(0, 2, 1, 3)
    k = k.reshape(B, L, RET_HEADS, RET_DK).transpose(0, 2, 1, 3)
    v = v.reshape(B, L, RET_HEADS, RET_DV).transpose(0, 2, 1, 3)
    q = rotary(q, pos) * jnp.asarray(RET_DK ** -0.5, q.dtype)
    k = rotary(k, pos)
    if state is None:
        y, S_new = retention_prompt(q, k, v)
    else:
        y, S_new = retention_chunk(q, k, v, state.astype(q.dtype))
    yf = y.astype(jnp.float32)
    mu = jnp.mean(yf, axis=-1, keepdims=True)
    var = jnp.mean(jnp.square(yf - mu), axis=-1, keepdims=True)
    yn = ((yf - mu) * lax.rsqrt(var + GN_EPS)).astype(h.dtype)
    yn = yn.transpose(0, 2, 1, 3).reshape(B, L, RET_V)
    return (jax.nn.silu(g) * yn) @ w_out, S_new

def conv_layer(h, w_in, conv_w, w_out, state):
    L = h.shape[1]
    proj = h @ w_in
    b_gate, c_gate, v, z = jnp.split(proj, 4, axis=-1)
    u = c_gate * v
    if state is None:
        up = jnp.pad(u, ((0, 0), (CONV_WIDTH - 1, 0), (0, 0)))
    else:
        up = jnp.concatenate([state.astype(u.dtype), u], axis=1)
    conv = sum(conv_w[j] * up[:, j:j + L] for j in range(CONV_WIDTH))
    new_state = up[:, -(CONV_WIDTH - 1):]
    return (jax.nn.silu(z) * b_gate * conv) @ w_out, new_state

def setup_inputs(seed: int = 0) -> dict:
    key = jax.random.key(seed)
    ks = jax.random.split(key, 13)
    f32 = jnp.float32
    x_prompt = jax.random.normal(ks[0], (BATCH, SEQ, D_MODEL), f32)
    x_sample = jax.random.normal(ks[1], (DEC_BATCH, DEC_SEQ, D_MODEL), f32)
    gam = 1.0 - np.exp2(-5.0 - np.arange(RET_HEADS, dtype=np.float32))
    s_scale = jnp.asarray((1.0 / (1.0 - gam)) ** 0.5, f32)[None, None, :, None, None]
    state_ret = jax.random.normal(ks[2], (N_RET_LAYERS, DEC_BATCH, RET_HEADS, RET_DK, RET_DV), f32) * s_scale
    state_conv = jax.random.normal(ks[3], (N_CONV_LAYERS, DEC_BATCH, CONV_WIDTH - 1, CONV_E), f32)
    meta = jax.random.normal(ks[4], (N_META, D_MODEL), f32)
    w_ret_in = jax.random.normal(ks[5], (N_RET_LAYERS, D_MODEL, 2 * RET_QK + 2 * RET_V), f32) * D_MODEL ** -0.5
    w_ret_out = (jax.random.normal(ks[6], (N_RET_LAYERS, RET_V, D_MODEL), f32)
                 * (2.0 / (RET_V + D_MODEL)) ** 0.5 * DEEPNORM_BETA)
    w_conv_in = jax.random.normal(ks[7], (N_CONV_LAYERS, D_MODEL, 4 * CONV_E), f32) * D_MODEL ** -0.5
    conv_w = jax.random.normal(ks[8], (N_CONV_LAYERS, CONV_WIDTH, CONV_E), f32) * CONV_WIDTH ** -0.5
    w_conv_out = (jax.random.normal(ks[9], (N_CONV_LAYERS, CONV_E, D_MODEL), f32)
                  * (2.0 / (CONV_E + D_MODEL)) ** 0.5 * DEEPNORM_BETA)
    ln_g = 1.0 + 0.02 * jax.random.normal(ks[10], (DEPTH, D_MODEL), f32)
    ln_b = 0.02 * jax.random.normal(ks[11], (DEPTH, D_MODEL), f32)
    return {"x_prompt": x_prompt, "x_sample": x_sample, "state_ret": state_ret, "state_conv": state_conv,
            "meta": meta, "w_ret_in": w_ret_in, "w_ret_out": w_ret_out, "w_conv_in": w_conv_in,
            "conv_w": conv_w, "w_conv_out": w_conv_out, "ln_g": ln_g, "ln_b": ln_b}

def reference(x_prompt, x_sample, state_ret, state_conv, meta, w_ret_in, w_ret_out,
              w_conv_in, conv_w, w_conv_out, ln_g, ln_b):
    B = x_prompt.shape[0]
    xp = jnp.concatenate(
        [jnp.broadcast_to(meta[None].astype(x_prompt.dtype), (B, N_META, D_MODEL)), x_prompt], axis=1)
    xs = x_sample
    pos_p = jnp.arange(N_META + x_prompt.shape[1], dtype=jnp.int32)
    pos_s = PAST_LEN + jnp.arange(x_sample.shape[1], dtype=jnp.int32)
    alpha = jnp.asarray(DEEPNORM_ALPHA, xp.dtype)
    ret_p, ret_s, conv_p, conv_s = [], [], [], []
    for i in range(DEPTH):
        j = i // N_MIXERS
        if i % N_MIXERS == 0:
            mp, sp = retention_layer(xp, pos_p, w_ret_in[j], w_ret_out[j], None)
            ms, ss = retention_layer(xs, pos_s, w_ret_in[j], w_ret_out[j], state_ret[j])
            ret_p.append(sp)
            ret_s.append(ss)
        else:
            mp, sp = conv_layer(xp, w_conv_in[j], conv_w[j], w_conv_out[j], None)
            ms, ss = conv_layer(xs, w_conv_in[j], conv_w[j], w_conv_out[j], state_conv[j])
            conv_p.append(sp)
            conv_s.append(ss)
        xp = layer_norm(alpha * xp + mp, ln_g[i], ln_b[i])
        xs = layer_norm(alpha * xs + ms, ln_g[i], ln_b[i])
    y_prompt = xp[:, N_META:]
    y_sample = xs
    return (y_prompt, y_sample, jnp.stack(ret_p), jnp.stack(ret_s), jnp.stack(conv_p), jnp.stack(conv_s))


_drawn_inputs = setup_inputs


def setup_inputs(seed=0):
    import zlib

    import numpy as np

    out = dict(_drawn_inputs(seed))
    spreads = {}
    factors = {}
    for name, (base, spread) in spreads.items():
        noise = np.random.default_rng([zlib.crc32(name.encode()), seed]).standard_normal(out[name].shape)
        drawn = base * np.exp(spread * noise) if base else spread * noise
        out[name] = __import__('jax').numpy.asarray(drawn.astype(out[name].dtype))
    for name, factor in factors.items():
        out[name] = (out[name] * factor).astype(out[name].dtype)
    return out
```

```python
import math
from contextlib import ExitStack

import numpy as np

import concourse.bass as bass
from concourse import mybir

F32 = mybir.dt.float32
F32R = mybir.dt.float32r
ALU = mybir.AluOpType
ACT = mybir.ActivationFunctionType

P = 128
D = 2048
KT = D // P
SEQ, META, NB, DSEQ, PAST = 256, 16, 8, 8, 2048
NSAMP = NB * DSEQ
PROMPT = META + SEQ
T = PROMPT + NSAMP
WIDTH = 3
CUT = META - (WIDTH - 1)
N = T - CUT
NOUT = N - (WIDTH - 1)
NP_ = PROMPT - CUT
HEADS, DK, DV = 8, 256, 512
DKB, DVB = DK // P, DV // P
ALPHA = float(np.float32(4.0 ** 0.25))
LN_EPS, GN_EPS = 1e-5, 1e-6

KEY = [(0, 128), (128, 128), (256, 80)]
QRY = [(0, 128 - CUT), (128 - CUT, 128), (256 - CUT, 80)]
SC = [(0, NP_), (128 - CUT, NP_ - (128 - CUT)), (256 - CUT, 80)]
A_AT = [0, NP_ + NSAMP, NP_ + NSAMP + SC[1][1] + NSAMP]
A_LEN = A_AT[2] + 80
M_AT = [0, SC[0][1], SC[0][1] + SC[1][1]]
QD_AT = M_AT[2] + SC[2][1]
KD_AT = QD_AT + NSAMP
TAB = KD_AT + T

HALF = 1024
CPH = 32
RAW = 4
SPL = 2
NE = KT
CPE = 8
HEAD_CH = HEADS * CPH
CONV_CH = NE * CPE
OUT_CH = KT * 2
ROWS_U = 10


KV_AT = {21: (0,), 22: (1,), 23: (2, 3), 24: (4,), 25: (5,), 26: (6,), 27: (7, 8), 28: (9,), 29: (10, 11),
         30: (12, 13), 31: (14, 15)}
KB_AT = {20: (0,), 21: (1,), 23: (2,), 24: (3,), 27: (4,), 28: (5,), 29: (6,), 30: (7,)}


class Count:

    def __init__(self, sem, per=1, credit=0):
        self.sem, self.per, self.credit = sem, per, credit

    def at(self, r, j=1):
        return r * self.per + (j + self.credit)


def hybrid_step(nc, x_t, w_head, w_conv, w_cout, s_in, tables, trig, consts, lnp, cw, cs_in,
                y_t, s_prompt, s_out, cs_out):
    ctx = ExitStack()
    with ctx:
        def sb(name, shape, dt=F32):
            return ctx.enter_context(nc.sbuf_tensor(name, [P] + shape, dt))

        def count(name, per=1, credit=0):
            return Count(ctx.enter_context(nc.semaphore(name)), per, credit)

        xh, xl = sb("x_hi", [KT, T], F32R), sb("x_lo", [KT, T], F32R)
        acc = sb("residual", [KT, T])
        w_raw = sb("w_raw", [RAW, HALF])
        w_hi, w_lo = sb("w_hi", [SPL, HALF], F32R), sb("w_lo", [SPL, HALF], F32R)
        con = sb("constants", [3 * P + 8])
        gate_touch = sb("table_touch", [1])
        lnt = sb("ln_params", [2, 2, KT])
        bank_p = [ctx.enter_context(nc.psum_tensor(f"proj{i}", [P, 512], F32)) for i in range(2)]
        bank_q = ctx.enter_context(nc.psum_tensor("qs", [P, 512], F32))
        bank_r = [ctx.enter_context(nc.psum_tensor(f"side{i}", [P, 512], F32)) for i in range(5)]
        ident, ones = con[:, 0:P], con[:, P:2 * P]
        fold_raw = con[:, 2 * P:2 * P + 80]
        row_mask = con[:, 3 * P:3 * P + 1]
        bmask = con[:, 3 * P + 1:3 * P + 5]

        ret = ExitStack()

        def rb(name, shape, dt=F32):
            return ret.enter_context(nc.sbuf_tensor(name, [P] + shape, dt))

        tr = rb("cos_sin", [2, T])
        tab = rb("head_table", [TAB])
        sdec = rb("state_decay", [HEADS])
        fold = rb("fold", [80], F32R)
        qkz = rb("qk_or_z", [2 * DVB * T], F32R)
        raws = rb("qk_raw_or_gate", [2 * DKB * T])
        tmp = rb("tmp", [2, T])
        vt_yn = rb("v_t_or_y_norm", [3 * DV])
        v_hi, v_lo = rb("v_hi", [3, DV], F32R), rb("v_lo", [3, DV], F32R)
        k_hi, k_lo = rb("k_hi", [3, DK], F32R), rb("k_lo", [3, DK], F32R)
        a_hi, a_lo = rb("a_hi", [A_LEN], F32R), rb("a_lo", [A_LEN], F32R)
        qz = rb("q_spread", [DKB, NB * 136], F32R)
        stage = rb("stack_t_or_fold", [(DKB + DVB) * 2 * P], F32R)
        k_st, v_st = rb("k_stack", [2, DK], F32R), rb("v_stack", [2, DV], F32R)
        k_b = rb("k_of_sample", [2, DK], F32R)
        sa = rb("state_for_q", [2, DKB, DV])
        sb_ = rb("state_update", [2, DKB, DV])
        s_hi, s_lo = rb("s_hi", [2, DV], F32R), rb("s_lo", [2, DV], F32R)
        pst = rb("prompt_state", [DKB, DV])
        sd_h = rb("state_decay_of_head", [1])
        stat, mv, rstd = rb("gn_stats", [3, 6]), rb("gn_mean_var", [3, 2]), rb("gn_rstd", [3])
        gvar, mhalf = rb("gn_var_eps", [3]), rb("minus_half", [3])

        q_hi = qkz[:, 0:DKB * N].rearrange("p (d n) -> p d n", d=DKB)
        q_lo = qkz[:, DKB * N:2 * DKB * N].rearrange("p (d n) -> p d n", d=DKB)
        kk = qkz[:, 2 * DKB * N:2 * DKB * N + 2 * DKB * T].rearrange("p (s d n) -> p s d n", s=2, d=DKB)
        kt_hi, kt_lo = kk[:, 0], kk[:, 1]
        z_hi = qkz[:, 0:DVB * N].rearrange("p (d n) -> p d n", d=DVB)
        z_lo = qkz[:, DVB * N:2 * DVB * N].rearrange("p (d n) -> p d n", d=DVB)
        q_raw = raws[:, 0:DKB * N].rearrange("p (d n) -> p d n", d=DKB)
        k_raw = raws[:, 0:DKB * T].rearrange("p (d n) -> p d n", d=DKB)
        k_dec = raws[:, DKB * T:2 * DKB * T].rearrange("p (d n) -> p d n", d=DKB)
        gate = raws[:, 0:DVB * N].rearrange("p (d n) -> p d n", d=DVB)
        v_t = vt_yn[:, 0:DVB * T].rearrange("p (d n) -> p d n", d=DVB)
        y_n = vt_yn[:, :].rearrange("p (t n) -> p t n", t=3)
        st_k = stage[:, 0:DKB * 2 * P].rearrange("p (d f c n) -> p d f c n", d=DKB, f=2, c=4)
        st_v = stage[:, DKB * 2 * P:].rearrange("p (d f c n) -> p d f c n", d=DVB, f=2, c=4)
        y_f = stage[:, 0:2 * DV].rearrange("p (s n) -> p s n", s=2)
        qz_rows = qz[:, :, :].rearrange("p k (b c) -> p k b c", c=136)

        ret.close()
        m_hi, m_lo = sb("m_hi", [NE, NOUT], F32R), sb("m_lo", [NE, NOUT], F32R)
        cwt, csi = sb("conv_w", [NE, WIDTH]), sb("conv_state_in", [NE, NB, 2])
        cso = sb("conv_state_out", [NE, 1 + NB, 2])
        w_j = sb("conv_w_block", [WIDTH])
        c_sb, z_sb, b_z, cv, m_f = (sb(n, [w]) for n, w in (
            ("c_gate", N), ("silu_z", NOUT), ("gate_product", NOUT), ("conv", NOUT), ("m", NOUT)))
        u = sb("u", [NP_ + NB * ROWS_U])
        ln_sq, ln_y = sb("ln_square", [2, N]), sb("ln_y", [2, N])
        ln_v = sb("ln_var", [3, N])
        u_s = u[:, NP_:].rearrange("p (b r) -> p b r", r=ROWS_U)
        cv_s = cv[:, SEQ:].rearrange("p (b r) -> p b r", r=DSEQ)

        con_in, trig_in, ln_in, cw_in = count("con_in"), count("trig_in"), count("ln_in"), count("cw_in")
        x_in = [count(f"x_in{i}") for i in range(4)]
        x_h, x_l, x_acc = count("x_hi_made"), count("x_lo_made"), count("residual_made")
        half_set, fold_set, zero_set = count("minus_half_set"), count("fold_set"), count("zeros_set")
        w_in = [count(f"w_in{s}", 16 * CPH // RAW) for s in range(RAW)]
        w_h = count("w_hi_made", CPH)
        w_l = count("w_lo_made", CPH, RAW)
        w_hu, w_lu = count("w_hi_used", CPH, SPL), count("w_lo_used", CPH, SPL)
        o_even = count("out_even_done", 8)
        p_act = count("proj_read_act", 8)
        p_dve = count("proj_read_dve", 20, 2)
        tab_in = count("tab_in")
        q_t, q_rot, q_h, q_l = count("q_temp"), count("q_rotated", 2), count("q_hi_made"), count("q_lo_made")
        qs_t, qz_h, qz_l = count("q_decayed"), count("q_spread_hi"), count("q_spread_lo")
        k_t, k_rot, k_h, k_l = count("k_temp"), count("k_rotated", 2), count("k_hi_made"), count("k_lo_made")
        k_d = count("k_decayed", 1)
        sk_h, sk_l = count("stack_k_hi", DKB), count("stack_k_lo", DKB)
        sv_h, sv_l = count("stack_v_hi", DVB), count("stack_v_lo", DVB)
        sd_set = count("state_decay_set")
        sc_done, a_f, a_h, a_l = count("scores_done", 3), count("a_masked", 3), count("a_hi_made", 3), count("a_lo_made", 3)
        kt_done, kn_h, kn_l = count("k_turned", 3), count("k_rows_hi", 3), count("k_rows_lo", 3)
        ks_done, ks_made = count("k_stack_turned"), count("k_stack_made")
        vt_done, vn_h, vn_l = count("v_turned", 3), count("v_rows_hi", 3), count("v_rows_lo", 3)
        vs_done, vs_made = count("v_stack_turned", 2), count("v_stack_made", 2)
        sa_in = [count(f"state_q_in{i}", 64) for i in range(2)]
        s_h = count("s_hi_made", 16)
        s_l = count("s_lo_made", 16, 4)
        s_q = count("s_used", 16, 2)
        yf_h, yf_l = count("y_fold_hi"), count("y_fold_lo")
        y_done, y_st, y_ag = count("y_done", 3), count("y_stats", 3), count("y_aggregated", 3)
        y_ve, y_rs, y_nm = count("y_var_eps"), count("y_rstd"), count("y_normed", 3)
        yt_done, z_f, z_h, z_l = count("y_turned", 4), count("z_made", 4), count("z_hi_made", 4), count("z_lo_made", 4)
        st_done, st_read = count("prompt_state_done", 2), count("prompt_state_read", 2)
        st_out, st_free = count("prompt_state_out", 32), count("prompt_state_free", 1, 1)
        kb_made = count("k_b_made", 8)
        kv_done = count("kv_done", 16)
        s_new = count("s_new_made", 16)
        sb_in = [count(f"state_u_in{i}", 64) for i in range(2)]
        sb_out = [count(f"state_u_out{i}", 64) for i in range(2)]
        gate_set = count("gate_set")
        passed = count("passed")
        ln_sum = [count(f"ln{i}_sum") for i in range(2)]
        ln_c, ln_s2, ln_var = ([count(f"ln{i}_{n}") for i in range(2)] for n in ("centred", "square", "var"))
        ln_ve, ln_sd, ln_rs, ln_m = ([count(f"ln{i}_{n}") for i in range(2)] for n in ("var_eps", "std", "rstd", "scaled"))
        ln_o, ln_h, ln_l, ln_a = ([count(f"ln{i}_{n}") for i in range(2)] for n in ("y", "hi", "lo", "alpha"))
        c_c, c_v, c_z, c_b = count("c_read"), count("v_read", 2), count("z_read"), count("b_read")
        c_w, c_st, c_x, c_m, c_mh, c_ml = (count("conv_w_ready"), count("conv_state_ready"), count("conv_sum", 6),
                                           count("m_made"), count("m_hi_made"), count("m_lo_made"))
        cs_made = count("conv_state_made", 2)
        o_read = count("out_read", 2)
        y_out = [count(f"y_out{i}") for i in range(2)]
        cs_st = count("conv_state_stored")

        def conv_done(j, i):
            return j * CPE + (HEAD_CH + SPL + i + 1)

        def out_done(j, i):
            return j * 4 + (HEAD_CH + CONV_CH + SPL + i + 1)

        block = ctx.enter_context(nc.Block())

        def w(src, slot):
            return src[:, slot, :].rearrange("p (k n) -> p k n", k=8)

        @block.sync
        def _(sp):
            sp.dma_start(con[:, :], consts).then_inc(con_in.sem, 16)

            def load_chunk(base, r, per, i, src):
                sp.wait_ge(w_l.sem, r * per + (base + i + 1))
                sp.dma_start(w_raw[:, i % RAW, :], src).then_inc(w_in[i % RAW].sem, 16)

            for c in range(4):
                sp.dma_start(acc[:, 4 * c:4 * c + 4, :], x_t[:, 4 * c:4 * c + 4, :]).then_inc(x_in[c].sem, 16)
            sp.dma_start(tr[:, :, :], trig).then_inc(trig_in.sem, 16)
            sp.dma_start(sdec[:, :], tables[0, :, TAB:TAB + HEADS]).then_inc(trig_in.sem, 16)
            sp.dma_start(lnt[:, :, :, :], lnp).then_inc(ln_in.sem, 16)
            with sp.Fori(0, HEADS) as h:
                for i in range(CPH):
                    load_chunk(0, h, CPH, i, w_head[h, i])
                    if i >= 8 and i % 2 == 0 and i < 8 + 2 * NB:
                        b = (i - 8) // 2
                        sp.wait_ge(s_l.sem, s_l.at(h, 2 * b - 2))
                        sp.dma_start(sa[:, b % 2, :, :], s_in[b, h]).then_inc(sa_in[b % 2].sem, 16)
            with sp.Fori(0, NE) as j:
                for i in range(CPE):
                    load_chunk(HEAD_CH, j, CPE, i, w_conv[j, i])
            with sp.Fori(0, OUT_CH // 4) as j:
                for i in range(4):
                    load_chunk(HEAD_CH + CONV_CH, j, 4, i, w_cout[j, i])
            for k in range(KT):
                sp.wait_ge(ln_o[1].sem, k + 1)
                sp.dma_start(y_t[:, k, :], ln_y[:, k % 2, 2:N]).then_inc(y_out[k % 2].sem, 16)
            for i in range(2):
                sp.wait_ge(y_out[i].sem, 16 * KT // 2)
            sp.wait_ge(cs_st.sem, 16)

        @block.gpsimd
        def _(pool):
            pool.sem_inc(st_free.sem, st_free.credit)
            pool.memset(mhalf[:, :], -0.5).then_inc(half_set.sem, 1)
            pool.dma_start(tab[:, :], tables[0, :, 0:TAB]).then_inc(tab_in.sem, 16)
            for b in range(2):
                pool.dma_start(sb_[:, b, :, :], s_in[b, 0]).then_inc(sb_in[b].sem, 16)
            pool.wait_ge(half_set.sem, 1)

            def head(h, last):
                for b in range(NB):
                    pool.wait_ge(s_new.sem, s_new.at(h, 2 * b + 2))
                    pool.sem_inc(passed.sem, 1)
                    pool.dma_start(s_out[b, h], sb_[:, b % 2, :, :]).then_inc(sb_out[b % 2].sem, 16)
                    if b == 0:
                        pool.wait_ge(y_ve.sem, y_ve.at(h))
                        pool.tensor_tensor(rstd[:, :], gvar[:, :], mhalf[:, :], ALU.pow).then_inc(y_rs.sem, 1)
                    if b == 2:
                        pool.wait_ge(st_read.sem, st_read.at(h, 2))
                        pool.sem_inc(passed.sem, 1)
                        pool.dma_start(s_prompt[h], pst[:, :, :]).then_inc(st_out.sem, 16)
                    if not last and b == 3:
                        pool.wait_ge(a_f.sem, a_f.at(h, 3))
                        pool.sem_inc(passed.sem, 1)
                        pool.dma_start(tab[:, :], tables[h + 1, :, 0:TAB]).then_inc(tab_in.sem, 16)
                    if b == 5:
                        pool.wait_ge(st_out.sem, h * 16 + 16)
                        pool.sem_inc(st_free.sem, 1)
                    if not (last and b >= NB - 2):
                        pool.wait_ge(sb_out[b % 2].sem, h * 64 + 16 * (b // 2 + 1))
                        nxt = s_in[b + 2, h] if b < NB - 2 else s_in[b + 2 - NB, h + 1]
                        pool.sem_inc(passed.sem, 1)
                        pool.dma_start(sb_[:, b % 2, :, :], nxt).then_inc(sb_in[b % 2].sem, 16)

            with pool.Fori(0, HEADS - 1) as h:
                head(h, False)
            head(HEADS - 1, True)
            for b in range(2):
                pool.wait_ge(sb_out[b].sem, 16 * HEADS * NB // 2)
            pool.wait_ge(ln_c[0].sem, 1)
            pool.dma_start(cwt[:, :, :], cw).then_inc(cw_in.sem, 16)
            pool.dma_start(csi[:, :, :, :], cs_in).then_inc(cw_in.sem, 16)
            pool.wait_ge(cs_made.sem, 2 * NE)
            pool.dma_start(cs_out, cso[:, :, :, :]).then_inc(cs_st.sem, 16)
            pool.wait_ge(cs_st.sem, 16)

        @block.scalar
        def _(act):
            def round_chunk(base, r, per, i):
                rounds = per // RAW
                first = base // RAW
                act.wait_ge(w_in[i % RAW].sem, r * (16 * rounds) + 16 * (first + i // RAW + 1))
                act.wait_ge(w_hu.sem, r * per + (base + i + 1))
                act.wait_ge(w_l.sem, r * per + (base + i + 1 - SPL + RAW))
                act.copy(w_hi[:, i % SPL, :], w_raw[:, i % RAW, :]).then_inc(w_h.sem, 1)

            act.wait_ge(con_in.sem, 16)
            act.wait_ge(zero_set.sem, 1)
            act.copy(fold[:, :], fold_raw).then_inc(fold_set.sem, 1)
            for c in range(4):
                act.wait_ge(x_in[c].sem, 16)
                act.copy(xh[:, 4 * c:4 * c + 4, :], acc[:, 4 * c:4 * c + 4, :]).then_inc(x_h.sem, 1)

            with act.Fori(0, HEADS) as h:
                act.activation(gate_touch[:, :], con[:, 0:1], ACT.Silu).then_inc(gate_set.sem, 1)

                def s_round(t):
                    b = t // 2
                    if t % 2 == 0:
                        act.wait_ge(sa_in[b % 2].sem, h * 64 + 16 * (b // 2 + 1))
                    act.wait_ge(s_q.sem, s_q.at(h, t - 1))
                    act.copy(s_hi[:, t % 2, :], sa[:, b % 2, t % 2, :]).then_inc(s_h.sem, 1)

                def side(i):
                    if i == 4:
                        act.wait_ge(q_rot.sem, q_rot.at(h, 2))
                        act.copy(q_hi, q_raw).then_inc(q_h.sem, 1)
                        act.wait_ge(qs_t.sem, qs_t.at(h))
                        act.copy(qz_rows[:, :, :, 0:8],
                                 tmp[:, 0, 0:DKB * NSAMP].rearrange("p (d b r) -> p d b r", d=DKB, b=NB)
                                 ).then_inc(qz_h.sem, 1)
                    if i == 8:
                        act.wait_ge(k_rot.sem, k_rot.at(h, 2))
                        act.copy(kt_hi, k_raw).then_inc(k_h.sem, 1)
                    if i == 9:
                        act.wait_ge(k_d.sem, k_d.at(h))
                        for d in range(DKB):
                            src = k_dec[:, d, PROMPT:].rearrange("p (f n) -> p f n", f=2)
                            act.copy(st_k[:, d, :, 0, :], src)
                            act.copy(st_k[:, d, :, 1, :], src).then_inc(sk_h.sem, 1)
                    if 10 <= i <= 16 and i % 2 == 0:
                        g = 4 + (i - 10) // 2
                        act.wait_ge(w_lu.sem, w_lu.at(h, 2 * g + 2))
                        act.copy(v_t[:, g - 4, :], bank_p[g % 2][:, 0:T]).then_inc(p_act.sem, 1)
                    if i == 12:
                        for m in range(3):
                            rows = KEY[m][1]
                            src = (bank_r[3][0:rows, 256 * m:256 * m + 256] if m < 2 else bank_r[4][0:rows, 0:256])
                            act.wait_ge(kt_done.sem, kt_done.at(h, m + 1))
                            if m < 2:
                                act.copy(k_hi[0:rows, m, :], src).then_inc(kn_h.sem, 1)
                            else:
                                act.activation(k_hi[0:rows, m, :], src, ACT.Copy,
                                               scale=row_mask[0:rows, :]).then_inc(kn_h.sem, 1)
                    if i == 12:
                        act.wait_ge(ks_done.sem, ks_done.at(h))
                        act.copy(k_st[:, :, :], bank_r[0][:, :].rearrange("p (f n) -> p f n", f=2)).then_inc(ks_made.sem, 1)
                    if i in (13, 14):
                        for m in ((0, 1), (2,))[i - 13]:
                            act.wait_ge(a_f.sem, a_f.at(h, m + 1))
                            n = SC[m][1]
                            at = tmp[:, m % 2, 0:n]
                            rows = KEY[m][1]
                            act.copy(a_hi[0:rows, A_AT[m]:A_AT[m] + n], at[0:rows]).then_inc(a_h.sem, 1)
                    if i == 17:
                        act.wait_ge(p_act.sem, p_act.at(h, 4))
                        for d in range(DVB):
                            src = v_t[:, d, PROMPT:].rearrange("p (f n) -> p f n", f=2)
                            act.copy(st_v[:, d, :, 0, :], src)
                            act.copy(st_v[:, d, :, 2, :], src).then_inc(sv_h.sem, 1)
                    if i == 18:
                        for m in range(3):
                            rows = KEY[m][1]
                            act.wait_ge(vt_done.sem, vt_done.at(h, m + 1))
                            act.copy(v_hi[0:rows, m, :], bank_r[m][0:rows, :]).then_inc(vn_h.sem, 1)
                    if i == 19:
                        for f in range(2):
                            act.wait_ge(vs_done.sem, vs_done.at(h, f + 1))
                            act.copy(v_st[:, f, :], bank_r[3 + f][:, :]).then_inc(vs_made.sem, 1)
                    if 18 <= i <= 24 and i % 2 == 0:
                        g = 8 + (i - 18) // 2
                        act.wait_ge(w_lu.sem, w_lu.at(h, 2 * g + 2))
                        act.activation(gate[:, g - 8, :], bank_p[g % 2][:, 0:N], ACT.Silu).then_inc(p_act.sem, 1)
                    if i == 22:
                        act.wait_ge(s_q.sem, s_q.at(h, 2 * NB))
                        act.copy(y_f[:, 0, :], bank_q[:, :]).then_inc(yf_h.sem, 1)
                    if i == 21:
                        for d in range(DKB):
                            act.wait_ge(st_done.sem, st_done.at(h, d + 1))
                            if d == 0:
                                act.wait_ge(st_free.sem, st_free.at(h, 0))
                            act.copy(pst[:, d, :], bank_r[3 + d][:, :]).then_inc(st_read.sem, 1)
                    if i == 24:
                        for j in range(DVB):
                            act.wait_ge(z_f.sem, z_f.at(h, j + 1))
                            act.copy(z_hi[:, j, :], tmp[:, j % 2, 0:N]).then_inc(z_h.sem, 1)
                    for b in KB_AT.get(i, ()):
                        if b >= 2:
                            act.wait_ge(kv_done.sem, kv_done.at(h, 2 * b - 2))
                        act.wait_ge(ks_made.sem, ks_made.at(h))
                        act.activation(k_b[:, b % 2, :], k_st[:, b // 4, :], ACT.Copy,
                                       scale=bmask[:, b % 4:b % 4 + 1]).then_inc(kb_made.sem, 1)

                for i in range(CPH):
                    round_chunk(0, h, CPH, i)
                    side(i)
                    if 6 <= i < 22:
                        s_round(i - 6)

            def norm(n, c0):
                for k in range(KT):
                    act.wait_ge(ln_c[n].sem, k + 1)
                    if k >= 2:
                        act.wait_ge(ln_var[n].sem, k - 1)
                    act.activation(ln_sq[:, k % 2, c0:N], acc[:, k, CUT + c0:T], ACT.Square).then_inc(ln_s2[n].sem, 1)
                act.wait_ge(ln_ve[n].sem, 1)
                act.activation(ln_v[:, 1, c0:N], ln_v[:, 0, c0:N], ACT.Sqrt).then_inc(ln_sd[n].sem, 1)

            norm(0, 0)
            for i in range(SPL):
                round_chunk(HEAD_CH, 0, CPE, i)
            for k in range(KT):
                act.wait_ge(ln_o[0].sem, k + 1)
                act.copy(xh[:, k, CUT:T], ln_y[:, k % 2, :]).then_inc(ln_h[0].sem, 1)
                act.mul(acc[:, k, CUT:T], ln_y[:, k % 2, :], ALPHA).then_inc(ln_a[0].sem, 1)

            def conv(j, lo, at):
                def go(i):
                    if i >= lo:
                        round_chunk(HEAD_CH, at, CPE, i)
                act.activation(gate_touch[:, :], con[:, 0:1], ACT.Silu).then_inc(gate_set.sem, 1)
                for i in range(CPE):
                    go(i)
                    if i == 2:
                        act.wait_ge(w_lu.sem, conv_done(j, 1))
                        act.copy(c_sb[:, :], bank_p[0][:, 0:N]).then_inc(c_c.sem, 1)
                    if i == 6:
                        act.wait_ge(w_lu.sem, conv_done(j, 5))
                        act.activation(z_sb[:, :], bank_p[0][:, 0:NOUT], ACT.Silu).then_inc(c_z.sem, 1)

            def conv_hi(j):
                act.wait_ge(c_m.sem, c_m.at(j))
                act.copy(m_hi[:, j, :], m_f[:, :]).then_inc(c_mh.sem, 1)

            conv(0, SPL, 0)
            with act.Fori(1, NE) as j:
                act.activation(gate_touch[:, :], con[:, 0:1], ACT.Silu).then_inc(gate_set.sem, 1)
                for i in range(CPE):
                    round_chunk(HEAD_CH, j, CPE, i)
                    if i == 1:
                        conv_hi(j - 1)
                    if i == 2:
                        act.wait_ge(w_lu.sem, conv_done(j, 1))
                        act.copy(c_sb[:, :], bank_p[0][:, 0:N]).then_inc(c_c.sem, 1)
                    if i == 6:
                        act.wait_ge(w_lu.sem, conv_done(j, 5))
                        act.activation(z_sb[:, :], bank_p[0][:, 0:NOUT], ACT.Silu).then_inc(c_z.sem, 1)
            for i in range(2):
                round_chunk(HEAD_CH + CONV_CH, 0, 4, i)
            conv_hi(NE - 1)
            for i in range(2, 4):
                round_chunk(HEAD_CH + CONV_CH, 0, 4, i)
            with act.Fori(1, OUT_CH // 4) as j:
                for i in range(4):
                    round_chunk(HEAD_CH + CONV_CH, j, 4, i)
            norm(1, 2)

        @block.vector
        def _(dve):
            f = lambda ap: ap.bitcast(F32)
            TT = dve.tensor_tensor

            def rest_chunk(base, r, per, i):
                dve.wait_ge(w_h.sem, r * per + (base + i + 1))
                dve.wait_ge(w_lu.sem, r * per + (base + i + 1))
                TT(w_lo[:, i % SPL, :], w_raw[:, i % RAW, :], f(w_hi[:, i % SPL, :]), ALU.subtract).then_inc(w_l.sem, 1)

            dve.sem_inc(w_l.sem, w_l.credit)
            dve.sem_inc(p_dve.sem, p_dve.credit)
            dve.sem_inc(s_l.sem, s_l.credit)
            dve.memzero(f(a_hi[:, :]))
            dve.memzero(f(a_lo[:, :]))
            dve.memzero(f(qz[:, :, :]))
            dve.memset(mv[:, :, :], 0.0).then_inc(zero_set.sem, 1)
            for c in range(4):
                cs = slice(4 * c, 4 * c + 4)
                dve.wait_ge(x_h.sem, c + 1)
                TT(xl[:, cs, :], acc[:, cs, :], f(xh[:, cs, :]), ALU.subtract).then_inc(x_l.sem, 1)
            for c in range(4):
                dve.wait_ge(x_l.sem, c + 1)
                cs = acc[:, 4 * c:4 * c + 4, CUT:T]
                dve.tensor_scalar(cs, cs, ALPHA, None, ALU.mult).then_inc(x_acc.sem, 1)
            dve.wait_ge(x_acc.sem, 4)
            dve.wait_ge(trig_in.sem, 32)
            dve.wait_ge(zero_set.sem, 1)
            add = ALU.add

            with dve.Fori(0, HEADS) as h:

                def q_or_k(i, bank, raw, t_sem, rot_sem, c0):
                    cos, sin = tr[:, 0, c0:T], tr[:, 1, c0:T]
                    n = T - c0
                    src = bank[:, 0:n]
                    if i == 0:
                        TT(raw[:, 0, :], src, cos, ALU.mult)
                        TT(raw[:, 1, :], src, sin, ALU.mult).then_inc(p_dve.sem, 1)
                    else:
                        TT(tmp[:, 0, 0:n], src, sin, ALU.mult).then_inc(t_sem.sem, 1)
                        TT(tmp[:, 1, 0:n], src, cos, ALU.mult).then_inc(p_dve.sem, 1)
                        dve.wait_ge(t_sem.sem, t_sem.at(h))
                        TT(raw[:, 0, :], raw[:, 0, :], tmp[:, 0, 0:n], ALU.subtract).then_inc(rot_sem.sem, 1)
                        dve.wait_ge(p_dve.sem, p_dve.at(h, 2 if raw is q_raw else 4))
                        TT(raw[:, 1, :], raw[:, 1, :], tmp[:, 1, 0:n], add).then_inc(rot_sem.sem, 1)

                def s_rest(t):
                    b = t // 2
                    dve.wait_ge(s_h.sem, s_h.at(h, t + 1))
                    dve.wait_ge(s_q.sem, s_q.at(h, t - 1))
                    TT(s_lo[:, t % 2, :], sa[:, b % 2, t % 2, :], f(s_hi[:, t % 2, :]), ALU.subtract).then_inc(s_l.sem, 1)

                def kv_update(t):
                    b, bank = t // 2, bank_r[3 + t % 2]
                    if t % 2 == 0:
                        dve.wait_ge(sb_in[b % 2].sem, h * 64 + 16 * (b // 2 + 1))
                    dve.wait_ge(kv_done.sem, kv_done.at(h, t + 1))
                    dve.wait_ge(sd_set.sem, sd_set.at(h))
                    s = sb_[:, b % 2, t % 2, :]
                    dve.scalar_tensor_tensor(s, s, sd_h[:, :], bank[:, :], ALU.mult, add).then_inc(s_new.sem, 1)

                def out_read(c):
                    for e in range(2):
                        if e == 0:
                            dve.wait_ge(o_even.sem, o_even.at(h, c + 1))
                        else:
                            dve.wait_ge(w_lu.sem, w_lu.at(h, 24 + c + 1))
                        a = acc[:, 2 * c + e, CUT:T]
                        TT(a, a, bank_p[e][:, 0:N], add).then_inc(p_dve.sem, 1)

                def side(i):
                    if i == 2:
                        dve.tensor_copy(sd_h[:, :], sdec[:, bass.ds(h, 1)]).then_inc(sd_set.sem, 1)
                        dve.wait_ge(w_lu.sem, w_lu.at(h, 2))
                        q_or_k(0, bank_p[0], q_raw, q_t, q_rot, CUT)
                    if i == 4:
                        dve.wait_ge(w_lu.sem, w_lu.at(h, 4))
                        q_or_k(1, bank_p[1], q_raw, q_t, q_rot, CUT)
                        dve.wait_ge(tab_in.sem, h * 16 + 16)
                        dve.wait_ge(q_rot.sem, q_rot.at(h, 2))
                        dec = tab[:, QD_AT:QD_AT + NSAMP].unsqueeze(1).to_broadcast([P, DKB, NSAMP])
                        qs = tmp[:, 0, 0:DKB * NSAMP].rearrange("p (d n) -> p d n", d=DKB)
                        TT(qs, q_raw[:, :, NP_:N], dec, ALU.mult).then_inc(qs_t.sem, 1)
                        dve.wait_ge(q_h.sem, q_h.at(h))
                        TT(q_lo, q_raw, f(q_hi), ALU.subtract).then_inc(q_l.sem, 1)
                        dve.wait_ge(qz_h.sem, qz_h.at(h))
                        qs4 = qs.rearrange("p d (b r) -> p d b r", b=NB)
                        for d in range(DKB):
                            z = TT(qz_rows[:, d, :, 64:72], qs4[:, d], f(qz_rows[:, d, :, 0:8]), ALU.subtract)
                        z.then_inc(qz_l.sem, 1)
                    if i == 6:
                        dve.wait_ge(w_lu.sem, w_lu.at(h, 6))
                        q_or_k(0, bank_p[0], k_raw, k_t, k_rot, 0)
                    if i == 8:
                        dve.wait_ge(w_lu.sem, w_lu.at(h, 8))
                        q_or_k(1, bank_p[1], k_raw, k_t, k_rot, 0)
                        dve.wait_ge(k_h.sem, k_h.at(h))
                        TT(kt_lo, k_raw, f(kt_hi), ALU.subtract).then_inc(k_l.sem, 1)
                    if i == 9:
                        dve.wait_ge(k_rot.sem, k_rot.at(h, 2))
                        dec = tab[:, KD_AT:KD_AT + T].unsqueeze(1).to_broadcast([P, DKB, T])
                        TT(k_dec, k_raw, dec, ALU.mult).then_inc(k_d.sem, 1)
                        for d in range(DKB):
                            dve.wait_ge(sk_h.sem, sk_h.at(h, d + 1))
                            src = k_dec[:, d, PROMPT:].rearrange("p (f n) -> p f n", f=2)
                            hi = f(st_k[:, d, :, 0, :])
                            TT(st_k[:, d, :, 2, :], src, hi, ALU.subtract)
                            TT(st_k[:, d, :, 3, :], src, hi, ALU.subtract).then_inc(sk_l.sem, 1)
                    if i == 12:
                        for m in range(3):
                            rows = KEY[m][1]
                            src = (bank_r[3][0:rows, 256 * m:256 * m + 256] if m < 2 else bank_r[4][0:rows, 0:256])
                            dve.wait_ge(kn_h.sem, kn_h.at(h, max(m + 1, 2)))
                            o, hi = k_lo[0:rows, m, :], f(k_hi[0:rows, m, :])
                            if m < 2:
                                TT(o, src, hi, ALU.subtract).then_inc(kn_l.sem, 1)
                            else:
                                dve.scalar_tensor_tensor(o, src, row_mask[0:rows, :], hi, ALU.mult,
                                                         ALU.subtract).then_inc(kn_l.sem, 1)
                    if i in (13, 14):
                        ms = ((0, 1), (2,))[i - 13]
                        for m in ms:
                            rows, n, bank = KEY[m][1], SC[m][1], bank_r[(1, 2, 0)[m]]
                            dve.wait_ge(sc_done.sem, sc_done.at(h, m + 1))
                            if m >= 2:
                                dve.wait_ge(a_l.sem, a_l.at(h, m - 1))
                            TT(tmp[0:rows, m % 2, 0:n], bank[0:rows, 0:n], tab[0:rows, M_AT[m]:M_AT[m] + n],
                               ALU.mult).then_inc(a_f.sem, 1)
                        for m in ms:
                            rows, n = KEY[m][1], SC[m][1]
                            at = slice(A_AT[m], A_AT[m] + n)
                            dve.wait_ge(a_h.sem, a_h.at(h, m + 1))
                            TT(a_lo[0:rows, at], tmp[0:rows, m % 2, 0:n], f(a_hi[0:rows, at]), ALU.subtract).then_inc(a_l.sem, 1)
                    if i == 17:
                        for d in range(DVB):
                            dve.wait_ge(sv_h.sem, sv_h.at(h, d + 1))
                            src = v_t[:, d, PROMPT:].rearrange("p (f n) -> p f n", f=2)
                            hi = f(st_v[:, d, :, 0, :])
                            TT(st_v[:, d, :, 1, :], src, hi, ALU.subtract)
                            TT(st_v[:, d, :, 3, :], src, hi, ALU.subtract).then_inc(sv_l.sem, 1)
                    if i == 18:
                        for m in range(3):
                            rows = KEY[m][1]
                            dve.wait_ge(vn_h.sem, vn_h.at(h, m + 1))
                            TT(v_lo[0:rows, m, :], bank_r[m][0:rows, :], f(v_hi[0:rows, m, :]), ALU.subtract).then_inc(vn_l.sem, 1)
                    if i == 22:
                        dve.wait_ge(yf_h.sem, yf_h.at(h))
                        TT(y_f[:, 1, :], bank_q[:, :], f(y_f[:, 0, :]), ALU.subtract).then_inc(yf_l.sem, 1)
                    if i in (21, 23):
                        for t in ((0, 1), (2,))[(i - 21) // 2]:
                            rows = QRY[t][1]
                            dve.wait_ge(y_done.sem, y_done.at(h, t + 1))
                            dve.bn_stats(stat[0:rows, t, :], bank_r[t][0:rows, :]).then_inc(y_st.sem, 1)
                            dve.wait_ge(y_st.sem, y_st.at(h, t + 1))
                            dve.sem_inc(passed.sem, 1)
                            dve.bn_aggr(mv[0:rows, t, :], stat[0:rows, t, :]).then_inc(y_ag.sem, 1)
                    if i == 23:
                        dve.wait_ge(y_ag.sem, y_ag.at(h, 3))
                        dve.tensor_scalar(gvar[:, :], mv[:, :, 1], GN_EPS, None, add).then_inc(y_ve.sem, 1)
                    if i == 24:
                        dve.wait_ge(y_rs.sem, y_rs.at(h))
                        for t in range(3):
                            rows = QRY[t][1]
                            dve.tensor_scalar(y_n[0:rows, t, :], bank_r[t][0:rows, :], mv[0:rows, t, 0:1],
                                              rstd[0:rows, t:t + 1], ALU.subtract, ALU.mult).then_inc(y_nm.sem, 1)
                        for t in KV_AT[23]:
                            kv_update(t)
                        for j in range(DVB):
                            dve.wait_ge(yt_done.sem, yt_done.at(h, j + 1))
                            dve.wait_ge(p_act.sem, p_act.at(h, 5 + j))
                            TT(tmp[:, j % 2, 0:N], bank_r[j % 3][:, 0:N], gate[:, j, :], ALU.mult).then_inc(z_f.sem, 1)
                            dve.wait_ge(z_h.sem, z_h.at(h, j + 1))
                            TT(z_lo[:, j, :], tmp[:, j % 2, 0:N], f(z_hi[:, j, :]), ALU.subtract).then_inc(z_l.sem, 1)
                    if i >= 25:
                        out_read(i - 25)
                    for t in KV_AT.get(i - 1, ()) if i != 24 else ():
                        kv_update(t)

                for i in range(CPH):
                    rest_chunk(0, h, CPH, i)
                    side(i)
                    if 6 <= i < 22:
                        s_rest(i - 6)
                out_read(7)
                for t in KV_AT[31]:
                    kv_update(t)

            def norm(n, c0):
                mean, var = bank_r[0][:, c0:N], bank_r[1][:, c0:N]
                dve.wait_ge(ln_sum[n].sem, 1)
                for k in range(KT):
                    a = acc[:, k, CUT + c0:T]
                    TT(a, a, mean, ALU.subtract).then_inc(ln_c[n].sem, 1)
                dve.wait_ge(ln_var[n].sem, KT)
                dve.tensor_scalar(ln_v[:, 0, c0:N], var, LN_EPS, None, add).then_inc(ln_ve[n].sem, 1)
                dve.wait_ge(ln_sd[n].sem, 1)
                dve.reciprocal(ln_v[:, 2, c0:N], ln_v[:, 1, c0:N]).then_inc(ln_rs[n].sem, 1)
                dve.wait_ge(ln_rs[n].sem, 1)
                dve.wait_ge(ln_in.sem, 16)
                for k in range(KT):
                    a = acc[:, k, CUT + c0:T]
                    TT(a, a, ln_v[:, 2, c0:N], ALU.mult).then_inc(ln_m[n].sem, 1)
                    dve.wait_ge(ln_m[n].sem, k + 1)
                    if n == 0:
                        if k >= 2:
                            dve.wait_ge(ln_a[0].sem, k - 1)
                    elif k >= 2:
                        dve.wait_ge(y_out[k % 2].sem, 16 * (k // 2))
                    dve.tensor_scalar(ln_y[:, k % 2, c0:N], a, lnt[:, 0, n, k:k + 1], lnt[:, 1, n, k:k + 1],
                                      ALU.mult, add).then_inc(ln_o[n].sem, 1)
                    if n == 0:
                        dve.wait_ge(ln_h[0].sem, k + 1)
                        TT(xl[:, k, CUT:T], ln_y[:, k % 2, :], f(xh[:, k, CUT:T]), ALU.subtract).then_inc(ln_l[0].sem, 1)

            norm(0, 0)
            dve.wait_ge(cw_in.sem, 32)

            def conv(j, at):
                for i in range(CPE):
                    rest_chunk(HEAD_CH, at, CPE, i)
                    if i == 0:
                        dve.tensor_copy(w_j[:, :], cwt[:, bass.ds(j, 1), :].rearrange("p a b -> p (a b)")).then_inc(c_w.sem, 1)
                        dve.tensor_copy(u_s[:, :, 0:2], csi[:, bass.ds(j, 1), :, :].rearrange("p a b c -> p (a b) c")).then_inc(c_st.sem, 1)
                    if i == 4:
                        dve.wait_ge(w_lu.sem, conv_done(j, 3))
                        dve.wait_ge(c_c.sem, c_c.at(j))
                        TT(u[:, 0:NP_], bank_p[1][:, 0:NP_], c_sb[:, 0:NP_], ALU.mult).then_inc(c_v.sem, 1)
                        bs = lambda ap: ap.rearrange("p (b r) -> p b r", r=DSEQ)
                        TT(u_s[:, :, 2:], bs(bank_p[1][:, NP_:N]), bs(c_sb[:, NP_:N]), ALU.mult).then_inc(c_v.sem, 1)
                        dve.wait_ge(c_v.sem, c_v.at(j, 2))
                        dve.wait_ge(c_w.sem, c_w.at(j))
                        dve.wait_ge(c_st.sem, c_st.at(j))
                        for n in range(WIDTH):
                            w0 = w_j[:, n:n + 1]
                            for s, (dst, src) in enumerate(((cv[:, 0:SEQ], u[:, n:n + SEQ]), (cv_s, u_s[:, :, n:n + DSEQ]))):
                                if n == 0:
                                    dve.tensor_scalar(dst, src, w0, None, ALU.mult).then_inc(c_x.sem, 1)
                                else:
                                    dve.wait_ge(c_x.sem, c_x.at(j, 2 * (n - 1) + s + 1))
                                    dve.scalar_tensor_tensor(dst, src, w0, dst, ALU.mult, add).then_inc(c_x.sem, 1)
                        dve.tensor_copy(cso[:, bass.ds(j, 1), 0, :].rearrange("p a c -> p (a c)"), u[:, NP_ - 2:NP_]).then_inc(cs_made.sem, 1)
                        dve.tensor_copy(cso[:, bass.ds(j, 1), 1:, :].rearrange("p a b c -> p (a b) c"), u_s[:, :, DSEQ:]).then_inc(cs_made.sem, 1)

            def conv_end(j):
                dve.wait_ge(w_lu.sem, conv_done(j, 7))
                dve.wait_ge(c_z.sem, c_z.at(j))
                TT(b_z[:, :], bank_p[1][:, 0:NOUT], z_sb[:, :], ALU.mult).then_inc(c_b.sem, 1)
                dve.wait_ge(c_b.sem, c_b.at(j))
                dve.wait_ge(c_x.sem, c_x.at(j, 6))
                TT(m_f[:, :], b_z[:, :], cv[:, :], ALU.mult).then_inc(c_m.sem, 1)

            def conv_rest(j):
                dve.wait_ge(c_mh.sem, c_mh.at(j))
                at = bass.ds(j, 1)
                sq = lambda ap: ap.rearrange("p a n -> p (a n)")
                TT(sq(m_lo[:, at, :]), m_f[:, :], f(sq(m_hi[:, at, :])), ALU.subtract).then_inc(c_ml.sem, 1)

            with dve.Fori(0, NE) as j:
                conv(j, j)
                conv_end(j)
                conv_rest(j)

            def block_read(j, e):
                dve.wait_ge(w_lu.sem, out_done(j, 2 * e + 1))
                a = acc[:, bass.ds(2 * j + e, 1), META:T].rearrange("p a n -> p (a n)")
                TT(a, a, bank_p[e][:, 0:NOUT], add).then_inc(o_read.sem, 1)

            with dve.Fori(0, OUT_CH // 4) as j:
                for i in range(4):
                    rest_chunk(HEAD_CH + CONV_CH, j, 4, i)
                    if i == 2:
                        block_read(j, 0)
                block_read(j, 1)
            norm(1, 2)

        @block.tensor
        def _(pe):
            mm = pe.matmul

            def three(out, a_hi_, a_lo_, b_hi_, b_lo_, start, stop):
                mm(out, a_hi_, b_hi_, start=start, stop=False)
                mm(out, a_hi_, b_lo_, start=False, stop=False)
                return mm(out, a_lo_, b_hi_, start=False, stop=stop)

            def turn(out, src):
                n = src.shape[0]
                return pe.transpose(out, src if src.dtype == F32 else src.bitcast(F32), ident[0:n, 0:n])

            def proj(base, r, per, i, bank, n, rhs_h, rhs_l, first, last, by_block=None):
                wh, wl = w(w_hi, i % SPL), w(w_lo, i % SPL)
                pe.wait_ge(w_h.sem, r * per + (base + i + 1))
                for k in range(8):
                    if by_block:
                        by_block(k)
                    mm(bank[:, 0:n], wh[:, k, :], rhs_h(k), start=(first and k == 0), stop=False)
                    x = mm(bank[:, 0:n], wh[:, k, :], rhs_l(k), start=False, stop=False)
                x.then_inc(w_hu.sem, 1)
                pe.wait_ge(w_l.sem, r * per + (base + i + 1 + RAW))
                for k in range(8):
                    x = mm(bank[:, 0:n], wl[:, k, :], rhs_h(k), start=False, stop=(last and k == 7))
                x.then_inc(w_lu.sem, 1)

            pe.sem_inc(w_hu.sem, w_hu.credit)
            pe.sem_inc(w_lu.sem, w_lu.credit)
            pe.sem_inc(s_q.sem, s_q.credit)
            pe.wait_ge(con_in.sem, 16)
            pe.wait_ge(x_h.sem, 4)
            pe.wait_ge(x_l.sem, 4)
            pe.wait_ge(fold_set.sem, 1)
            pe.wait_ge(zero_set.sem, 1)

            with pe.Fori(0, HEADS) as h:
                def side(i):
                    if i == 10:
                        pe.wait_ge(k_d.sem, k_d.at(h))
                        for m, (t0, rows) in enumerate(KEY):
                            bank, c0 = (bank_r[3], 256 * m) if m < 2 else (bank_r[4], 0)
                            for d in range(DKB):
                                x = turn(bank[0:rows, c0 + P * d:c0 + P * d + P], k_dec[:, d, t0:t0 + rows])
                            x.then_inc(kt_done.sem, 1)
                        pe.wait_ge(sk_l.sem, sk_l.at(h, DKB))
                        for half in range(2):
                            for d in range(DKB):
                                x = turn(bank_r[0][:, 256 * half + P * d:256 * half + P * d + P],
                                         st_k[:, d, half].rearrange("p c n -> p (c n)"))
                        x.then_inc(ks_done.sem, 1)
                    if i in (11, 13):
                        pe.wait_ge(q_l.sem, q_l.at(h))
                        pe.wait_ge(k_l.sem, k_l.at(h))
                        if i == 13:
                            pe.wait_ge(ks_made.sem, ks_made.at(h))
                        for m in ((0, 1), (2,))[(i - 11) // 2]:
                            (t0, rows), (c0, n), bank = KEY[m], SC[m], bank_r[(1, 2, 0)[m]]
                            for d in range(DKB):
                                x = three(bank[0:rows, 0:n], kt_hi[:, d, t0:t0 + rows], kt_lo[:, d, t0:t0 + rows],
                                          q_hi[:, d, c0:c0 + n], q_lo[:, d, c0:c0 + n], d == 0, d == DKB - 1)
                            x.then_inc(sc_done.sem, 1)
                    if i == 17:
                        pe.wait_ge(p_act.sem, p_act.at(h, 4))
                        pe.wait_ge(a_f.sem, a_f.at(h, 3))
                        for m, (t0, rows) in enumerate(KEY):
                            for d in range(DVB):
                                x = turn(bank_r[m][0:rows, P * d:P * d + P], v_t[:, d, t0:t0 + rows])
                            x.then_inc(vt_done.sem, 1)
                    if i == 18:
                        pe.wait_ge(sv_l.sem, sv_l.at(h, DVB))
                        pe.wait_ge(kn_l.sem, kn_l.at(h, 3))
                        for half in range(2):
                            for d in range(DVB):
                                x = turn(bank_r[3 + half][:, P * d:P * d + P],
                                         st_v[:, d, half].rearrange("p c n -> p (c n)"))
                            x.then_inc(vs_done.sem, 1)
                    if i == 19:
                        pe.wait_ge(vn_l.sem, vn_l.at(h, 3))
                        pe.wait_ge(a_l.sem, a_l.at(h, 3))
                        for t in range(2):
                            rows = QRY[t][1]
                            for m in range(t + 1):
                                at = A_AT[m] + QRY[t][0] - SC[m][0]
                                x = three(bank_r[t][0:rows, :], a_hi[:, at:at + rows], a_lo[:, at:at + rows],
                                          v_hi[:, m, :], v_lo[:, m, :], m == 0, m == t)
                            x.then_inc(y_done.sem, 1)
                    if i == 20:
                        pe.wait_ge(vs_made.sem, vs_made.at(h, 2))
                        for d in range(DKB):
                            for m in range(3):
                                rows = KEY[m][1]
                                c = slice(P * d, P * d + P)
                                x = three(bank_r[3 + d][:, :], k_hi[0:rows, m, c], k_lo[0:rows, m, c],
                                          v_hi[0:rows, m, :], v_lo[0:rows, m, :], m == 0, m == 2)
                            x.then_inc(st_done.sem, 1)
                    if 6 <= i < 22:
                        t = i - 6
                        b, d = t // 2, t % 2
                        pe.wait_ge(s_l.sem, s_l.at(h, t + 1))
                        if t == 0:
                            pe.wait_ge(qz_l.sem, qz_l.at(h))
                        qb = qz[:, d, P * b:P * b + P]
                        mm(bank_q[:, :], qb, s_hi[:, t % 2, :], start=(t == 0), stop=False)
                        x = mm(bank_q[:, :], qb, s_lo[:, t % 2, :], start=False, stop=(t == 15))
                        x.then_inc(s_q.sem, 1)
                    if i == 22:
                        rows = QRY[2][1]
                        o = bank_r[2][0:rows, :]
                        pe.wait_ge(yf_l.sem, yf_l.at(h))
                        mm(o, fold[:, :], y_f[:, 0, :], start=True, stop=False)
                        mm(o, fold[:, :], y_f[:, 1, :], start=False, stop=False)
                        for m in range(3):
                            at = A_AT[m] + QRY[2][0] - SC[m][0]
                            kr = KEY[m][1]
                            x = three(o, a_hi[0:kr, at:at + rows], a_lo[0:kr, at:at + rows],
                                      v_hi[0:kr, m, :], v_lo[0:kr, m, :], False, m == 2)
                        x.then_inc(y_done.sem, 1)
                    for t in KV_AT.get(i, ()):
                        b = t // 2
                        if t < 2:
                            pe.wait_ge(st_read.sem, st_read.at(h, t + 1))
                        else:
                            pe.wait_ge(s_new.sem, s_new.at(h, t - 1))
                        pe.wait_ge(kb_made.sem, kb_made.at(h, b + 1))
                        mm(bank_r[3 + t % 2][:, :], k_b[:, b % 2, P * (t % 2):P * (t % 2) + P], v_st[:, b // 4, :],
                           start=True, stop=True).then_inc(kv_done.sem, 1)
                    if i == 23:
                        pe.wait_ge(y_nm.sem, y_nm.at(h, 3))
                        for j in range(DVB):
                            if j == DVB - 1:
                                pe.wait_ge(z_f.sem, z_f.at(h, 1))
                            for t, (c0, rows) in enumerate(QRY):
                                x = turn(bank_r[j % 3][:, c0:c0 + rows], y_n[0:rows, t, P * j:P * j + P])
                            x.then_inc(yt_done.sem, 1)

                def out(i):
                    c = i - 24
                    wh = w_hi[:, i % SPL, :].rearrange("p (k n) -> p k n", k=DVB)
                    wl = w_lo[:, i % SPL, :].rearrange("p (k n) -> p k n", k=DVB)
                    pe.wait_ge(w_h.sem, w_h.at(h, i + 1))
                    for e in range(2):
                        g = 12 + 2 * c + e
                        if g < 14:
                            pe.wait_ge(p_act.sem, p_act.at(h, g - 5))
                        else:
                            pe.wait_ge(p_dve.sem, p_dve.at(h, g - 9))
                        for k in range(DVB):
                            if c == 0 and e == 0:
                                pe.wait_ge(z_l.sem, z_l.at(h, k + 1))
                            x = mm(bank_p[e][:, 0:N], wh[:, k, P * e:P * e + P], z_hi[:, k, :], start=(k == 0), stop=False)
                            x = mm(bank_p[e][:, 0:N], wh[:, k, P * e:P * e + P], z_lo[:, k, :], start=False, stop=False)
                    x.then_inc(w_hu.sem, 1)
                    pe.wait_ge(w_l.sem, w_l.at(h, i + 1))
                    for e in range(2):
                        for k in range(DVB):
                            x = mm(bank_p[e][:, 0:N], wl[:, k, P * e:P * e + P], z_hi[:, k, :], start=False, stop=(k == DVB - 1))
                        x.then_inc((o_even if e == 0 else w_lu).sem, 1)

                for i in range(24):
                    g, kept = i // 2, i < 4 or i >= 16
                    if i % 2 == 0:
                        if g < 2:
                            pe.wait_ge(p_dve.sem, p_dve.at(h, g - 1))
                        elif g < 6:
                            pe.wait_ge(p_dve.sem, p_dve.at(h, g - 1))
                        else:
                            pe.wait_ge(p_act.sem, p_act.at(h, g - 5))
                    c0, k0 = (CUT if kept else 0), 8 * (i % 2)
                    proj(0, h, CPH, i, bank_p[g % 2], T - c0, lambda k: xh[:, k0 + k, c0:T],
                         lambda k: xl[:, k0 + k, c0:T], i % 2 == 0, i % 2 == 1)
                    side(i)
                for i in range(24, CPH):
                    out(i)
                    side(i)

            def norm(n, c0):
                for k in range(KT):
                    x = mm(bank_r[0][:, c0:N], ones, acc[:, k, CUT + c0:T], start=(k == 0), stop=(k == KT - 1))
                x.then_inc(ln_sum[n].sem, 1)
                for k in range(KT):
                    pe.wait_ge(ln_s2[n].sem, k + 1)
                    mm(bank_r[1][:, c0:N], ones, ln_sq[:, k % 2, c0:N], start=(k == 0), stop=(k == KT - 1)).then_inc(ln_var[n].sem, 1)

            pe.wait_ge(p_dve.sem, p_dve.at(HEADS - 1, 20))
            pe.wait_ge(s_new.sem, s_new.at(HEADS - 1, 16))
            norm(0, 0)

            def conv(j, at, first):
                for i in range(CPE):
                    g, k0 = i // 2, 8 * (i % 2)
                    c0 = CUT if g < 2 else META
                    if i % 2 == 0 and not (first and g < 2):
                        if g == 0:
                            pe.wait_ge(c_z.sem, c_z.at(j, 0))
                        if g == 1:
                            pe.wait_ge(c_b.sem, c_b.at(j, 0))
                        if g == 2:
                            pe.wait_ge(c_c.sem, c_c.at(j))
                        if g == 3:
                            pe.wait_ge(c_v.sem, c_v.at(j, 2))

                    def ready(k):
                        pe.wait_ge(ln_l[0].sem, k0 + k + 1)

                    proj(HEAD_CH, at, CPE, i, bank_p[g % 2], T - c0, lambda k: xh[:, k0 + k, c0:T],
                         lambda k: xl[:, k0 + k, c0:T], i % 2 == 0, i % 2 == 1, ready if first and i < 2 else None)

            conv(0, 0, True)
            with pe.Fori(1, NE) as j:
                conv(j, j, False)

            def out_conv(j, first):
                for i in range(4):
                    g, k0 = i // 2, 8 * (i % 2)
                    if i % 2 == 0 and not first:
                        pe.wait_ge(o_read.sem, o_read.at(j, g - 1))

                    def ready(k):
                        pe.wait_ge(c_ml.sem, k0 + k + 1)

                    proj(HEAD_CH + CONV_CH, j, 4, i, bank_p[g % 2], NOUT, lambda k: m_hi[:, k0 + k, :],
                         lambda k: m_lo[:, k0 + k, :], i % 2 == 0, i % 2 == 1, ready if first and i < 2 else None)

            pe.wait_ge(c_z.sem, c_z.at(NE - 1))
            pe.wait_ge(c_b.sem, c_b.at(NE - 1))
            out_conv(0, True)
            with pe.Fori(1, OUT_CH // 4) as j:
                out_conv(j, False)
            pe.wait_ge(o_read.sem, o_read.at(OUT_CH // 4 - 1, 2))
            norm(1, 2)


def head_tables():
    pos = np.concatenate([np.arange(PROMPT), np.tile(PAST + np.arange(DSEQ), NB)]).astype(np.float32)
    e = -np.arange(P, dtype=np.float32) * np.float32(2) / np.float32(DK)
    ang = (pos[None, :] * (10000.0 ** e.astype(np.float64)).astype(np.float32)[:, None]).astype(np.float64)
    trig = np.stack([np.cos(ang), np.sin(ang)], 1).astype(np.float32)
    lg = np.log1p(-np.exp2(-5.0 - np.arange(HEADS)))
    tok = np.arange(T)
    samp = np.where(tok < PROMPT, -1, (tok - PROMPT) // DSEQ)
    inner = np.where(tok < PROMPT, tok, (tok - PROMPT) % DSEQ)
    tables = np.zeros((HEADS, P, TAB + HEADS), np.float32)
    for h in range(HEADS):
        for m, (t0, rows) in enumerate(KEY):
            c0, n = SC[m]
            keys, qs = tok[t0:t0 + rows], tok[CUT + c0:CUT + c0 + n]
            diff = inner[qs][None, :] - inner[keys][:, None]
            ok = (samp[qs][None, :] == samp[keys][:, None]) & (diff >= 0)
            tables[h, 0:rows, M_AT[m]:M_AT[m] + n] = np.where(ok, np.exp(np.maximum(diff, 0) * lg[h]), 0) * DK ** -0.5
        tables[h, :, QD_AT:QD_AT + NSAMP] = np.exp((inner[PROMPT:] + 1) * lg[h]) * DK ** -0.5
        last = np.where(samp < 0, PROMPT - 1, DSEQ - 1)
        tables[h, :, KD_AT:KD_AT + T] = np.exp((last - inner) * lg[h])
        tables[:, :, TAB + h] = np.exp(DSEQ * lg[h])
    con = np.zeros((P, 3 * P + 8), np.float32)
    con[:, 0:P] = np.eye(P)
    con[:, P:2 * P] = 1.0 / D
    for j in range(NSAMP):
        con[[j, NSAMP + j], 2 * P + META + j] = 1.0
    con[0:META, 3 * P] = 1.0
    for b in range(4):
        con[:, 3 * P + 1 + b] = (np.arange(P) % 32) // DSEQ == b
    return tables, trig, con


def kernel(x_prompt, x_sample, state_ret, state_conv, meta, w_ret_in, w_ret_out,
           w_conv_in, conv_w, w_conv_out, ln_g, ln_b):
    import concourse.bacc as bacc
    from concourse.bass_utils import run_bass_kernel_spmd

    A = np.asarray
    tables, trig, con = head_tables()
    x = np.concatenate([A(meta), A(x_prompt)[0], A(x_sample).reshape(NSAMP, D)], 0)

    def blocks(wm, rows):
        k, c = wm.shape
        t = wm.reshape(k // (rows * P), rows, P, c // P, P)
        return t.transpose(3, 0, 2, 1, 4).reshape(c // P, k // (rows * P), P, rows * P)

    w_in = A(w_ret_in)[0]
    qk = HEADS * DK
    b = blocks(w_in, 8)
    nq, nv = qk // P, HEADS * DVB
    parts = []
    for at, n in ((0, DKB), (nq, DKB), (2 * nq, DVB), (2 * nq + nv, DVB)):
        parts.append(b[at:at + HEADS * n].reshape(HEADS, n * 2, P, HALF))
    wo = A(w_ret_out)[0].reshape(HEADS, DVB, P, KT // 2, 2 * P).transpose(0, 3, 2, 1, 4)
    parts.append(wo.reshape(HEADS, 8, P, HALF))
    w_head = np.concatenate(parts, 1)
    bc = blocks(A(w_conv_in)[0], 8).reshape(4, NE, 2, P, HALF)
    w_conv = np.stack([bc[1], bc[2], bc[3], bc[0]], 1).reshape(NE, CPE, P, HALF)
    w_cout = blocks(A(w_conv_out)[0], 8).reshape(OUT_CH // 4, 4, P, HALF)
    ins = {
        "x_t": x.reshape(T, KT, P).transpose(2, 1, 0),
        "w_head": w_head, "w_conv": w_conv, "w_cout": w_cout,
        "s_in": A(state_ret)[0].reshape(NB, HEADS, DKB, P, DV).transpose(0, 1, 3, 2, 4),
        "tables": tables, "trig": trig, "consts": con,
        "lnp": np.stack([A(ln_g), A(ln_b)]).reshape(2, 2, KT, P).transpose(3, 0, 1, 2),
        "cw": A(conv_w)[0].reshape(WIDTH, NE, P).transpose(2, 1, 0),
        "cs_in": A(state_conv)[0].reshape(NB, 2, NE, P).transpose(3, 2, 0, 1),
    }
    outs = {
        "y_t": [P, KT, NOUT], "s_prompt": [HEADS, P, DKB, DV], "s_out": [NB, HEADS, P, DKB, DV],
        "cs_out": [P, NE, 1 + NB, 2],
    }
    nc = bacc.Bacc("TRN2", target_bir_lowering=False, num_devices=1)
    ins = {k: np.ascontiguousarray(v) for k, v in ins.items()}
    aps = {k: nc.dram_tensor(k, v.shape, F32, kind="ExternalInput").ap() for k, v in ins.items()}
    aps |= {k: nc.dram_tensor(k, s, F32, kind="ExternalOutput").ap() for k, s in outs.items()}
    hybrid_step(nc, **aps)
    r = run_bass_kernel_spmd(nc, [ins], core_ids=[0]).results[0]
    y = r["y_t"].transpose(2, 1, 0).reshape(NOUT, D)
    sp = r["s_prompt"].transpose(0, 2, 1, 3).reshape(1, 1, HEADS, DK, DV)
    ss = r["s_out"].transpose(0, 1, 3, 2, 4).reshape(1, NB, HEADS, DK, DV)
    cs = r["cs_out"].transpose(2, 3, 1, 0).reshape(1 + NB, 2, D)
    return (y[:SEQ].reshape(1, SEQ, D), y[SEQ:].reshape(NB, DSEQ, D), sp, ss, cs[None, 0:1], cs[None, 1:])
```

```python
import math
from contextlib import ExitStack

import numpy as np

import concourse.bass as bass
from concourse import mybir

F32 = mybir.dt.float32
F32R = mybir.dt.float32r
ALU = mybir.AluOpType
ACT = mybir.ActivationFunctionType

P = 128
D = 2048
KT = D // P
SEQ, META, NB, DSEQ, PAST = 256, 16, 8, 8, 2048
NSAMP = NB * DSEQ
PROMPT = META + SEQ
T = PROMPT + NSAMP
WIDTH = 3
CUT = META - (WIDTH - 1)
N = T - CUT
NOUT = N - (WIDTH - 1)
NP_ = PROMPT - CUT
HEADS, DK, DV = 8, 256, 512
DKB, DVB = DK // P, DV // P
ALPHA = float(np.float32(4.0 ** 0.25))
LN_EPS, GN_EPS = 1e-5, 1e-6

KEY = [(0, 128), (128, 128), (256, 80)]
QRY = [(0, 128 - CUT), (128 - CUT, 128), (256 - CUT, 80)]
SC = [(0, NP_), (128 - CUT, NP_ - (128 - CUT)), (256 - CUT, 80)]
A_AT = [0, NP_ + NSAMP, NP_ + NSAMP + SC[1][1] + NSAMP]
A_LEN = A_AT[2] + 80
M_AT = [0, SC[0][1], SC[0][1] + SC[1][1]]
QD_AT = M_AT[2] + SC[2][1]
KD_AT = QD_AT + NSAMP
TAB = KD_AT + T

HALF = 1024
CPH = 32
RAW = 4
SPL = 2
NE = KT
CPE = 8
HEAD_CH = HEADS * CPH
CONV_CH = NE * CPE
OUT_CH = KT * 2
ROWS_U = 10


QS_AT = {6: (0,), 7: (1,), 8: (2,), 9: (3,), 10: (4,), 11: (5,), 12: (6, 7), 13: (8,), 14: (9, 10), 15: (11,),
         16: (12, 13), 17: (14,), 18: (15,)}
KV_AT = {19: 0, 20: 1, 21: 2, 22: 3, 24: 4, 25: 5, 26: 6, 27: 7, 29: 8, 30: 9, 32: 10, 33: 11, 34: 12, 36: 13, 37: 14,
         39: 15}
KB_AT = {18: 0, 20: 1, 22: 2, 24: 3, 27: 4, 30: 5, 33: 6, 36: 7}
KV_NEXT = min(t for i, t in KV_AT.items() if i >= CPH) // 2
SA_AT = {6: 0, 8: 1, 12: 2, 14: 3, 16: 4, 17: 5, 18: 6, 20: 7}


def due(table, i, first=False, last=False):
    own = [(0, table[i])] if i in table and not last else []
    return own + ([(1, table[i + CPH])] if i + CPH in table and not first else [])


class Count:

    def __init__(self, sem, per=1, credit=0):
        self.sem, self.per, self.credit = sem, per, credit

    def at(self, r, j=1, back=0):
        return r * self.per + (j + self.credit - back * self.per)


def hybrid_step(nc, x_t, w_head, w_conv, w_cout, s_in, tables, trig, consts, lnp, cw, cs_in,
                y_t, s_prompt, s_out, cs_out):
    ctx = ExitStack()
    with ctx:
        def sb(name, shape, dt=F32):
            return ctx.enter_context(nc.sbuf_tensor(name, [P] + shape, dt))

        def count(name, per=1, credit=0):
            return Count(ctx.enter_context(nc.semaphore(name)), per, credit)

        xh, xl = sb("x_hi", [KT, T], F32R), sb("x_lo", [KT, T], F32R)
        acc = sb("residual", [KT, T])
        w_raw = sb("w_raw", [RAW, HALF])
        w_hi, w_lo = sb("w_hi", [SPL, HALF], F32R), sb("w_lo", [SPL, HALF], F32R)
        con = sb("constants", [3 * P + 8])
        gate_touch = sb("table_touch", [1])
        lnt = sb("ln_params", [2, 2, KT])
        bank_p = [ctx.enter_context(nc.psum_tensor(f"proj{i}", [P, 512], F32)) for i in range(2)]
        bank_q = ctx.enter_context(nc.psum_tensor("qs", [P, 512], F32))
        bank_r = [ctx.enter_context(nc.psum_tensor(f"side{i}", [P, 512], F32)) for i in range(5)]
        ident, ones = con[:, 0:P], con[:, P:2 * P]
        fold_raw = con[:, 2 * P:2 * P + 80]
        row_mask = con[:, 3 * P:3 * P + 1]
        bmask = con[:, 3 * P + 1:3 * P + 5]

        k_st, v_st = sb("k_stack", [2, DK], F32R), sb("v_stack", [2, DV], F32R)
        k_b = sb("k_of_sample", [2, DK], F32R)
        sb_ = sb("state_update", [4, DKB, DV])
        sd_h = sb("state_decay_of_head", [1])

        ret = ExitStack()

        def rb(name, shape, dt=F32):
            return ret.enter_context(nc.sbuf_tensor(name, [P] + shape, dt))

        tr = rb("cos_sin", [2, T])
        tab = rb("head_table", [TAB])
        sdec = rb("state_decay", [HEADS])
        fold = rb("fold", [80], F32R)
        qkz = rb("qk_or_z", [2 * DVB * T], F32R)
        raws = rb("qk_raw_or_gate", [2 * DKB * T])
        tmp = rb("tmp", [2, T])
        vt_yn = rb("v_t_or_y_norm", [3 * DV])
        v_hi, v_lo = rb("v_hi", [3, DV], F32R), rb("v_lo", [3, DV], F32R)
        k_hi, k_lo = rb("k_hi", [3, DK], F32R), rb("k_lo", [3, DK], F32R)
        a_hi, a_lo = rb("a_hi", [A_LEN], F32R), rb("a_lo", [A_LEN], F32R)
        qz = rb("q_spread", [DKB, NB * 136], F32R)
        stage = rb("stack_t_or_fold", [(DKB + DVB) * 2 * P], F32R)
        sa = rb("state_for_q_or_prompt_state", [2, DKB, DV])
        s_hi, s_lo = rb("s_hi", [2, DV], F32R), rb("s_lo", [2, DV], F32R)
        stat, mv, rstd = rb("gn_stats", [3, 6]), rb("gn_mean_var", [3, 2]), rb("gn_rstd", [3])
        gvar, mhalf = rb("gn_var_eps", [3]), rb("minus_half", [3])

        q_hi = qkz[:, 0:DKB * N].rearrange("p (d n) -> p d n", d=DKB)
        q_lo = qkz[:, DKB * N:2 * DKB * N].rearrange("p (d n) -> p d n", d=DKB)
        kk = qkz[:, 2 * DKB * N:2 * DKB * N + 2 * DKB * T].rearrange("p (s d n) -> p s d n", s=2, d=DKB)
        kt_hi, kt_lo = kk[:, 0], kk[:, 1]
        z_hi = qkz[:, 0:DVB * N].rearrange("p (d n) -> p d n", d=DVB)
        z_lo = qkz[:, DVB * N:2 * DVB * N].rearrange("p (d n) -> p d n", d=DVB)
        q_raw = raws[:, 0:DKB * N].rearrange("p (d n) -> p d n", d=DKB)
        k_raw = raws[:, 0:DKB * T].rearrange("p (d n) -> p d n", d=DKB)
        k_dec = raws[:, DKB * T:2 * DKB * T].rearrange("p (d n) -> p d n", d=DKB)
        gate = raws[:, 0:DVB * N].rearrange("p (d n) -> p d n", d=DVB)
        v_t = vt_yn[:, 0:DVB * T].rearrange("p (d n) -> p d n", d=DVB)
        y_n = vt_yn[:, :].rearrange("p (t n) -> p t n", t=3)
        st_k = stage[:, 0:DKB * 2 * P].rearrange("p (d f c n) -> p d f c n", d=DKB, f=2, c=4)
        st_v = stage[:, DKB * 2 * P:].rearrange("p (d f c n) -> p d f c n", d=DVB, f=2, c=4)
        pst = sa[:, 0]
        y_f = stage[:, 0:2 * DV].rearrange("p (s n) -> p s n", s=2)
        qz_rows = qz[:, :, :].rearrange("p k (b c) -> p k b c", c=136)

        ret.close()
        m_hi, m_lo = sb("m_hi", [NE, NOUT], F32R), sb("m_lo", [NE, NOUT], F32R)
        cwt, csi = sb("conv_w", [NE, WIDTH]), sb("conv_state_in", [NE, NB, 2])
        cso = sb("conv_state_out", [NE, 1 + NB, 2])
        w_j = sb("conv_w_block", [WIDTH])
        c_sb, z_sb, b_z, cv, m_f = (sb(n, [w]) for n, w in (
            ("c_gate", N), ("silu_z", NOUT), ("gate_product", NOUT), ("conv", NOUT), ("m", NOUT)))
        u = sb("u", [NP_ + NB * ROWS_U])
        ln_sq, ln_y = sb("ln_square", [2, N]), sb("ln_y", [2, N])
        ln_v = sb("ln_var", [3, N])
        u_s = u[:, NP_:].rearrange("p (b r) -> p b r", r=ROWS_U)
        cv_s = cv[:, SEQ:].rearrange("p (b r) -> p b r", r=DSEQ)

        con_in, trig_in, ln_in, cw_in = count("con_in"), count("trig_in"), count("ln_in"), count("cw_in")
        x_in = [count(f"x_in{i}") for i in range(4)]
        x_h, x_l, x_acc = count("x_hi_made"), count("x_lo_made"), count("residual_made")
        half_set, fold_set, zero_set = count("minus_half_set"), count("fold_set"), count("zeros_set")
        w_in = [count(f"w_in{s}", 16 * CPH // RAW) for s in range(RAW)]
        w_h = count("w_hi_made", CPH)
        w_l = count("w_lo_made", CPH, RAW)
        w_hu, w_lu = count("w_hi_used", CPH, SPL), count("w_lo_used", CPH, SPL)
        o_even = count("out_even_done", 8)
        p_act = count("proj_read_act", 8)
        p_dve = count("proj_read_dve", 20, 2)
        tab_in = count("tab_in")
        q_t, q_rot, q_h, q_l = count("q_temp"), count("q_rotated", 2), count("q_hi_made"), count("q_lo_made")
        qs_t, qz_h, qz_l = count("q_decayed"), count("q_spread_hi"), count("q_spread_lo")
        k_t, k_rot, k_h, k_l = count("k_temp"), count("k_rotated", 2), count("k_hi_made"), count("k_lo_made")
        k_d = count("k_decayed", 1)
        sk_h, sk_l = count("stack_k_hi", DKB), count("stack_k_lo", DKB)
        sv_h, sv_l = count("stack_v_hi", DVB), count("stack_v_lo", DVB)
        sd_set = count("state_decay_set")
        sc_done, a_f, a_h, a_l = count("scores_done", 3), count("a_masked", 3), count("a_hi_made", 3), count("a_lo_made", 3)
        kt_done, kn_h, kn_l = count("k_turned", 3), count("k_rows_hi", 3), count("k_rows_lo", 3)
        ks_done, ks_made = count("k_stack_turned"), count("k_stack_made")
        vt_done, vn_h, vn_l = count("v_turned", 3), count("v_rows_hi", 3), count("v_rows_lo", 3)
        vs_done, vs_made = count("v_stack_turned", 2), count("v_stack_made", 2)
        sa_in = [count(f"state_q_in{i}", 64) for i in range(2)]
        s_h = count("s_hi_made", 16)
        s_l = count("s_lo_made", 16, 4)
        s_q = count("s_used", 16, 2)
        yf_h, yf_l = count("y_fold_hi"), count("y_fold_lo")
        y_done, y_st, y_ag = count("y_done", 3), count("y_stats", 3), count("y_aggregated", 3)
        y_ve, y_rs, y_nm = count("y_var_eps"), count("y_rstd"), count("y_normed", 3)
        yt_done, z_f, z_h, z_l = count("y_turned", 4), count("z_made", 4), count("z_hi_made", 4), count("z_lo_made", 4)
        st_done, st_read = count("prompt_state_done", 2), count("prompt_state_read", 2, 1)
        st_out, st_free = count("prompt_state_out", 32), count("prompt_state_free", 1, 1)
        kb_made = count("k_b_made", 8)
        kv_done = count("kv_done", 16)
        s_new = count("s_new_made", 16, 1)
        sb_in = [count(f"state_u_in{i}", 32) for i in range(4)]
        sb_out = [count(f"state_u_out{i}", 32) for i in range(4)]
        gate_set = count("gate_set")
        passed = count("passed")
        ln_sum = [count(f"ln{i}_sum") for i in range(2)]
        ln_c, ln_s2, ln_var = ([count(f"ln{i}_{n}") for i in range(2)] for n in ("centred", "square", "var"))
        ln_ve, ln_sd, ln_rs, ln_m = ([count(f"ln{i}_{n}") for i in range(2)] for n in ("var_eps", "std", "rstd", "scaled"))
        ln_o, ln_h, ln_l, ln_a = ([count(f"ln{i}_{n}") for i in range(2)] for n in ("y", "hi", "lo", "alpha"))
        c_c, c_v, c_z, c_b = count("c_read"), count("v_read", 2), count("z_read"), count("b_read")
        c_w, c_st, c_x, c_m, c_mh, c_ml = (count("conv_w_ready"), count("conv_state_ready"), count("conv_sum", 6),
                                           count("m_made"), count("m_hi_made"), count("m_lo_made"))
        cs_made = count("conv_state_made", 2)
        o_read = count("out_read", 2)
        y_out = [count(f"y_out{i}") for i in range(2)]
        cs_st = count("conv_state_stored")

        def conv_done(j, i):
            return j * CPE + (HEAD_CH + SPL + i + 1)

        def out_done(j, i):
            return j * 4 + (HEAD_CH + CONV_CH + SPL + i + 1)

        block = ctx.enter_context(nc.Block())

        def w(src, slot):
            return src[:, slot, :].rearrange("p (k n) -> p k n", k=8)

        @block.sync
        def _(sp):
            sp.dma_start(con[:, :], consts).then_inc(con_in.sem, 16)

            def load_chunk(base, r, per, i, src):
                sp.wait_ge(w_l.sem, r * per + (base + i + 1))
                sp.dma_start(w_raw[:, i % RAW, :], src).then_inc(w_in[i % RAW].sem, 16)

            for c in range(4):
                sp.dma_start(acc[:, 4 * c:4 * c + 4, :], x_t[:, 4 * c:4 * c + 4, :]).then_inc(x_in[c].sem, 16)
                if c in (1, 3):
                    load_chunk(0, 0, CPH, c // 2, w_head[0, c // 2])
            sp.dma_start(tr[:, :, :], trig).then_inc(trig_in.sem, 16)
            sp.dma_start(sdec[:, :], tables[0, :, TAB:TAB + HEADS]).then_inc(trig_in.sem, 16)
            sp.dma_start(lnt[:, :, :, :], lnp).then_inc(ln_in.sem, 16)

            def head_loads(h, first):
                for i in range(first, CPH):
                    load_chunk(0, h, CPH, i, w_head[h, i])
                    if i in SA_AT:
                        b = SA_AT[i]
                        sp.wait_ge(s_l.sem, s_l.at(h, 2 * b - 2))
                        if b == 0:
                            sp.sem_inc(passed.sem, 1)
                            sp.wait_ge(st_free.sem, st_free.at(h, 0))
                        sp.dma_start(sa[:, b % 2, :, :], s_in[b, h]).then_inc(sa_in[b % 2].sem, 16)

            head_loads(0, 2)
            with sp.Fori(1, HEADS) as h:
                head_loads(h, 0)
            with sp.Fori(0, NE) as j:
                for i in range(CPE):
                    load_chunk(HEAD_CH, j, CPE, i, w_conv[j, i])
            with sp.Fori(0, OUT_CH // 4) as j:
                for i in range(4):
                    load_chunk(HEAD_CH + CONV_CH, j, 4, i, w_cout[j, i])
            for k in range(KT):
                sp.wait_ge(ln_o[1].sem, k + 1)
                sp.dma_start(y_t[:, k, :], ln_y[:, k % 2, 2:N]).then_inc(y_out[k % 2].sem, 16)
            for i in range(2):
                sp.wait_ge(y_out[i].sem, 16 * KT // 2)
            sp.wait_ge(cs_st.sem, 16)

        @block.gpsimd
        def _(pool):
            pool.sem_inc(st_free.sem, st_free.credit)
            pool.memset(mhalf[:, :], -0.5).then_inc(half_set.sem, 1)
            pool.wait_ge(x_in[3].sem, 16)
            pool.dma_start(tab[:, :], tables[0, :, 0:TAB]).then_inc(tab_in.sem, 16)
            for b in range(4):
                pool.dma_start(sb_[:, b, :, :], s_in[b, 0]).then_inc(sb_in[b].sem, 16)
            pool.wait_ge(half_set.sem, 1)

            def store(h, b, back=0):
                pool.wait_ge(s_new.sem, s_new.at(h, 2 * b + 2, back))
                pool.sem_inc(passed.sem, 1)
                pool.dma_start(s_out[b, h - back], sb_[:, b % 4, :, :]).then_inc(sb_out[b % 4].sem, 16)

            def reload(h, b, back=0):
                pool.wait_ge(sb_out[b % 4].sem, sb_out[b % 4].at(h, 16 * (b // 4 + 1), back))
                pool.sem_inc(passed.sem, 1)
                nxt = s_in[b + 4, h - back] if b < NB - 4 else s_in[b + 4 - NB, h + 1 - back]
                pool.dma_start(sb_[:, b % 4, :, :], nxt).then_inc(sb_in[b % 4].sem, 16)

            def head(h, first, last):
                if not first:
                    for b in range(KV_NEXT, NB):
                        store(h, b, 1)
                        reload(h, b - 1, 1)
                pool.wait_ge(y_ve.sem, y_ve.at(h))
                pool.tensor_tensor(rstd[:, :], gvar[:, :], mhalf[:, :], ALU.pow).then_inc(y_rs.sem, 1)
                if not last:
                    pool.wait_ge(a_f.sem, a_f.at(h, 3))
                    pool.sem_inc(passed.sem, 1)
                    pool.dma_start(tab[:, :], tables[h + 1, :, 0:TAB]).then_inc(tab_in.sem, 16)
                for b in range(KV_NEXT):
                    if b == 2:
                        pool.wait_ge(st_read.sem, st_read.at(h, 2))
                        pool.sem_inc(passed.sem, 1)
                        pool.dma_start(s_prompt[h], pst[:, :, :]).then_inc(st_out.sem, 16)
                    if b == 4:
                        pool.wait_ge(st_out.sem, h * 16 + 16)
                        pool.sem_inc(st_free.sem, 1)
                    store(h, b)
                    if b:
                        reload(h, b - 1)
                    elif not first:
                        reload(h, NB - 1, 1)

            head(0, True, False)
            with pool.Fori(1, HEADS - 1) as h:
                head(h, False, False)
            head(HEADS - 1, False, True)
            pool.wait_ge(ln_sum[0].sem, 1)
            pool.dma_start(cwt[:, :, :], cw).then_inc(cw_in.sem, 16)
            pool.dma_start(csi[:, :, :, :], cs_in).then_inc(cw_in.sem, 16)
            for b in range(KV_NEXT, NB):
                store(HEADS, b, 1)
            for b in range(4):
                pool.wait_ge(sb_out[b].sem, 32 * HEADS)
            pool.wait_ge(cs_made.sem, 2 * NE)
            pool.dma_start(cs_out, cso[:, :, :, :]).then_inc(cs_st.sem, 16)
            pool.wait_ge(cs_st.sem, 16)

        @block.scalar
        def _(act):
            def round_chunk(base, r, per, i):
                rounds = per // RAW
                first = base // RAW
                act.wait_ge(w_in[i % RAW].sem, r * (16 * rounds) + 16 * (first + i // RAW + 1))
                act.wait_ge(w_hu.sem, r * per + (base + i + 1))
                act.wait_ge(w_l.sem, r * per + (base + i + 1 - SPL + RAW))
                act.copy(w_hi[:, i % SPL, :], w_raw[:, i % RAW, :]).then_inc(w_h.sem, 1)

            act.sem_inc(st_read.sem, st_read.credit)
            act.wait_ge(con_in.sem, 16)
            act.wait_ge(zero_set.sem, 1)
            act.copy(fold[:, :], fold_raw).then_inc(fold_set.sem, 1)
            for c in range(4):
                act.wait_ge(x_in[c].sem, 16)
                act.copy(xh[:, 4 * c:4 * c + 4, :], acc[:, 4 * c:4 * c + 4, :]).then_inc(x_h.sem, 1)
                if c == 1:
                    round_chunk(0, 0, CPH, 0)

            def kb_make(h, b, back):
                if b >= 2:
                    act.wait_ge(kv_done.sem, kv_done.at(h, 2 * b - 2, back))
                act.wait_ge(ks_made.sem, ks_made.at(h, 1, back))
                act.activation(k_b[:, b % 2, :], k_st[:, b // 4, :], ACT.Copy,
                               scale=bmask[:, b % 4:b % 4 + 1]).then_inc(kb_made.sem, 1)

            def head(h, first):
                act.activation(gate_touch[:, :], con[:, 0:1], ACT.Silu).then_inc(gate_set.sem, 1)

                def s_round(t):
                    b = t // 2
                    if t % 2 == 0:
                        act.wait_ge(sa_in[b % 2].sem, h * 64 + 16 * (b // 2 + 1))
                    act.wait_ge(s_q.sem, s_q.at(h, t - 1))
                    act.copy(s_hi[:, t % 2, :], sa[:, b % 2, t % 2, :]).then_inc(s_h.sem, 1)

                def side(i):
                    if i == 4:
                        act.wait_ge(q_rot.sem, q_rot.at(h, 2))
                        act.copy(q_hi, q_raw).then_inc(q_h.sem, 1)
                        act.wait_ge(qs_t.sem, qs_t.at(h))
                        act.copy(qz_rows[:, :, :, 0:8],
                                 tmp[:, 0, 0:DKB * NSAMP].rearrange("p (d b r) -> p d b r", d=DKB, b=NB)
                                 ).then_inc(qz_h.sem, 1)
                    if i == 8:
                        act.wait_ge(k_rot.sem, k_rot.at(h, 2))
                        act.copy(kt_hi, k_raw).then_inc(k_h.sem, 1)
                    if i == 9:
                        act.wait_ge(k_d.sem, k_d.at(h))
                        for d in range(DKB):
                            src = k_dec[:, d, PROMPT:].rearrange("p (f n) -> p f n", f=2)
                            act.copy(st_k[:, d, :, 0, :], src)
                            act.copy(st_k[:, d, :, 1, :], src).then_inc(sk_h.sem, 1)
                    if 10 <= i <= 16 and i % 2 == 0:
                        g = 4 + (i - 10) // 2
                        act.wait_ge(w_lu.sem, w_lu.at(h, 2 * g + 2))
                        act.copy(v_t[:, g - 4, :], bank_p[g % 2][:, 0:T]).then_inc(p_act.sem, 1)
                    if i == 12:
                        for m in range(3):
                            rows = KEY[m][1]
                            src = (bank_r[3][0:rows, 256 * m:256 * m + 256] if m < 2 else bank_r[4][0:rows, 0:256])
                            act.wait_ge(kt_done.sem, kt_done.at(h, m + 1))
                            if m < 2:
                                act.copy(k_hi[0:rows, m, :], src).then_inc(kn_h.sem, 1)
                            else:
                                act.activation(k_hi[0:rows, m, :], src, ACT.Copy,
                                               scale=row_mask[0:rows, :]).then_inc(kn_h.sem, 1)
                    if i == 12:
                        act.wait_ge(ks_done.sem, ks_done.at(h))
                        act.copy(k_st[:, :, :], bank_r[0][:, :].rearrange("p (f n) -> p f n", f=2)).then_inc(ks_made.sem, 1)
                    if i in (13, 14):
                        for m in ((0, 1), (2,))[i - 13]:
                            act.wait_ge(a_f.sem, a_f.at(h, m + 1))
                            n = SC[m][1]
                            at = tmp[:, m % 2, 0:n]
                            rows = KEY[m][1]
                            act.copy(a_hi[0:rows, A_AT[m]:A_AT[m] + n], at[0:rows]).then_inc(a_h.sem, 1)
                    if i == 16:
                        act.wait_ge(p_act.sem, p_act.at(h, 4))
                        for d in range(DVB):
                            src = v_t[:, d, PROMPT:].rearrange("p (f n) -> p f n", f=2)
                            act.copy(st_v[:, d, :, 0, :], src)
                            act.copy(st_v[:, d, :, 2, :], src).then_inc(sv_h.sem, 1)
                    if i == 17:
                        for m in range(3):
                            rows = KEY[m][1]
                            act.wait_ge(vt_done.sem, vt_done.at(h, m + 1))
                            act.copy(v_hi[0:rows, m, :], bank_r[m][0:rows, :]).then_inc(vn_h.sem, 1)
                    if i == 18:
                        for f in range(2):
                            act.wait_ge(vs_done.sem, vs_done.at(h, f + 1))
                            act.copy(v_st[:, f, :], bank_r[3 + f][:, :]).then_inc(vs_made.sem, 1)
                    if 18 <= i <= 24 and i % 2 == 0:
                        g = 8 + (i - 18) // 2
                        act.wait_ge(w_lu.sem, w_lu.at(h, 2 * g + 2))
                        act.activation(gate[:, g - 8, :], bank_p[g % 2][:, 0:N], ACT.Silu).then_inc(p_act.sem, 1)
                    if i == 19:
                        act.wait_ge(s_q.sem, s_q.at(h, 2 * NB))
                        act.copy(y_f[:, 0, :], bank_q[:, :]).then_inc(yf_h.sem, 1)
                    if i in (23, 24):
                        d = i - 23
                        act.wait_ge(st_done.sem, st_done.at(h, d + 1))
                        act.copy(pst[:, d, :], bank_q[:, :]).then_inc(st_read.sem, 1)
                    if i in (23, 24):
                        for j in range(3) if i == 23 else (3,):
                            act.wait_ge(z_f.sem, z_f.at(h, j + 1))
                            act.copy(z_hi[:, j, :], tmp[:, j % 2, 0:N]).then_inc(z_h.sem, 1)
                    for back, b in due(KB_AT, i, first):
                        kb_make(h, b, back)

                for i in range(CPH):
                    if i:
                        round_chunk(0, h, CPH, i)
                    side(i)
                    for t in QS_AT.get(i, ()):
                        s_round(t)
                round_chunk(0, h, CPH, CPH)

            head(0, True)
            with act.Fori(1, HEADS) as h:
                head(h, False)

            def norm(n, c0):
                for k in range(KT):
                    act.wait_ge(ln_c[n].sem, k + 1)
                    if k >= 2:
                        act.wait_ge(ln_var[n].sem, k - 1)
                    act.activation(ln_sq[:, k % 2, c0:N], acc[:, k, CUT + c0:T], ACT.Square).then_inc(ln_s2[n].sem, 1)
                act.wait_ge(ln_ve[n].sem, 1)
                act.activation(ln_v[:, 1, c0:N], ln_v[:, 0, c0:N], ACT.Sqrt).then_inc(ln_sd[n].sem, 1)

            round_chunk(HEAD_CH, 0, CPE, 1)
            norm(0, 0)
            for k in range(KT):
                act.wait_ge(ln_o[0].sem, k + 1)
                act.copy(xh[:, k, CUT:T], ln_y[:, k % 2, :]).then_inc(ln_h[0].sem, 1)
                act.mul(acc[:, k, CUT:T], ln_y[:, k % 2, :], ALPHA).then_inc(ln_a[0].sem, 1)

            def conv_hi(j):
                act.wait_ge(c_m.sem, c_m.at(j))
                act.copy(m_hi[:, bass.ds(j, 1), :].rearrange("p a n -> p (a n)"), m_f[:, :]).then_inc(c_mh.sem, 1)

            def conv(j, done):
                act.activation(gate_touch[:, :], con[:, 0:1], ACT.Silu).then_inc(gate_set.sem, 1)
                for i in range(CPE):
                    if i > done:
                        round_chunk(HEAD_CH, j, CPE, i)
                    if done:
                        for back, b in due(KB_AT, i, last=True):
                            kb_make(HEADS, b, back)
                    if i == 2:
                        act.wait_ge(w_lu.sem, conv_done(j, 1))
                        act.copy(c_sb[:, :], bank_p[0][:, 0:N]).then_inc(c_c.sem, 1)
                    if i == 6:
                        act.wait_ge(w_lu.sem, conv_done(j, 5))
                        act.activation(z_sb[:, :], bank_p[0][:, 0:NOUT], ACT.Silu).then_inc(c_z.sem, 1)
                round_chunk(HEAD_CH, j, CPE, CPE)
                conv_hi(j)

            conv(0, 1)
            with act.Fori(1, NE) as j:
                conv(j, 0)

            def out_chunks(j, last):
                for i in range(1, 4 if last else 5):
                    round_chunk(HEAD_CH + CONV_CH, j, 4, i)

            with act.Fori(0, OUT_CH // 4 - 1) as j:
                out_chunks(j, False)
            out_chunks(OUT_CH // 4 - 1, True)
            norm(1, 2)

        @block.vector
        def _(dve):
            f = lambda ap: ap.bitcast(F32)
            TT = dve.tensor_tensor

            def rest_chunk(base, r, per, i):
                dve.wait_ge(w_h.sem, r * per + (base + i + 1))
                dve.wait_ge(w_lu.sem, r * per + (base + i + 1))
                TT(w_lo[:, i % SPL, :], w_raw[:, i % RAW, :], f(w_hi[:, i % SPL, :]), ALU.subtract).then_inc(w_l.sem, 1)

            dve.sem_inc(w_l.sem, w_l.credit)
            dve.sem_inc(p_dve.sem, p_dve.credit)
            dve.sem_inc(s_l.sem, s_l.credit)
            dve.sem_inc(s_new.sem, s_new.credit)
            dve.memzero(f(a_hi[:, :]))
            dve.memzero(f(a_lo[:, :]))
            dve.memzero(f(qz[:, :, :]))
            dve.memset(mv[:, :, :], 0.0).then_inc(zero_set.sem, 1)
            for c in range(4):
                cs = slice(4 * c, 4 * c + 4)
                dve.wait_ge(x_h.sem, c + 1)
                TT(xl[:, cs, :], acc[:, cs, :], f(xh[:, cs, :]), ALU.subtract).then_inc(x_l.sem, 1)
                if c == 1:
                    rest_chunk(0, 0, CPH, 0)
            for c in range(4):
                dve.wait_ge(x_l.sem, c + 1)
                cs = acc[:, 4 * c:4 * c + 4, CUT:T]
                dve.tensor_scalar(cs, cs, ALPHA, None, ALU.mult).then_inc(x_acc.sem, 1)
            dve.wait_ge(x_acc.sem, 4)
            dve.wait_ge(trig_in.sem, 32)
            dve.wait_ge(zero_set.sem, 1)
            add = ALU.add

            def kv_update(h, t, back):
                b, bank = t // 2, bank_r[3 + t % 2]
                if t % 2 == 0:
                    dve.wait_ge(sb_in[b % 4].sem, sb_in[b % 4].at(h, 16 * (b // 4 + 1), back))
                dve.wait_ge(kv_done.sem, kv_done.at(h, t + 1, back))
                dve.wait_ge(sd_set.sem, sd_set.at(h, 1, back))
                s = sb_[:, b % 4, t % 2, :]
                dve.scalar_tensor_tensor(s, s, sd_h[:, :], bank[:, :], ALU.mult, add).then_inc(s_new.sem, 1)

            def head(h, first):

                def q_or_k(i, bank, raw, t_sem, rot_sem, c0):
                    cos, sin = tr[:, 0, c0:T], tr[:, 1, c0:T]
                    n = T - c0
                    src = bank[:, 0:n]
                    if i == 0:
                        TT(raw[:, 0, :], src, cos, ALU.mult)
                        TT(raw[:, 1, :], src, sin, ALU.mult).then_inc(p_dve.sem, 1)
                    else:
                        TT(tmp[:, 0, 0:n], src, sin, ALU.mult).then_inc(t_sem.sem, 1)
                        TT(tmp[:, 1, 0:n], src, cos, ALU.mult).then_inc(p_dve.sem, 1)
                        dve.wait_ge(t_sem.sem, t_sem.at(h))
                        TT(raw[:, 0, :], raw[:, 0, :], tmp[:, 0, 0:n], ALU.subtract).then_inc(rot_sem.sem, 1)
                        dve.wait_ge(p_dve.sem, p_dve.at(h, 2 if raw is q_raw else 4))
                        TT(raw[:, 1, :], raw[:, 1, :], tmp[:, 1, 0:n], add).then_inc(rot_sem.sem, 1)

                def s_rest(t):
                    b = t // 2
                    dve.wait_ge(s_h.sem, s_h.at(h, t + 1))
                    dve.wait_ge(s_q.sem, s_q.at(h, t - 1))
                    TT(s_lo[:, t % 2, :], sa[:, b % 2, t % 2, :], f(s_hi[:, t % 2, :]), ALU.subtract).then_inc(s_l.sem, 1)

                def out_read(c):
                    for e in range(2):
                        if e == 0:
                            dve.wait_ge(o_even.sem, o_even.at(h, c + 1))
                        else:
                            dve.wait_ge(w_lu.sem, w_lu.at(h, 24 + c + 1))
                        a = acc[:, 2 * c + e, CUT:T]
                        TT(a, a, bank_p[e][:, 0:N], add).then_inc(p_dve.sem, 1)

                def side(i):
                    if i == 2:
                        dve.wait_ge(w_lu.sem, w_lu.at(h, 2))
                        q_or_k(0, bank_p[0], q_raw, q_t, q_rot, CUT)
                    if i == 4:
                        dve.wait_ge(w_lu.sem, w_lu.at(h, 4))
                        q_or_k(1, bank_p[1], q_raw, q_t, q_rot, CUT)
                        dve.wait_ge(tab_in.sem, h * 16 + 16)
                        dve.wait_ge(q_rot.sem, q_rot.at(h, 2))
                        dec = tab[:, QD_AT:QD_AT + NSAMP].unsqueeze(1).to_broadcast([P, DKB, NSAMP])
                        qs = tmp[:, 0, 0:DKB * NSAMP].rearrange("p (d n) -> p d n", d=DKB)
                        TT(qs, q_raw[:, :, NP_:N], dec, ALU.mult).then_inc(qs_t.sem, 1)
                        dve.wait_ge(q_h.sem, q_h.at(h))
                        TT(q_lo, q_raw, f(q_hi), ALU.subtract).then_inc(q_l.sem, 1)
                        dve.wait_ge(qz_h.sem, qz_h.at(h))
                        qs4 = qs.rearrange("p d (b r) -> p d b r", b=NB)
                        for d in range(DKB):
                            z = TT(qz_rows[:, d, :, 64:72], qs4[:, d], f(qz_rows[:, d, :, 0:8]), ALU.subtract)
                        z.then_inc(qz_l.sem, 1)
                    if i == 6:
                        dve.wait_ge(w_lu.sem, w_lu.at(h, 6))
                        q_or_k(0, bank_p[0], k_raw, k_t, k_rot, 0)
                    if i == 8:
                        dve.wait_ge(w_lu.sem, w_lu.at(h, 8))
                        q_or_k(1, bank_p[1], k_raw, k_t, k_rot, 0)
                        dve.wait_ge(k_h.sem, k_h.at(h))
                        TT(kt_lo, k_raw, f(kt_hi), ALU.subtract).then_inc(k_l.sem, 1)
                    if i == 9:
                        dve.wait_ge(k_rot.sem, k_rot.at(h, 2))
                        dec = tab[:, KD_AT:KD_AT + T].unsqueeze(1).to_broadcast([P, DKB, T])
                        TT(k_dec, k_raw, dec, ALU.mult).then_inc(k_d.sem, 1)
                        for d in range(DKB):
                            dve.wait_ge(sk_h.sem, sk_h.at(h, d + 1))
                            src = k_dec[:, d, PROMPT:].rearrange("p (f n) -> p f n", f=2)
                            hi = f(st_k[:, d, :, 0, :])
                            TT(st_k[:, d, :, 2, :], src, hi, ALU.subtract)
                            TT(st_k[:, d, :, 3, :], src, hi, ALU.subtract).then_inc(sk_l.sem, 1)
                    if i == 12:
                        for m in range(3):
                            rows = KEY[m][1]
                            src = (bank_r[3][0:rows, 256 * m:256 * m + 256] if m < 2 else bank_r[4][0:rows, 0:256])
                            dve.wait_ge(kn_h.sem, kn_h.at(h, max(m + 1, 2)))
                            o, hi = k_lo[0:rows, m, :], f(k_hi[0:rows, m, :])
                            if m < 2:
                                TT(o, src, hi, ALU.subtract).then_inc(kn_l.sem, 1)
                            else:
                                dve.scalar_tensor_tensor(o, src, row_mask[0:rows, :], hi, ALU.mult,
                                                         ALU.subtract).then_inc(kn_l.sem, 1)
                    if i in (13, 14):
                        ms = ((0, 1), (2,))[i - 13]
                        for m in ms:
                            rows, n, bank = KEY[m][1], SC[m][1], bank_r[(1, 2, 0)[m]]
                            dve.wait_ge(sc_done.sem, sc_done.at(h, m + 1))
                            if m >= 2:
                                dve.wait_ge(a_l.sem, a_l.at(h, m - 1))
                            TT(tmp[0:rows, m % 2, 0:n], bank[0:rows, 0:n], tab[0:rows, M_AT[m]:M_AT[m] + n],
                               ALU.mult).then_inc(a_f.sem, 1)
                        for m in ms:
                            rows, n = KEY[m][1], SC[m][1]
                            at = slice(A_AT[m], A_AT[m] + n)
                            dve.wait_ge(a_h.sem, a_h.at(h, m + 1))
                            TT(a_lo[0:rows, at], tmp[0:rows, m % 2, 0:n], f(a_hi[0:rows, at]), ALU.subtract).then_inc(a_l.sem, 1)
                    if i == 16:
                        for d in range(DVB):
                            dve.wait_ge(sv_h.sem, sv_h.at(h, d + 1))
                            src = v_t[:, d, PROMPT:].rearrange("p (f n) -> p f n", f=2)
                            hi = f(st_v[:, d, :, 0, :])
                            TT(st_v[:, d, :, 1, :], src, hi, ALU.subtract)
                            TT(st_v[:, d, :, 3, :], src, hi, ALU.subtract).then_inc(sv_l.sem, 1)
                    if i == 17:
                        for m in range(3):
                            rows = KEY[m][1]
                            dve.wait_ge(vn_h.sem, vn_h.at(h, m + 1))
                            TT(v_lo[0:rows, m, :], bank_r[m][0:rows, :], f(v_hi[0:rows, m, :]), ALU.subtract).then_inc(vn_l.sem, 1)
                    if i == 19:
                        dve.wait_ge(s_new.sem, s_new.at(h, 0))
                        dve.tensor_copy(sd_h[:, :], sdec[:, bass.ds(h, 1)]).then_inc(sd_set.sem, 1)
                        dve.wait_ge(yf_h.sem, yf_h.at(h))
                        TT(y_f[:, 1, :], bank_q[:, :], f(y_f[:, 0, :]), ALU.subtract).then_inc(yf_l.sem, 1)
                    if i in (19, 20):
                        for t in ((0, 1), (2,))[i - 19]:
                            rows = QRY[t][1]
                            dve.wait_ge(y_done.sem, y_done.at(h, t + 1))
                            dve.bn_stats(stat[0:rows, t, :], bank_r[t][0:rows, :]).then_inc(y_st.sem, 1)
                            dve.wait_ge(y_st.sem, y_st.at(h, t + 1))
                            dve.sem_inc(passed.sem, 1)
                            dve.bn_aggr(mv[0:rows, t, :], stat[0:rows, t, :]).then_inc(y_ag.sem, 1)
                    if i == 20:
                        dve.wait_ge(y_ag.sem, y_ag.at(h, 3))
                        dve.tensor_scalar(gvar[:, :], mv[:, :, 1], GN_EPS, None, add).then_inc(y_ve.sem, 1)
                    if i == 21:
                        dve.wait_ge(y_rs.sem, y_rs.at(h))
                        for t in range(3):
                            rows = QRY[t][1]
                            dve.tensor_scalar(y_n[0:rows, t, :], bank_r[t][0:rows, :], mv[0:rows, t, 0:1],
                                              rstd[0:rows, t:t + 1], ALU.subtract, ALU.mult).then_inc(y_nm.sem, 1)
                    if i in (23, 24):
                        for j in range(3) if i == 23 else (3,):
                            dve.wait_ge(yt_done.sem, yt_done.at(h, j + 1))
                            dve.wait_ge(p_act.sem, p_act.at(h, 5 + j))
                            if j >= 2:
                                dve.wait_ge(z_l.sem, z_l.at(h, j - 1))
                            TT(tmp[:, j % 2, 0:N], bank_r[j % 3][:, 0:N], gate[:, j, :], ALU.mult).then_inc(z_f.sem, 1)
                            dve.wait_ge(z_h.sem, z_h.at(h, j + 1))
                            TT(z_lo[:, j, :], tmp[:, j % 2, 0:N], f(z_hi[:, j, :]), ALU.subtract).then_inc(z_l.sem, 1)
                    if i >= 25:
                        out_read(i - 25)
                    for back, t in due(KV_AT, i - 1, first):
                        kv_update(h, t, back)

                for i in range(CPH):
                    if i:
                        rest_chunk(0, h, CPH, i)
                    side(i)
                    for t in QS_AT.get(i, ()):
                        s_rest(t)
                rest_chunk(0, h, CPH, CPH)
                out_read(7)

            head(0, True)
            with dve.Fori(1, HEADS) as h:
                head(h, False)

            def norm(n, c0):
                mean, var = bank_r[0][:, c0:N], bank_r[1][:, c0:N]
                dve.wait_ge(ln_sum[n].sem, 1)
                for k in range(KT):
                    a = acc[:, k, CUT + c0:T]
                    TT(a, a, mean, ALU.subtract).then_inc(ln_c[n].sem, 1)
                dve.wait_ge(ln_var[n].sem, KT)
                dve.tensor_scalar(ln_v[:, 0, c0:N], var, LN_EPS, None, add).then_inc(ln_ve[n].sem, 1)
                dve.wait_ge(ln_sd[n].sem, 1)
                dve.reciprocal(ln_v[:, 2, c0:N], ln_v[:, 1, c0:N]).then_inc(ln_rs[n].sem, 1)
                dve.wait_ge(ln_rs[n].sem, 1)
                dve.wait_ge(ln_in.sem, 16)
                for k in range(KT):
                    a = acc[:, k, CUT + c0:T]
                    TT(a, a, ln_v[:, 2, c0:N], ALU.mult).then_inc(ln_m[n].sem, 1)
                    dve.wait_ge(ln_m[n].sem, k + 1)
                    if n == 0:
                        if k >= 2:
                            dve.wait_ge(ln_a[0].sem, k - 1)
                    elif k >= 2:
                        dve.wait_ge(y_out[k % 2].sem, 16 * (k // 2))
                    dve.tensor_scalar(ln_y[:, k % 2, c0:N], a, lnt[:, 0, n, k:k + 1], lnt[:, 1, n, k:k + 1],
                                      ALU.mult, add).then_inc(ln_o[n].sem, 1)
                    if n == 0:
                        dve.wait_ge(ln_h[0].sem, k + 1)
                        TT(xl[:, k, CUT:T], ln_y[:, k % 2, :], f(xh[:, k, CUT:T]), ALU.subtract).then_inc(ln_l[0].sem, 1)

            rest_chunk(HEAD_CH, 0, CPE, 1)
            norm(0, 0)
            dve.wait_ge(cw_in.sem, 32)

            def conv(j, done):
                for i in range(CPE):
                    if i > done:
                        rest_chunk(HEAD_CH, j, CPE, i)
                    if done:
                        for back, t in due(KV_AT, i - 1, last=True):
                            kv_update(HEADS, t, back)
                    if i == 0:
                        dve.tensor_copy(w_j[:, :], cwt[:, bass.ds(j, 1), :].rearrange("p a b -> p (a b)")).then_inc(c_w.sem, 1)
                        dve.tensor_copy(u_s[:, :, 0:2], csi[:, bass.ds(j, 1), :, :].rearrange("p a b c -> p (a b) c")).then_inc(c_st.sem, 1)
                    if i == 4:
                        dve.wait_ge(w_lu.sem, conv_done(j, 3))
                        dve.wait_ge(c_c.sem, c_c.at(j))
                        TT(u[:, 0:NP_], bank_p[1][:, 0:NP_], c_sb[:, 0:NP_], ALU.mult).then_inc(c_v.sem, 1)
                        bs = lambda ap: ap.rearrange("p (b r) -> p b r", r=DSEQ)
                        TT(u_s[:, :, 2:], bs(bank_p[1][:, NP_:N]), bs(c_sb[:, NP_:N]), ALU.mult).then_inc(c_v.sem, 1)
                        dve.wait_ge(c_v.sem, c_v.at(j, 2))
                        dve.wait_ge(c_w.sem, c_w.at(j))
                        dve.wait_ge(c_st.sem, c_st.at(j))
                        for n in range(WIDTH):
                            w0 = w_j[:, n:n + 1]
                            for s, (dst, src) in enumerate(((cv[:, 0:SEQ], u[:, n:n + SEQ]), (cv_s, u_s[:, :, n:n + DSEQ]))):
                                if n == 0:
                                    dve.tensor_scalar(dst, src, w0, None, ALU.mult).then_inc(c_x.sem, 1)
                                else:
                                    dve.wait_ge(c_x.sem, c_x.at(j, 2 * (n - 1) + s + 1))
                                    dve.scalar_tensor_tensor(dst, src, w0, dst, ALU.mult, add).then_inc(c_x.sem, 1)
                        dve.tensor_copy(cso[:, bass.ds(j, 1), 0, :].rearrange("p a c -> p (a c)"), u[:, NP_ - 2:NP_]).then_inc(cs_made.sem, 1)
                        dve.tensor_copy(cso[:, bass.ds(j, 1), 1:, :].rearrange("p a b c -> p (a b) c"), u_s[:, :, DSEQ:]).then_inc(cs_made.sem, 1)

            def conv_end(j):
                dve.wait_ge(w_lu.sem, conv_done(j, 7))
                dve.wait_ge(c_z.sem, c_z.at(j))
                TT(b_z[:, :], bank_p[1][:, 0:NOUT], z_sb[:, :], ALU.mult).then_inc(c_b.sem, 1)
                dve.wait_ge(c_b.sem, c_b.at(j))
                dve.wait_ge(c_x.sem, c_x.at(j, 6))
                TT(m_f[:, :], b_z[:, :], cv[:, :], ALU.mult).then_inc(c_m.sem, 1)

            def conv_rest(j):
                dve.wait_ge(c_mh.sem, c_mh.at(j))
                at = bass.ds(j, 1)
                sq = lambda ap: ap.rearrange("p a n -> p (a n)")
                TT(sq(m_lo[:, at, :]), m_f[:, :], f(sq(m_hi[:, at, :])), ALU.subtract).then_inc(c_ml.sem, 1)

            def conv_all(j, done):
                conv(j, done)
                rest_chunk(HEAD_CH, j, CPE, CPE)
                if done:
                    for back, t in due(KV_AT, CPE - 1, last=True):
                        kv_update(HEADS, t, back)
                conv_end(j)
                conv_rest(j)

            conv_all(0, 1)
            with dve.Fori(1, NE) as j:
                conv_all(j, 0)

            def block_read(j, e):
                dve.wait_ge(w_lu.sem, out_done(j, 2 * e + 1))
                a = acc[:, bass.ds(2 * j + e, 1), META:T].rearrange("p a n -> p (a n)")
                TT(a, a, bank_p[e][:, 0:NOUT], add).then_inc(o_read.sem, 1)

            def out_chunks(j, last):
                for i in range(1, 4 if last else 5):
                    rest_chunk(HEAD_CH + CONV_CH, j, 4, i)
                    if i == 2:
                        block_read(j, 0)
                block_read(j, 1)

            with dve.Fori(0, OUT_CH // 4 - 1) as j:
                out_chunks(j, False)
            out_chunks(OUT_CH // 4 - 1, True)
            norm(1, 2)

        @block.tensor
        def _(pe):
            mm = pe.matmul

            def three(out, a_hi_, a_lo_, b_hi_, b_lo_, start, stop):
                mm(out, a_hi_, b_hi_, start=start, stop=False)
                mm(out, a_hi_, b_lo_, start=False, stop=False)
                return mm(out, a_lo_, b_hi_, start=False, stop=stop)

            def turn(out, src):
                n = src.shape[0]
                return pe.transpose(out, src if src.dtype == F32 else src.bitcast(F32), ident[0:n, 0:n])

            def proj(base, r, per, i, bank, n, rhs_h, rhs_l, first, last, by_block=None):
                wh, wl = w(w_hi, i % SPL), w(w_lo, i % SPL)
                pe.wait_ge(w_h.sem, r * per + (base + i + 1))
                for k in range(8):
                    if by_block:
                        by_block(k)
                    mm(bank[:, 0:n], wh[:, k, :], rhs_h(k), start=(first and k == 0), stop=False)
                    x = mm(bank[:, 0:n], wh[:, k, :], rhs_l(k), start=False, stop=False)
                x.then_inc(w_hu.sem, 1)
                pe.wait_ge(w_l.sem, r * per + (base + i + 1 + RAW))
                for k in range(8):
                    x = mm(bank[:, 0:n], wl[:, k, :], rhs_h(k), start=False, stop=(last and k == 7))
                x.then_inc(w_lu.sem, 1)

            pe.sem_inc(w_hu.sem, w_hu.credit)
            pe.sem_inc(w_lu.sem, w_lu.credit)
            pe.sem_inc(s_q.sem, s_q.credit)
            pe.wait_ge(con_in.sem, 16)
            pe.wait_ge(fold_set.sem, 1)
            pe.wait_ge(zero_set.sem, 1)

            def kv_multiply(h, t, back):
                b = t // 2
                if t < 2:
                    pe.wait_ge(vs_made.sem, vs_made.at(h, t + 1))
                else:
                    pe.wait_ge(s_new.sem, s_new.at(h, t - 1, back))
                pe.wait_ge(kb_made.sem, kb_made.at(h, b + 1, back))
                mm(bank_r[3 + t % 2][:, :], k_b[:, b % 2, P * (t % 2):P * (t % 2) + P], v_st[:, b // 4, :],
                   start=True, stop=True).then_inc(kv_done.sem, 1)

            def head(h, first):
                def side(i):
                    if i == 10:
                        pe.wait_ge(k_d.sem, k_d.at(h))
                        pe.wait_ge(s_new.sem, s_new.at(h, 0))
                        for m, (t0, rows) in enumerate(KEY):
                            bank, c0 = (bank_r[3], 256 * m) if m < 2 else (bank_r[4], 0)
                            for d in range(DKB):
                                x = turn(bank[0:rows, c0 + P * d:c0 + P * d + P], k_dec[:, d, t0:t0 + rows])
                            x.then_inc(kt_done.sem, 1)
                        pe.wait_ge(sk_l.sem, sk_l.at(h, DKB))
                        for half in range(2):
                            for d in range(DKB):
                                x = turn(bank_r[0][:, 256 * half + P * d:256 * half + P * d + P],
                                         st_k[:, d, half].rearrange("p c n -> p (c n)"))
                        x.then_inc(ks_done.sem, 1)
                    if i in (11, 13):
                        pe.wait_ge(q_l.sem, q_l.at(h))
                        pe.wait_ge(k_l.sem, k_l.at(h))
                        if i == 13:
                            pe.wait_ge(ks_made.sem, ks_made.at(h))
                        for m in ((0, 1), (2,))[(i - 11) // 2]:
                            (t0, rows), (c0, n), bank = KEY[m], SC[m], bank_r[(1, 2, 0)[m]]
                            for d in range(DKB):
                                x = three(bank[0:rows, 0:n], kt_hi[:, d, t0:t0 + rows], kt_lo[:, d, t0:t0 + rows],
                                          q_hi[:, d, c0:c0 + n], q_lo[:, d, c0:c0 + n], d == 0, d == DKB - 1)
                            x.then_inc(sc_done.sem, 1)
                    if i == 16:
                        pe.wait_ge(p_act.sem, p_act.at(h, 4))
                        pe.wait_ge(a_f.sem, a_f.at(h, 3))
                        for m, (t0, rows) in enumerate(KEY):
                            for d in range(DVB):
                                x = turn(bank_r[m][0:rows, P * d:P * d + P], v_t[:, d, t0:t0 + rows])
                            x.then_inc(vt_done.sem, 1)
                    if i == 17:
                        pe.wait_ge(sv_l.sem, sv_l.at(h, DVB))
                        pe.wait_ge(kn_l.sem, kn_l.at(h, 3))
                        for half in range(2):
                            for d in range(DVB):
                                x = turn(bank_r[3 + half][:, P * d:P * d + P],
                                         st_v[:, d, half].rearrange("p c n -> p (c n)"))
                            x.then_inc(vs_done.sem, 1)
                    if i == 18:
                        pe.wait_ge(vn_l.sem, vn_l.at(h, 3))
                        pe.wait_ge(a_l.sem, a_l.at(h, 3))
                        for t in range(2):
                            rows = QRY[t][1]
                            for m in range(t + 1):
                                at = A_AT[m] + QRY[t][0] - SC[m][0]
                                x = three(bank_r[t][0:rows, :], a_hi[:, at:at + rows], a_lo[:, at:at + rows],
                                          v_hi[:, m, :], v_lo[:, m, :], m == 0, m == t)
                            x.then_inc(y_done.sem, 1)
                    if i in (22, 23):
                        d = i - 22
                        if d:
                            pe.wait_ge(st_read.sem, st_read.at(h, 1))
                        for m in range(3):
                            rows = KEY[m][1]
                            c = slice(P * d, P * d + P)
                            x = three(bank_q[:, :], k_hi[0:rows, m, c], k_lo[0:rows, m, c],
                                      v_hi[0:rows, m, :], v_lo[0:rows, m, :], m == 0, m == 2)
                        x.then_inc(st_done.sem, 1)
                    for t in QS_AT.get(i, ()):
                        b, d = t // 2, t % 2
                        pe.wait_ge(s_l.sem, s_l.at(h, t + 1))
                        if t == 0:
                            pe.wait_ge(qz_l.sem, qz_l.at(h))
                            pe.wait_ge(st_read.sem, st_read.at(h, 0))
                        qb = qz[:, d, P * b:P * b + P]
                        mm(bank_q[:, :], qb, s_hi[:, t % 2, :], start=(t == 0), stop=False)
                        x = mm(bank_q[:, :], qb, s_lo[:, t % 2, :], start=False, stop=(t == 15))
                        x.then_inc(s_q.sem, 1)
                    if i == 19:
                        rows = QRY[2][1]
                        o = bank_r[2][0:rows, :]
                        pe.wait_ge(yf_l.sem, yf_l.at(h))
                        mm(o, fold[:, :], y_f[:, 0, :], start=True, stop=False)
                        mm(o, fold[:, :], y_f[:, 1, :], start=False, stop=False)
                        for m in range(3):
                            at = A_AT[m] + QRY[2][0] - SC[m][0]
                            kr = KEY[m][1]
                            x = three(o, a_hi[0:kr, at:at + rows], a_lo[0:kr, at:at + rows],
                                      v_hi[0:kr, m, :], v_lo[0:kr, m, :], False, m == 2)
                        x.then_inc(y_done.sem, 1)
                    for back, t in due(KV_AT, i, first):
                        kv_multiply(h, t, back)
                    if i in (22, 23):
                        pe.wait_ge(y_nm.sem, y_nm.at(h, 3))
                        for j in range(3) if i == 22 else (3,):
                            if j == 3:
                                pe.wait_ge(z_f.sem, z_f.at(h, 1))
                            for t, (c0, rows) in enumerate(QRY):
                                x = turn(bank_r[j % 3][:, c0:c0 + rows], y_n[0:rows, t, P * j:P * j + P])
                            x.then_inc(yt_done.sem, 1)

                def out(i):
                    c = i - 24
                    wh = w_hi[:, i % SPL, :].rearrange("p (k n) -> p k n", k=DVB)
                    wl = w_lo[:, i % SPL, :].rearrange("p (k n) -> p k n", k=DVB)
                    pe.wait_ge(w_h.sem, w_h.at(h, i + 1))
                    for e in range(2):
                        g = 12 + 2 * c + e
                        if g < 14:
                            pe.wait_ge(p_act.sem, p_act.at(h, g - 5))
                        else:
                            pe.wait_ge(p_dve.sem, p_dve.at(h, g - 9))
                        for k in range(DVB):
                            if c == 0 and e == 0:
                                pe.wait_ge(z_l.sem, z_l.at(h, k + 1))
                            x = mm(bank_p[e][:, 0:N], wh[:, k, P * e:P * e + P], z_hi[:, k, :], start=(k == 0), stop=False)
                            x = mm(bank_p[e][:, 0:N], wh[:, k, P * e:P * e + P], z_lo[:, k, :], start=False, stop=False)
                    x.then_inc(w_hu.sem, 1)
                    pe.wait_ge(w_l.sem, w_l.at(h, i + 1))
                    for e in range(2):
                        for k in range(DVB):
                            x = mm(bank_p[e][:, 0:N], wl[:, k, P * e:P * e + P], z_hi[:, k, :], start=False, stop=(k == DVB - 1))
                        x.then_inc((o_even if e == 0 else w_lu).sem, 1)

                for i in range(24):
                    g, kept = i // 2, i < 4 or i >= 16
                    if i % 2 == 0:
                        if g < 2:
                            pe.wait_ge(p_dve.sem, p_dve.at(h, g - 1))
                        elif g < 6:
                            pe.wait_ge(p_dve.sem, p_dve.at(h, g - 1))
                        else:
                            pe.wait_ge(p_act.sem, p_act.at(h, g - 5))
                    if i < 2:
                        pe.wait_ge(x_l.sem, 2 * (i + 1))
                    c0, k0 = (CUT if kept else 0), 8 * (i % 2)
                    proj(0, h, CPH, i, bank_p[g % 2], T - c0, lambda k: xh[:, k0 + k, c0:T],
                         lambda k: xl[:, k0 + k, c0:T], i % 2 == 0, i % 2 == 1)
                    side(i)
                for i in range(24, CPH):
                    out(i)
                    side(i)

            head(0, True)
            with pe.Fori(1, HEADS) as h:
                head(h, False)

            def norm(n, c0):
                for k in range(KT):
                    x = mm(bank_r[0][:, c0:N], ones, acc[:, k, CUT + c0:T], start=(k == 0), stop=(k == KT - 1))
                x.then_inc(ln_sum[n].sem, 1)
                for k in range(KT):
                    pe.wait_ge(ln_s2[n].sem, k + 1)
                    mm(bank_r[1][:, c0:N], ones, ln_sq[:, k % 2, c0:N], start=(k == 0), stop=(k == KT - 1)).then_inc(ln_var[n].sem, 1)

            pe.wait_ge(p_dve.sem, p_dve.at(HEADS - 1, 20))
            norm(0, 0)

            def conv(j, at, first):
                for i in range(CPE):
                    g, k0 = i // 2, 8 * (i % 2)
                    c0 = CUT if g < 2 else META
                    if i % 2 == 0 and not (first and g < 2):
                        if g == 0:
                            pe.wait_ge(c_z.sem, c_z.at(j, 0))
                        if g == 1:
                            pe.wait_ge(c_b.sem, c_b.at(j, 0))
                        if g == 2:
                            pe.wait_ge(c_c.sem, c_c.at(j))
                        if g == 3:
                            pe.wait_ge(c_v.sem, c_v.at(j, 2))

                    def ready(k):
                        pe.wait_ge(ln_l[0].sem, k0 + k + 1)

                    proj(HEAD_CH, at, CPE, i, bank_p[g % 2], T - c0, lambda k: xh[:, k0 + k, c0:T],
                         lambda k: xl[:, k0 + k, c0:T], i % 2 == 0, i % 2 == 1, ready if first and i < 2 else None)
                    if first:
                        for back, t in due(KV_AT, i, last=True):
                            kv_multiply(HEADS, t, back)

            conv(0, 0, True)
            with pe.Fori(1, NE) as j:
                conv(j, j, False)

            def out_conv(j, first):
                for i in range(4):
                    g, k0 = i // 2, 8 * (i % 2)
                    if i % 2 == 0 and not first:
                        pe.wait_ge(o_read.sem, o_read.at(j, g - 1))

                    def ready(k):
                        pe.wait_ge(c_ml.sem, k0 + k + 1)

                    proj(HEAD_CH + CONV_CH, j, 4, i, bank_p[g % 2], NOUT, lambda k: m_hi[:, k0 + k, :],
                         lambda k: m_lo[:, k0 + k, :], i % 2 == 0, i % 2 == 1, ready if first and i < 2 else None)

            pe.wait_ge(c_z.sem, c_z.at(NE - 1))
            pe.wait_ge(c_b.sem, c_b.at(NE - 1))
            out_conv(0, True)
            with pe.Fori(1, OUT_CH // 4) as j:
                out_conv(j, False)
            pe.wait_ge(o_read.sem, o_read.at(OUT_CH // 4 - 1, 2))
            norm(1, 2)


def head_tables():
    pos = np.concatenate([np.arange(PROMPT), np.tile(PAST + np.arange(DSEQ), NB)]).astype(np.float32)
    e = -np.arange(P, dtype=np.float32) * np.float32(2) / np.float32(DK)
    ang = (pos[None, :] * (10000.0 ** e.astype(np.float64)).astype(np.float32)[:, None]).astype(np.float64)
    trig = np.stack([np.cos(ang), np.sin(ang)], 1).astype(np.float32)
    lg = np.log1p(-np.exp2(-5.0 - np.arange(HEADS)))
    tok = np.arange(T)
    samp = np.where(tok < PROMPT, -1, (tok - PROMPT) // DSEQ)
    inner = np.where(tok < PROMPT, tok, (tok - PROMPT) % DSEQ)
    tables = np.zeros((HEADS, P, TAB + HEADS), np.float32)
    for h in range(HEADS):
        for m, (t0, rows) in enumerate(KEY):
            c0, n = SC[m]
            keys, qs = tok[t0:t0 + rows], tok[CUT + c0:CUT + c0 + n]
            diff = inner[qs][None, :] - inner[keys][:, None]
            ok = (samp[qs][None, :] == samp[keys][:, None]) & (diff >= 0)
            tables[h, 0:rows, M_AT[m]:M_AT[m] + n] = np.where(ok, np.exp(np.maximum(diff, 0) * lg[h]), 0) * DK ** -0.5
        tables[h, :, QD_AT:QD_AT + NSAMP] = np.exp((inner[PROMPT:] + 1) * lg[h]) * DK ** -0.5
        last = np.where(samp < 0, PROMPT - 1, DSEQ - 1)
        tables[h, :, KD_AT:KD_AT + T] = np.exp((last - inner) * lg[h])
        tables[:, :, TAB + h] = np.exp(DSEQ * lg[h])
    con = np.zeros((P, 3 * P + 8), np.float32)
    con[:, 0:P] = np.eye(P)
    con[:, P:2 * P] = 1.0 / D
    for j in range(NSAMP):
        con[[j, NSAMP + j], 2 * P + META + j] = 1.0
    con[0:META, 3 * P] = 1.0
    for b in range(4):
        con[:, 3 * P + 1 + b] = (np.arange(P) % 32) // DSEQ == b
    return tables, trig, con


def kernel(x_prompt, x_sample, state_ret, state_conv, meta, w_ret_in, w_ret_out,
           w_conv_in, conv_w, w_conv_out, ln_g, ln_b):
    import concourse.bacc as bacc
    from concourse.bass_utils import run_bass_kernel_spmd

    A = np.asarray
    tables, trig, con = head_tables()
    x = np.concatenate([A(meta), A(x_prompt)[0], A(x_sample).reshape(NSAMP, D)], 0)

    def blocks(wm, rows):
        k, c = wm.shape
        t = wm.reshape(k // (rows * P), rows, P, c // P, P)
        return t.transpose(3, 0, 2, 1, 4).reshape(c // P, k // (rows * P), P, rows * P)

    w_in = A(w_ret_in)[0]
    qk = HEADS * DK
    b = blocks(w_in, 8)
    nq, nv = qk // P, HEADS * DVB
    parts = []
    for at, n in ((0, DKB), (nq, DKB), (2 * nq, DVB), (2 * nq + nv, DVB)):
        parts.append(b[at:at + HEADS * n].reshape(HEADS, n * 2, P, HALF))
    wo = A(w_ret_out)[0].reshape(HEADS, DVB, P, KT // 2, 2 * P).transpose(0, 3, 2, 1, 4)
    parts.append(wo.reshape(HEADS, 8, P, HALF))
    w_head = np.concatenate(parts, 1)
    bc = blocks(A(w_conv_in)[0], 8).reshape(4, NE, 2, P, HALF)
    w_conv = np.stack([bc[1], bc[2], bc[3], bc[0]], 1).reshape(NE, CPE, P, HALF)
    w_cout = blocks(A(w_conv_out)[0], 8).reshape(OUT_CH // 4, 4, P, HALF)
    ins = {
        "x_t": x.reshape(T, KT, P).transpose(2, 1, 0),
        "w_head": w_head, "w_conv": w_conv, "w_cout": w_cout,
        "s_in": A(state_ret)[0].reshape(NB, HEADS, DKB, P, DV).transpose(0, 1, 3, 2, 4),
        "tables": tables, "trig": trig, "consts": con,
        "lnp": np.stack([A(ln_g), A(ln_b)]).reshape(2, 2, KT, P).transpose(3, 0, 1, 2),
        "cw": A(conv_w)[0].reshape(WIDTH, NE, P).transpose(2, 1, 0),
        "cs_in": A(state_conv)[0].reshape(NB, 2, NE, P).transpose(3, 2, 0, 1),
    }
    outs = {
        "y_t": [P, KT, NOUT], "s_prompt": [HEADS, P, DKB, DV], "s_out": [NB, HEADS, P, DKB, DV],
        "cs_out": [P, NE, 1 + NB, 2],
    }
    nc = bacc.Bacc("TRN2", target_bir_lowering=False, num_devices=1)
    ins = {k: np.ascontiguousarray(v) for k, v in ins.items()}
    aps = {k: nc.dram_tensor(k, v.shape, F32, kind="ExternalInput").ap() for k, v in ins.items()}
    aps |= {k: nc.dram_tensor(k, s, F32, kind="ExternalOutput").ap() for k, s in outs.items()}
    hybrid_step(nc, **aps)
    r = run_bass_kernel_spmd(nc, [ins], core_ids=[0]).results[0]
    y = r["y_t"].transpose(2, 1, 0).reshape(NOUT, D)
    sp = r["s_prompt"].transpose(0, 2, 1, 3).reshape(1, 1, HEADS, DK, DV)
    ss = r["s_out"].transpose(0, 1, 3, 2, 4).reshape(1, NB, HEADS, DK, DV)
    cs = r["cs_out"].transpose(2, 3, 1, 0).reshape(1 + NB, 2, D)
    return (y[:SEQ].reshape(1, SEQ, D), y[SEQ:].reshape(NB, DSEQ, D), sp, ss, cs[None, 0:1], cs[None, 1:])
```

```python
from contextlib import ExitStack

import numpy as np

import concourse.bass as bass
from concourse import mybir

F32 = mybir.dt.float32
F32R = mybir.dt.float32r
ALU = mybir.AluOpType
ACT = mybir.ActivationFunctionType

P = 128
D = 2048
KT = D // P
SEQ, META, NB, DSEQ, PAST = 256, 16, 8, 8, 2048
NSAMP = NB * DSEQ
PROMPT = META + SEQ
T = PROMPT + NSAMP
WIDTH = 3
CUT = META - (WIDTH - 1)
N = T - CUT
NOUT = N - (WIDTH - 1)
NP_ = PROMPT - CUT
HEADS, DK, DV = 8, 256, 512
DKB, DVB = DK // P, DV // P
ALPHA = float(np.float32(4.0 ** 0.25))
LN_EPS, GN_EPS = 1e-5, 1e-6

KEY = [(0, 128), (128, 128), (256, 80)]
QRY = [(0, 128 - CUT), (128 - CUT, 128), (256 - CUT, 80)]
SC = [(0, NP_), (128 - CUT, NP_ - (128 - CUT)), (256 - CUT, 80)]
A_AT = [0, NP_ + NSAMP, NP_ + NSAMP + SC[1][1] + NSAMP]
A_LEN = A_AT[2] + 80
M_AT = [0, SC[0][1], SC[0][1] + SC[1][1]]
QD_AT = M_AT[2] + SC[2][1]
KD_AT = QD_AT + NSAMP
TAB = KD_AT + T

HALF = 1024
CPH = 32
RAW = 4
SPL = 2
NE = KT
CPE = 8
HEAD_CH = HEADS * CPH
CONV_CH = NE * CPE
OUT_CH = KT * 2
ROWS_U = 10

FIRST = 4
SUMS = KT - 2
SQS = (6, KT - 2)
TURN = 3
LESS = (KT, 13)

QS_AT = {5: (0,), 6: (1,), 7: (2,), 10: (3, 4), 11: (5,), 12: (6, 7), 13: (8,), 14: (9, 10), 15: (11,),
         16: (12, 13), 17: (14,), 18: (15,)}
KV_AT = {19: 0, 20: 1, 21: 2, 22: 3, 24: 4, 25: 5, 26: 6, 27: 7, 29: 8, 30: 9, 32: 10, 33: 11, 34: 12, 36: 13, 37: 14,
         39: 15}
KB_AT = {18: 0, 20: 1, 22: 2, 24: 3, 27: 4, 30: 5, 33: 6, 36: 7}
EARLY = (4, 9)
XC = 8
KV_NEXT = min(t for i, t in KV_AT.items() if i >= CPH) // 2
SA_AT = {5: 0, 7: 1, 12: 2, 14: 3, 16: 4, 17: 5, 18: 6, 20: 7}


def due(table, i, first=False, last=False):
    own = [(0, table[i])] if i in table and not last else []
    return own + ([(1, table[i + CPH])] if i + CPH in table and not first else [])


class Count:

    def __init__(self, sem, per=1, credit=0):
        self.sem, self.per, self.credit = sem, per, credit

    def at(self, r, j=1, back=0):
        return r * self.per + (j + self.credit - back * self.per)


def hybrid_step(nc, x_t, w_head, w_conv, w_cout, s_in, tables, trig, consts, lnp, cw, cs_in,
                y_t, s_prompt, s_out, cs_out):
    ctx = ExitStack()
    with ctx:
        def sb(name, shape, dt=F32):
            return ctx.enter_context(nc.sbuf_tensor(name, [P] + shape, dt))

        def count(name, per=1, credit=0):
            return Count(ctx.enter_context(nc.semaphore(name)), per, credit)

        xh, xl = sb("x_hi", [KT, T], F32R), sb("x_lo", [KT, T], F32R)
        acc = sb("residual", [KT, T])
        w_raw = sb("w_raw", [RAW, HALF])
        w_hi, w_lo = sb("w_hi", [SPL, HALF], F32R), sb("w_lo", [SPL, HALF], F32R)
        con = sb("constants", [3 * P + 8])
        gate_touch = sb("table_touch", [1])
        lnt = sb("ln_params", [2, 2, KT])
        bank_p = [ctx.enter_context(nc.psum_tensor(f"proj{i}", [P, 512], F32)) for i in range(2)]
        bank_q = ctx.enter_context(nc.psum_tensor("qs", [P, 512], F32))
        bank_r = [ctx.enter_context(nc.psum_tensor(f"side{i}", [P, 512], F32)) for i in range(5)]
        ident, ones = con[:, 0:P], con[:, P:2 * P]
        fold_raw = con[:, 2 * P:2 * P + 80]
        row_mask = con[:, 3 * P:3 * P + 1]
        bmask = con[:, 3 * P + 1:3 * P + 5]

        k_st, v_st = sb("k_stack", [2, DK], F32R), sb("v_stack", [2, DV], F32R)
        k_b = sb("k_of_sample", [2, DK], F32R)
        sb_ = sb("state_update", [4, DKB, DV])
        sd_h = sb("state_decay_of_head", [1])

        ret = ExitStack()

        def rb(name, shape, dt=F32):
            return ret.enter_context(nc.sbuf_tensor(name, [P] + shape, dt))

        tr = rb("cos_sin", [2, T])
        tab = rb("head_table", [TAB])
        a_hi, a_lo = rb("a_hi", [A_LEN], F32R), rb("a_lo", [A_LEN], F32R)
        tmp = rb("tmp", [2, T])
        sdec = rb("state_decay", [HEADS])
        fold = rb("fold", [80], F32R)
        qkz = rb("qk_or_z", [2 * DVB * T], F32R)
        raws = rb("qk_raw_or_gate", [2 * DKB * T])
        vt_yn = rb("v_t_or_y_norm", [3 * DV])
        v_hi, v_lo = rb("v_hi", [3, DV], F32R), rb("v_lo", [3, DV], F32R)
        k_hi, k_lo = rb("k_hi", [3, DK], F32R), rb("k_lo", [3, DK], F32R)
        qz = rb("q_spread", [DKB, NB * 136], F32R)
        stage = rb("stack_t_or_fold", [(DKB + DVB) * 2 * P], F32R)
        sa = rb("state_for_q_or_prompt_state", [2, DKB, DV])
        s_hi, s_lo = rb("s_hi", [2, DV], F32R), rb("s_lo", [2, DV], F32R)
        stat, mv, rstd = rb("gn_stats", [3, 6]), rb("gn_mean_var", [3, 2]), rb("gn_rstd", [3])
        gvar, mhalf = rb("gn_var_eps", [3]), rb("minus_half", [3])

        q_hi = qkz[:, 0:DKB * N].rearrange("p (d n) -> p d n", d=DKB)
        q_lo = qkz[:, DKB * N:2 * DKB * N].rearrange("p (d n) -> p d n", d=DKB)
        kk = qkz[:, 2 * DKB * N:2 * DKB * N + 2 * DKB * T].rearrange("p (s d n) -> p s d n", s=2, d=DKB)
        kt_hi, kt_lo = kk[:, 0], kk[:, 1]
        z_hi = qkz[:, 0:DVB * N].rearrange("p (d n) -> p d n", d=DVB)
        z_lo = qkz[:, DVB * N:2 * DVB * N].rearrange("p (d n) -> p d n", d=DVB)
        q_raw = raws[:, 0:DKB * N].rearrange("p (d n) -> p d n", d=DKB)
        k_raw = raws[:, 0:DKB * T].rearrange("p (d n) -> p d n", d=DKB)
        k_dec = raws[:, DKB * T:2 * DKB * T].rearrange("p (d n) -> p d n", d=DKB)
        gate = raws[:, 0:DVB * N].rearrange("p (d n) -> p d n", d=DVB)
        v_t = vt_yn[:, 0:DVB * T].rearrange("p (d n) -> p d n", d=DVB)
        y_n = vt_yn[:, :].rearrange("p (t n) -> p t n", t=3)
        st_k = stage[:, 0:DKB * 2 * P].rearrange("p (d f c n) -> p d f c n", d=DKB, f=2, c=4)
        st_v = stage[:, DKB * 2 * P:].rearrange("p (d f c n) -> p d f c n", d=DVB, f=2, c=4)
        pst = sa[:, 0]
        y_f = stage[:, 0:2 * DV].rearrange("p (s n) -> p s n", s=2)
        qz_rows = qz[:, :, :].rearrange("p k (b c) -> p k b c", c=136)

        ret.close()
        ln_s4, ln_su, ln_qs, ln_c = (sb(n, [N]) for n in ("ln_first_sum_or_mean", "ln_sum", "ln_square_sum", "ln_first_mean"))
        ln_m = ln_s4
        ln_v, ln_x = sb("ln_var", [3, N]), sb("ln_centred", [TURN, N])
        m_hi, m_lo = sb("m_hi", [NE, NOUT], F32R), sb("m_lo", [NE, NOUT], F32R)
        cwt, csi = sb("conv_w", [NE, WIDTH]), sb("conv_state_in", [NE, NB, 2])
        cso = sb("conv_state_out", [NE, 1 + NB, 2])
        w_j = sb("conv_w_block", [WIDTH])
        c_sb, z_sb, b_z, cv, m_f = (sb(n, [w]) for n, w in (
            ("c_gate", N), ("silu_z", NOUT), ("gate_product", NOUT), ("conv", NOUT), ("m", NOUT)))
        u = sb("u", [NP_ + NB * ROWS_U])
        u_s = u[:, NP_:].rearrange("p (b r) -> p b r", r=ROWS_U)
        cv_s = cv[:, SEQ:].rearrange("p (b r) -> p b r", r=DSEQ)

        con_in, trig_in, ln_in, cw_in = count("con_in"), count("trig_in"), count("ln_in"), count("cw_in")
        x_in = [count(f"x_in{i}") for i in range(XC)]
        x_h, x_l, x_acc = count("x_hi_made"), count("x_lo_made"), count("residual_made")
        half_set, fold_set, touch_set, zero_set = count("minus_half_set"), count("fold_set"), count("touch_set"), count("zeros_set")
        w_in = [count(f"w_in{s}", 16 * CPH // RAW) for s in range(RAW)]
        w_h = count("w_hi_made", CPH)
        w_l = count("w_lo_made", CPH, RAW)
        w_hu, w_lu = count("w_hi_used", CPH, SPL), count("w_lo_used", CPH, SPL)
        o_even = count("out_even_done", 8)
        p_act = count("proj_read_act", 8)
        p_dve = count("proj_read_dve", 20, 2)
        tab_in = count("tab_in")
        q_t, q_rot, q_h, q_l = count("q_temp"), count("q_rotated", 2), count("q_hi_made"), count("q_lo_made")
        qs_t, qz_h, qz_l = count("q_decayed"), count("q_spread_hi"), count("q_spread_lo")
        k_t, k_rot, k_h, k_l = count("k_temp"), count("k_rotated", 2), count("k_hi_made"), count("k_lo_made")
        k_d = count("k_decayed", 1)
        sk_h, sk_l = count("stack_k_hi", DKB), count("stack_k_lo", DKB)
        sv_h, sv_l = count("stack_v_hi", DVB), count("stack_v_lo", DVB)
        sd_set = count("state_decay_set")
        sc_done, a_f, a_h, a_l = count("scores_done", 3), count("a_masked", 3), count("a_hi_made", 3), count("a_lo_made", 3)
        kt_done, kn_h, kn_l = count("k_turned", 3), count("k_rows_hi", 3), count("k_rows_lo", 3)
        ks_done, ks_made = count("k_stack_turned"), count("k_stack_made")
        vt_done, vn_h, vn_l = count("v_turned", 3), count("v_rows_hi", 3), count("v_rows_lo", 3)
        vs_done, vs_made = count("v_stack_turned", 2), count("v_stack_made", 2)
        sa_in = [count(f"state_q_in{i}", 64) for i in range(2)]
        s_h = count("s_hi_made", 16)
        s_l = count("s_lo_made", 16, 4)
        s_q = count("s_used", 16, 2)
        yf_h, yf_l = count("y_fold_hi"), count("y_fold_lo")
        y_done, y_st, y_ag = count("y_done", 3), count("y_stats", 3), count("y_aggregated", 3)
        y_ve, y_rs, y_nm = count("y_var_eps"), count("y_rstd"), count("y_normed", 3)
        yt_done, z_f, z_h, z_l = count("y_turned", 4), count("z_made", 4), count("z_hi_made", 4), count("z_lo_made", 4)
        st_done, st_read = count("prompt_state_done", 2), count("prompt_state_read", 2, 1)
        st_out, st_free = count("prompt_state_out", 32), count("prompt_state_free", 1, 1)
        kb_made = count("k_b_made", 8)
        kv_done = count("kv_done", 16)
        s_new = count("s_new_made", 16, 1)
        sb_in = [count(f"state_u_in{i}", 32) for i in range(4)]
        sb_out = [count(f"state_u_out{i}", 32) for i in range(4)]
        gate_set = count("gate_set")
        passed = count("passed")
        def norms(name, per=1, credit=0):
            return [count(f"ln{i}_{name}", per, credit) for i in range(2)]

        n_zero, n_su, n_first, n_c = norms("zeros"), norms("sum_made"), norms("first_mean_done"), norms("first_mean_read")
        n_x, n_sq = norms("centred", TURN), norms("squared", TURN)
        n_qs, n_qp = norms("square_added", TURN, TURN), norms("square_multiplied")
        n_mean, n_m, n_f, n_sd = norms("mean_done"), norms("mean_read"), norms("var_steps"), norms("std_made")
        n_t, n_t2, n_s, n_h, n_o, n_l = (norms(n) for n in ("less_mean", "less_mean_dve", "scaled", "hi", "y", "lo"))
        c_c, c_v, c_z, c_b = count("c_read"), count("v_read", 2), count("z_read"), count("b_read")
        c_w, c_st, c_x, c_m, c_mh, c_ml = (count("conv_w_ready"), count("conv_state_ready"), count("conv_sum", 6),
                                           count("m_made"), count("m_hi_made"), count("m_lo_made"))
        cs_made = count("conv_state_made", 2)
        o_read = count("out_read", 2)
        y_out = count("y_out")
        cs_st = count("conv_state_stored")

        def sums_read(n, k):
            return (p_dve.sem, p_dve.at(HEADS - 1, 5 + k)) if n == 0 else (o_read.sem, k + 1)

        def square_used(n, k):
            return (n_qs[n].sem, n_qs[n].at(0, k + 1)) if k < SQS[n] else (n_qp[n].sem, k + 1 - SQS[n])

        def blk(k, n=0):
            c = slice(META if n else CUT, T)
            return acc[:, k, c] if isinstance(k, int) else acc[:, bass.ds(k, 1), c].rearrange("p a n -> p (a n)")

        def cols(ap, n):
            return ap[:, 2 * n:N]

        def conv_done(j, i):
            return j * CPE + (HEAD_CH + SPL + i + 1)

        def out_done(j, i):
            return j * 4 + (HEAD_CH + CONV_CH + SPL + i + 1)

        block = ctx.enter_context(nc.Block())

        def w(src, slot):
            return src[:, slot, :].rearrange("p (k n) -> p k n", k=8)

        @block.sync
        def _(sp):
            def load_chunk(base, r, per, i, src):
                sp.wait_ge(w_l.sem, r * per + (base + i + 1))
                sp.dma_start(w_raw[:, i % RAW, :], src).then_inc(w_in[i % RAW].sem, 16)

            for c in range(XC):
                cs = slice(c * KT // XC, (c + 1) * KT // XC)
                sp.dma_start(acc[:, cs, :], x_t[:, cs, :]).then_inc(x_in[c].sem, 16)
                if c in (1, 3):
                    load_chunk(0, 0, CPH, c // 2, w_head[0, c // 2])
            sp.dma_start(tr[:, :, :], trig).then_inc(trig_in.sem, 16)
            sp.dma_start(con[:, :], consts).then_inc(con_in.sem, 16)
            sp.dma_start(sdec[:, :], tables[0, :, TAB:TAB + HEADS]).then_inc(trig_in.sem, 16)
            sp.dma_start(lnt[:, :, :, :], lnp).then_inc(ln_in.sem, 16)

            def head_loads(h, first):
                for i in range(first, CPH):
                    load_chunk(0, h, CPH, i, w_head[h, i])
                    if i in SA_AT:
                        b = SA_AT[i]
                        sp.wait_ge(s_l.sem, s_l.at(h, 2 * b - 2))
                        if b == 0:
                            sp.sem_inc(passed.sem, 1)
                            sp.wait_ge(st_free.sem, st_free.at(h, 0))
                        sp.dma_start(sa[:, b % 2, :, :], s_in[b, h]).then_inc(sa_in[b % 2].sem, 16)

            head_loads(0, 2)
            with sp.Fori(1, HEADS) as h:
                head_loads(h, 0)
            with sp.Fori(0, NE) as j:
                for i in range(CPE):
                    load_chunk(HEAD_CH, j, CPE, i, w_conv[j, i])
            with sp.Fori(0, OUT_CH // 4) as j:
                for i in range(4):
                    load_chunk(HEAD_CH + CONV_CH, j, 4, i, w_cout[j, i])
            groups = [(0, 4), (4, 8), (8, 12), (12, 14), (14, 16)]
            for a, b in groups:
                sp.wait_ge(n_o[1].sem, b)
                sp.dma_start(y_t[:, a:b, :], acc[:, a:b, META:T]).then_inc(y_out.sem, 16)
            sp.wait_ge(y_out.sem, 16 * len(groups))
            sp.wait_ge(cs_st.sem, 16)

        @block.gpsimd
        def _(pool):
            pool.sem_inc(st_free.sem, st_free.credit)
            pool.memset(mhalf[:, :], -0.5).then_inc(half_set.sem, 1)
            pool.memzero(a_hi[:, :].bitcast(F32))
            pool.memzero(a_lo[:, :].bitcast(F32))
            pool.memzero(qz[:, :, :].bitcast(F32))
            pool.memset(mv[:, :, :], 0.0).then_inc(zero_set.sem, 1)
            pool.wait_ge(x_in[XC - 1].sem, 16)
            pool.dma_start(tab[:, :], tables[0, :, 0:TAB]).then_inc(tab_in.sem, 16)
            for b in range(4):
                pool.dma_start(sb_[:, b, :, :], s_in[b, 0]).then_inc(sb_in[b].sem, 16)
            pool.wait_ge(half_set.sem, 1)

            def store(h, b, back=0):
                pool.wait_ge(s_new.sem, s_new.at(h, 2 * b + 2, back))
                pool.sem_inc(passed.sem, 1)
                pool.dma_start(s_out[b, h - back], sb_[:, b % 4, :, :]).then_inc(sb_out[b % 4].sem, 16)

            def reload(h, b, back=0):
                pool.wait_ge(sb_out[b % 4].sem, sb_out[b % 4].at(h, 16 * (b // 4 + 1), back))
                pool.sem_inc(passed.sem, 1)
                nxt = s_in[b + 4, h - back] if b < NB - 4 else s_in[b + 4 - NB, h + 1 - back]
                pool.dma_start(sb_[:, b % 4, :, :], nxt).then_inc(sb_in[b % 4].sem, 16)

            def norm_zero(n):
                sem, v = sums_read(n, 0)
                pool.wait_ge(sem, v)
                pool.memset(ln_s4[:, :], 0.0)
                pool.memset(ln_qs[:, :], 0.0).then_inc(n_zero[n].sem, 1)
                pool.wait_ge(n_zero[n].sem, 1)
                pool.sem_inc(n_qs[n].sem, n_qs[n].credit)

            def add_sum(n, k):
                sem, v = sums_read(n, k)
                pool.wait_ge(sem, v)
                if k:
                    pool.wait_ge(n_su[n].sem, k)
                src, dst = cols(ln_s4 if k <= FIRST else ln_su, n), cols(ln_s4 if k < FIRST else ln_su, n)
                pool.tensor_tensor(dst, src, blk(k, n), ALU.add).then_inc(n_su[n].sem, 1)

            def add_square(n, slot, made, before):
                pool.wait_ge(n_sq[n].sem, made)
                pool.wait_ge(n_qs[n].sem, before)
                s = cols(ln_qs, n)
                pool.tensor_tensor(s, s, cols(ln_x[:, slot], n), ALU.add).then_inc(n_qs[n].sem, 1)

            def less_mean(n):
                pool.wait_ge(n_m[n].sem, 1)
                for k in range(LESS[n]):
                    pool.tensor_tensor(blk(k, n), blk(k, n), cols(ln_m, n), ALU.subtract).then_inc(n_t[n].sem, 1)

            def head(h, first, last):
                if not first:
                    for b in range(KV_NEXT, NB):
                        store(h, b, 1)
                        reload(h, b - 1, 1)
                pool.wait_ge(y_ve.sem, y_ve.at(h))
                pool.tensor_tensor(rstd[:, :], gvar[:, :], mhalf[:, :], ALU.pow).then_inc(y_rs.sem, 1)
                if not last:
                    pool.wait_ge(a_f.sem, a_f.at(h, 3))
                    pool.sem_inc(passed.sem, 1)
                    pool.dma_start(tab[:, :], tables[h + 1, :, 0:TAB]).then_inc(tab_in.sem, 16)
                for b in range(KV_NEXT):
                    if b == 2:
                        pool.wait_ge(st_read.sem, st_read.at(h, 2))
                        pool.sem_inc(passed.sem, 1)
                        pool.dma_start(s_prompt[h], pst[:, :, :]).then_inc(st_out.sem, 16)
                    if b == 4:
                        pool.wait_ge(st_out.sem, h * 16 + 16)
                        pool.sem_inc(st_free.sem, 1)
                    if not last or b != 4:
                        store(h, b)
                    if last:
                        if b == 1:
                            norm_zero(0)
                        for k in {1: (0, 1), 2: (2, 3, 4, 5), 3: (6, 7, 8, 9, 10, 11), 4: (12, 13)}.get(b, ()):
                            add_sum(0, k)
                            if k in (9, 11):
                                for q in range(3 * (k // 2) - 12, 3 * (k // 2) - 9):
                                    add_square(0, q % TURN, q + 1, n_qs[0].at(0, q))
                    if last and b == 4:
                        store(h, b)
                    if b:
                        reload(h, b - 1)
                    elif not first:
                        reload(h, NB - 1, 1)

            head(0, True, False)
            with pool.Fori(1, HEADS - 1) as h:
                head(h, False, False)
            head(HEADS - 1, False, True)
            less_mean(0)
            pool.dma_start(cwt[:, :, :], cw).then_inc(cw_in.sem, 16)
            pool.dma_start(csi[:, :, :, :], cs_in).then_inc(cw_in.sem, 16)
            for b in range(KV_NEXT, NB):
                store(HEADS, b, 1)
            norm_zero(1)
            for k in range(6):
                add_sum(1, k)
            with pool.Fori(3, OUT_CH // 4 - 1) as j:
                for i in range(TURN):
                    add_square(1, i, n_sq[1].at(j, i - 5, 1), n_qs[1].at(j, i - 6, 1))
                for e in range(2):
                    pool.wait_ge(o_read.sem, o_read.at(j, e + 1))
                    pool.wait_ge(n_su[1].sem, 2 * j + e)
                    s = cols(ln_su, 1)
                    pool.tensor_tensor(s, s, blk(2 * j + e, 1), ALU.add).then_inc(n_su[1].sem, 1)
            for q in range(12, SQS[1]):
                add_square(1, q % TURN, q + 1, n_qs[1].at(0, q))
            less_mean(1)
            for b in range(4):
                pool.wait_ge(sb_out[b].sem, 32 * HEADS)
            pool.wait_ge(cs_made.sem, 2 * NE)
            pool.dma_start(cs_out, cso[:, :, :, :]).then_inc(cs_st.sem, 16)
            pool.wait_ge(cs_st.sem, 16)

        @block.scalar
        def _(act):
            def round_chunk(base, r, per, i):
                rounds = per // RAW
                first = base // RAW
                act.wait_ge(w_in[i % RAW].sem, r * (16 * rounds) + 16 * (first + i // RAW + 1))
                act.wait_ge(w_hu.sem, r * per + (base + i + 1))
                act.wait_ge(w_l.sem, r * per + (base + i + 1 - SPL + RAW))
                act.copy(w_hi[:, i % SPL, :], w_raw[:, i % RAW, :]).then_inc(w_h.sem, 1)

            act.sem_inc(st_read.sem, st_read.credit)
            act.wait_ge(touch_set.sem, 1)
            for c in range(XC):
                cs = slice(c * KT // XC, (c + 1) * KT // XC)
                act.wait_ge(x_in[c].sem, 16)
                act.copy(xh[:, cs, :], acc[:, cs, :]).then_inc(x_h.sem, 1)
                if c in (1, 5):
                    round_chunk(0, 0, CPH, c // 4)
            act.wait_ge(zero_set.sem, 1)

            def kb_make(h, b, back):
                if b >= 2:
                    act.wait_ge(kv_done.sem, kv_done.at(h, 2 * b - 2, back))
                act.wait_ge(ks_made.sem, ks_made.at(h, 1, back))
                act.activation(k_b[:, b % 2, :], k_st[:, b // 4, :], ACT.Copy,
                               scale=bmask[:, b % 4:b % 4 + 1]).then_inc(kb_made.sem, 1)

            def first_mean(n):
                act.wait_ge(n_first[n].sem, 1)
                act.activation(cols(ln_c, n), bank_q[:, 2 * n:N], ACT.Copy, scale=float(KT // FIRST)).then_inc(n_c[n].sem, 1)

            def square(n, slot, made):
                act.wait_ge(n_x[n].sem, made)
                x = cols(ln_x[:, slot], n)
                act.activation(x, x, ACT.Square).then_inc(n_sq[n].sem, 1)

            def head(h, first, last=False):
                act.activation(gate_touch[:, :], gate_touch[:, :], ACT.Silu).then_inc(gate_set.sem, 1)

                def s_round(t):
                    b = t // 2
                    if t % 2 == 0:
                        act.wait_ge(sa_in[b % 2].sem, h * 64 + 16 * (b // 2 + 1))
                    act.wait_ge(s_q.sem, s_q.at(h, t - 1))
                    act.copy(s_hi[:, t % 2, :], sa[:, b % 2, t % 2, :]).then_inc(s_h.sem, 1)

                def z_round(*js):
                    for j in js:
                        act.wait_ge(z_f.sem, z_f.at(h, j + 1))
                        act.copy(z_hi[:, j, :], tmp[:, j % 2, 0:N]).then_inc(z_h.sem, 1)

                def side(i):
                    if first and i == 2:
                        act.wait_ge(con_in.sem, 16)
                        act.copy(fold[:, :], fold_raw).then_inc(fold_set.sem, 1)
                    if i == 4:
                        act.wait_ge(q_rot.sem, q_rot.at(h, 2))
                        act.copy(q_hi, q_raw).then_inc(q_h.sem, 1)
                        act.wait_ge(qs_t.sem, qs_t.at(h))
                        act.copy(qz_rows[:, :, :, 0:8],
                                 tmp[:, 0, 0:DKB * NSAMP].rearrange("p (d b r) -> p d b r", d=DKB, b=NB)
                                 ).then_inc(qz_h.sem, 1)
                    if i == 8:
                        act.wait_ge(k_rot.sem, k_rot.at(h, 2))
                        act.copy(kt_hi, k_raw).then_inc(k_h.sem, 1)
                    if i == 9:
                        act.wait_ge(k_d.sem, k_d.at(h))
                        for d in range(DKB):
                            src = k_dec[:, d, PROMPT:].rearrange("p (f n) -> p f n", f=2)
                            act.copy(st_k[:, d, :, 0, :], src)
                            act.copy(st_k[:, d, :, 1, :], src).then_inc(sk_h.sem, 1)
                    if 10 <= i <= 16 and i % 2 == 0:
                        g = 4 + (i - 10) // 2
                        act.wait_ge(w_lu.sem, w_lu.at(h, 2 * g + 2))
                        act.copy(v_t[:, g - 4, :], bank_p[g % 2][:, 0:T]).then_inc(p_act.sem, 1)
                    if i == 12:
                        for m in range(3):
                            rows = KEY[m][1]
                            src = (bank_r[3][0:rows, 256 * m:256 * m + 256] if m < 2 else bank_r[4][0:rows, 0:256])
                            act.wait_ge(kt_done.sem, kt_done.at(h, m + 1))
                            if m < 2:
                                act.copy(k_hi[0:rows, m, :], src).then_inc(kn_h.sem, 1)
                            else:
                                act.activation(k_hi[0:rows, m, :], src, ACT.Copy,
                                               scale=row_mask[0:rows, :]).then_inc(kn_h.sem, 1)
                    if i == 12:
                        act.wait_ge(ks_done.sem, ks_done.at(h))
                        act.copy(k_st[:, :, :], bank_r[0][:, :].rearrange("p (f n) -> p f n", f=2)).then_inc(ks_made.sem, 1)
                    if i in (13, 14):
                        for m in ((0, 1), (2,))[i - 13]:
                            act.wait_ge(a_f.sem, a_f.at(h, m + 1))
                            n = SC[m][1]
                            at = tmp[:, m % 2, 0:n]
                            rows = KEY[m][1]
                            act.copy(a_hi[0:rows, A_AT[m]:A_AT[m] + n], at[0:rows]).then_inc(a_h.sem, 1)
                    if i == 16:
                        act.wait_ge(p_act.sem, p_act.at(h, 4))
                        for d in range(DVB):
                            src = v_t[:, d, PROMPT:].rearrange("p (f n) -> p f n", f=2)
                            act.copy(st_v[:, d, :, 0, :], src)
                            act.copy(st_v[:, d, :, 2, :], src).then_inc(sv_h.sem, 1)
                    if i == 17:
                        for m in range(3):
                            rows = KEY[m][1]
                            act.wait_ge(vt_done.sem, vt_done.at(h, m + 1))
                            act.copy(v_hi[0:rows, m, :], bank_r[m][0:rows, :]).then_inc(vn_h.sem, 1)
                    if i == 18:
                        for f in range(2):
                            act.wait_ge(vs_done.sem, vs_done.at(h, f + 1))
                            act.copy(v_st[:, f, :], bank_r[3 + f][:, :]).then_inc(vs_made.sem, 1)
                    if 18 <= i <= 24 and i % 2 == 0:
                        g = 8 + (i - 18) // 2
                        act.wait_ge(w_lu.sem, w_lu.at(h, 2 * g + 2))
                        act.activation(gate[:, g - 8, :], bank_p[g % 2][:, 0:N], ACT.Silu).then_inc(p_act.sem, 1)
                    if i == 19:
                        act.wait_ge(s_q.sem, s_q.at(h, 2 * NB))
                        act.copy(y_f[:, 0, :], bank_q[:, :]).then_inc(yf_h.sem, 1)
                    if i == 24:
                        z_round(3)
                    if i in (23, 24):
                        d = i - 23
                        act.wait_ge(st_done.sem, st_done.at(h, d + 1))
                        act.copy(pst[:, d, :], bank_q[:, :]).then_inc(st_read.sem, 1)
                    if i == 23:
                        z_round(0, 1, 2)
                    for back, b in due(KB_AT, i, first):
                        kb_make(h, b, back)

                for i in range(CPH):
                    if i > 1 and i - 1 not in EARLY or i == 1 and not first:
                        round_chunk(0, h, CPH, i)
                    if i in EARLY:
                        round_chunk(0, h, CPH, i + 1)
                    side(i)
                    for t in QS_AT.get(i, ()):
                        s_round(t)
                    if last and i == 29:
                        first_mean(0)
                    if last and i >= 30:
                        for k in range(TURN * (i - 30), TURN * (i - 29)):
                            square(0, k % TURN, k + 1)
                round_chunk(0, h, CPH, CPH)

            head(0, True)
            with act.Fori(1, HEADS - 1) as h:
                head(h, False)
            head(HEADS - 1, False, True)

            def norm(n, first):
                act.activation(gate_touch[:, :], gate_touch[:, :], ACT.Sqrt).then_inc(gate_set.sem, 1)
                for k in range(first, KT):
                    if n == 0 and k == 9:
                        round_chunk(HEAD_CH, 0, CPE, 1)
                    square(n, k % TURN, k + 1)
                act.wait_ge(n_mean[n].sem, 1)
                act.copy(cols(ln_m, n), bank_r[0][:, 2 * n:N]).then_inc(n_m[n].sem, 1)
                act.wait_ge(n_f[n].sem, 3)
                act.activation(cols(ln_v[:, 1], n), cols(ln_v[:, 0], n), ACT.Sqrt).then_inc(n_sd[n].sem, 1)

            def add_bias(n, k):
                act.activation(blk(k, n), blk(k, n), ACT.Identity, bias=lnt[:, 1, n, k:k + 1]).then_inc(n_o[n].sem, 1)

            norm(0, 6)
            act.wait_ge(ln_in.sem, 16)
            for k in range(KT):
                act.wait_ge(n_s[0].sem, k + 1)
                act.activation(xh[:, k, CUT:T], blk(k), ACT.Identity, bias=lnt[:, 1, 0, k:k + 1]).then_inc(n_h[0].sem, 1)
                if k in (10, 14):
                    round_chunk(HEAD_CH, 0, CPE, k // 4)

            def conv_hi(j):
                act.wait_ge(c_m.sem, c_m.at(j))
                act.copy(m_hi[:, bass.ds(j, 1), :].rearrange("p a n -> p (a n)"), m_f[:, :]).then_inc(c_mh.sem, 1)

            def conv(j, done):
                act.activation(gate_touch[:, :], gate_touch[:, :], ACT.Silu).then_inc(gate_set.sem, 1)
                for i in range(CPE):
                    if i > done:
                        round_chunk(HEAD_CH, j, CPE, i)
                    if done:
                        for back, b in due(KB_AT, i, last=True):
                            kb_make(HEADS, b, back)
                    if done and i >= 4:
                        for k in range(4 * i - 16, 4 * i - 12):
                            act.wait_ge(n_l[0].sem, k + 1)
                            add_bias(0, k)
                    if i == 3:
                        act.wait_ge(w_lu.sem, conv_done(j, 2))
                        act.copy(c_sb[:, :], bank_p[0][:, 0:N]).then_inc(c_c.sem, 1)
                    if i == 6:
                        act.wait_ge(w_lu.sem, conv_done(j, 5))
                        act.activation(z_sb[:, :], bank_p[0][:, 0:NOUT], ACT.Silu).then_inc(c_z.sem, 1)
                round_chunk(HEAD_CH, j, CPE, CPE)
                conv_hi(j)

            conv(0, 3)
            with act.Fori(1, NE) as j:
                conv(j, 0)

            def out_chunks(j):
                for i in range(1, 4 if isinstance(j, int) and j == OUT_CH // 4 - 1 else 5):
                    round_chunk(HEAD_CH + CONV_CH, j, 4, i)
                    if i == 2 and isinstance(j, int) and j == 2:
                        first_mean(1)
                    if i == 1 and not isinstance(j, int):
                        for q in range(TURN):
                            square(1, q, n_x[1].at(j, q - 5, 1))

            for j in range(3):
                out_chunks(j)
            with act.Fori(3, OUT_CH // 4 - 1) as j:
                out_chunks(j)
            out_chunks(OUT_CH // 4 - 1)
            norm(1, 12)
            for k in range(KT):
                act.wait_ge(n_s[1].sem, k + 1)
                add_bias(1, k)

        @block.vector
        def _(dve):
            f = lambda ap: ap.bitcast(F32)
            TT = dve.tensor_tensor

            def rest_chunk(base, r, per, i):
                dve.wait_ge(w_h.sem, r * per + (base + i + 1))
                dve.wait_ge(w_lu.sem, r * per + (base + i + 1))
                TT(w_lo[:, i % SPL, :], w_raw[:, i % RAW, :], f(w_hi[:, i % SPL, :]), ALU.subtract).then_inc(w_l.sem, 1)

            dve.sem_inc(w_l.sem, w_l.credit)
            dve.sem_inc(p_dve.sem, p_dve.credit)
            dve.sem_inc(s_l.sem, s_l.credit)
            dve.sem_inc(s_new.sem, s_new.credit)
            dve.memset(gate_touch[:, :], 0.0).then_inc(touch_set.sem, 1)
            for c in range(XC):
                cs = slice(c * KT // XC, (c + 1) * KT // XC)
                dve.wait_ge(x_h.sem, c + 1)
                TT(xl[:, cs, :], acc[:, cs, :], f(xh[:, cs, :]), ALU.subtract).then_inc(x_l.sem, 1)
                if c == 3:
                    rest_chunk(0, 0, CPH, 0)
            rest_chunk(0, 0, CPH, 1)
            for c in range(4):
                dve.wait_ge(x_l.sem, (c + 1) * XC // 4)
                cs = acc[:, 4 * c:4 * c + 4, CUT:T]
                dve.tensor_scalar(cs, cs, ALPHA, None, ALU.mult).then_inc(x_acc.sem, 1)
            dve.wait_ge(x_acc.sem, 4)
            dve.wait_ge(trig_in.sem, 32)
            dve.wait_ge(zero_set.sem, 1)
            add = ALU.add

            def kv_update(h, t, back):
                b, bank = t // 2, bank_r[3 + t % 2]
                if t % 2 == 0:
                    dve.wait_ge(sb_in[b % 4].sem, sb_in[b % 4].at(h, 16 * (b // 4 + 1), back))
                dve.wait_ge(kv_done.sem, kv_done.at(h, t + 1, back))
                dve.wait_ge(sd_set.sem, sd_set.at(h, 1, back))
                s = sb_[:, b % 4, t % 2, :]
                dve.scalar_tensor_tensor(s, s, sd_h[:, :], bank[:, :], ALU.mult, add).then_inc(s_new.sem, 1)

            def centre(n, k, slot, free):
                if free is not None:
                    dve.wait_ge(*free)
                dve.wait_ge(n_c[n].sem, 1)
                TT(cols(ln_x[:, slot], n), blk(k, n), cols(ln_c, n), ALU.subtract).then_inc(n_x[n].sem, 1)

            def centre_blocks(n, ks):
                for k in ks:
                    dve.wait_ge(*sums_read(n, k))
                    centre(n, k, k % TURN, square_used(n, k - TURN) if k >= TURN else None)

            def head(h, first, last=False):

                def q_or_k(i, bank, raw, t_sem, rot_sem, c0):
                    cos, sin = tr[:, 0, c0:T], tr[:, 1, c0:T]
                    n = T - c0
                    src = bank[:, 0:n]
                    if i == 0:
                        TT(raw[:, 0, :], src, cos, ALU.mult)
                        TT(raw[:, 1, :], src, sin, ALU.mult).then_inc(p_dve.sem, 1)
                    else:
                        TT(tmp[:, 0, 0:n], src, sin, ALU.mult).then_inc(t_sem.sem, 1)
                        TT(tmp[:, 1, 0:n], src, cos, ALU.mult).then_inc(p_dve.sem, 1)
                        dve.wait_ge(t_sem.sem, t_sem.at(h))
                        TT(raw[:, 0, :], raw[:, 0, :], tmp[:, 0, 0:n], ALU.subtract).then_inc(rot_sem.sem, 1)
                        dve.wait_ge(p_dve.sem, p_dve.at(h, 2 if raw is q_raw else 4))
                        TT(raw[:, 1, :], raw[:, 1, :], tmp[:, 1, 0:n], add).then_inc(rot_sem.sem, 1)

                def s_rest(t):
                    b = t // 2
                    dve.wait_ge(s_h.sem, s_h.at(h, t + 1))
                    dve.wait_ge(s_q.sem, s_q.at(h, t - 1))
                    TT(s_lo[:, t % 2, :], sa[:, b % 2, t % 2, :], f(s_hi[:, t % 2, :]), ALU.subtract).then_inc(s_l.sem, 1)

                def out_read(c):
                    for e in range(2):
                        if e == 0:
                            dve.wait_ge(o_even.sem, o_even.at(h, c + 1))
                        else:
                            dve.wait_ge(w_lu.sem, w_lu.at(h, 24 + c + 1))
                        a = acc[:, 2 * c + e, CUT:T]
                        TT(a, a, bank_p[e][:, 0:N], add).then_inc(p_dve.sem, 1)

                def side(i):
                    if i == 2:
                        dve.wait_ge(w_lu.sem, w_lu.at(h, 2))
                        q_or_k(0, bank_p[0], q_raw, q_t, q_rot, CUT)
                    if i == 4:
                        dve.wait_ge(w_lu.sem, w_lu.at(h, 4))
                        q_or_k(1, bank_p[1], q_raw, q_t, q_rot, CUT)
                        dve.wait_ge(tab_in.sem, h * 16 + 16)
                        dve.wait_ge(q_rot.sem, q_rot.at(h, 2))
                        dec = tab[:, QD_AT:QD_AT + NSAMP].unsqueeze(1).to_broadcast([P, DKB, NSAMP])
                        qs = tmp[:, 0, 0:DKB * NSAMP].rearrange("p (d n) -> p d n", d=DKB)
                        TT(qs, q_raw[:, :, NP_:N], dec, ALU.mult).then_inc(qs_t.sem, 1)
                        dve.wait_ge(q_h.sem, q_h.at(h))
                        TT(q_lo, q_raw, f(q_hi), ALU.subtract).then_inc(q_l.sem, 1)
                        dve.wait_ge(qz_h.sem, qz_h.at(h))
                        qs4 = qs.rearrange("p d (b r) -> p d b r", b=NB)
                        for d in range(DKB):
                            z = TT(qz_rows[:, d, :, 64:72], qs4[:, d], f(qz_rows[:, d, :, 0:8]), ALU.subtract)
                        z.then_inc(qz_l.sem, 1)
                    if i == 6:
                        dve.wait_ge(w_lu.sem, w_lu.at(h, 6))
                        q_or_k(0, bank_p[0], k_raw, k_t, k_rot, 0)
                    if i == 8:
                        dve.wait_ge(w_lu.sem, w_lu.at(h, 8))
                        q_or_k(1, bank_p[1], k_raw, k_t, k_rot, 0)
                        dve.wait_ge(k_h.sem, k_h.at(h))
                        TT(kt_lo, k_raw, f(kt_hi), ALU.subtract).then_inc(k_l.sem, 1)
                    if i == 9:
                        dve.wait_ge(k_rot.sem, k_rot.at(h, 2))
                        dec = tab[:, KD_AT:KD_AT + T].unsqueeze(1).to_broadcast([P, DKB, T])
                        TT(k_dec, k_raw, dec, ALU.mult).then_inc(k_d.sem, 1)
                        for d in range(DKB):
                            dve.wait_ge(sk_h.sem, sk_h.at(h, d + 1))
                            src = k_dec[:, d, PROMPT:].rearrange("p (f n) -> p f n", f=2)
                            hi = f(st_k[:, d, :, 0, :])
                            TT(st_k[:, d, :, 2, :], src, hi, ALU.subtract)
                            TT(st_k[:, d, :, 3, :], src, hi, ALU.subtract).then_inc(sk_l.sem, 1)
                    if i == 12:
                        for m in range(3):
                            rows = KEY[m][1]
                            src = (bank_r[3][0:rows, 256 * m:256 * m + 256] if m < 2 else bank_r[4][0:rows, 0:256])
                            dve.wait_ge(kn_h.sem, kn_h.at(h, max(m + 1, 2)))
                            o, hi = k_lo[0:rows, m, :], f(k_hi[0:rows, m, :])
                            if m < 2:
                                TT(o, src, hi, ALU.subtract).then_inc(kn_l.sem, 1)
                            else:
                                dve.scalar_tensor_tensor(o, src, row_mask[0:rows, :], hi, ALU.mult,
                                                         ALU.subtract).then_inc(kn_l.sem, 1)
                    if i in (13, 14):
                        ms = ((0, 1), (2,))[i - 13]
                        for m in ms:
                            rows, n, bank = KEY[m][1], SC[m][1], bank_r[(1, 2, 0)[m]]
                            dve.wait_ge(sc_done.sem, sc_done.at(h, m + 1))
                            if m >= 2:
                                dve.wait_ge(a_l.sem, a_l.at(h, m - 1))
                            TT(tmp[0:rows, m % 2, 0:n], bank[0:rows, 0:n], tab[0:rows, M_AT[m]:M_AT[m] + n],
                               ALU.mult).then_inc(a_f.sem, 1)
                        for m in ms:
                            rows, n = KEY[m][1], SC[m][1]
                            at = slice(A_AT[m], A_AT[m] + n)
                            dve.wait_ge(a_h.sem, a_h.at(h, m + 1))
                            TT(a_lo[0:rows, at], tmp[0:rows, m % 2, 0:n], f(a_hi[0:rows, at]), ALU.subtract).then_inc(a_l.sem, 1)
                    if i == 16:
                        for d in range(DVB):
                            dve.wait_ge(sv_h.sem, sv_h.at(h, d + 1))
                            src = v_t[:, d, PROMPT:].rearrange("p (f n) -> p f n", f=2)
                            hi = f(st_v[:, d, :, 0, :])
                            TT(st_v[:, d, :, 1, :], src, hi, ALU.subtract)
                            TT(st_v[:, d, :, 3, :], src, hi, ALU.subtract).then_inc(sv_l.sem, 1)
                    if i == 17:
                        for m in range(3):
                            rows = KEY[m][1]
                            dve.wait_ge(vn_h.sem, vn_h.at(h, m + 1))
                            TT(v_lo[0:rows, m, :], bank_r[m][0:rows, :], f(v_hi[0:rows, m, :]), ALU.subtract).then_inc(vn_l.sem, 1)
                    if i == 19:
                        dve.wait_ge(s_new.sem, s_new.at(h, 0))
                        dve.tensor_copy(sd_h[:, :], sdec[:, bass.ds(h, 1)]).then_inc(sd_set.sem, 1)
                        dve.wait_ge(yf_h.sem, yf_h.at(h))
                        TT(y_f[:, 1, :], bank_q[:, :], f(y_f[:, 0, :]), ALU.subtract).then_inc(yf_l.sem, 1)
                    if i in (19, 20):
                        for t in ((0, 1), (2,))[i - 19]:
                            rows = QRY[t][1]
                            dve.wait_ge(y_done.sem, y_done.at(h, t + 1))
                            dve.bn_stats(stat[0:rows, t, :], bank_r[t][0:rows, :]).then_inc(y_st.sem, 1)
                            dve.wait_ge(y_st.sem, y_st.at(h, t + 1))
                            dve.sem_inc(passed.sem, 1)
                            dve.bn_aggr(mv[0:rows, t, :], stat[0:rows, t, :]).then_inc(y_ag.sem, 1)
                    if i == 20:
                        dve.wait_ge(y_ag.sem, y_ag.at(h, 3))
                        dve.tensor_scalar(gvar[:, :], mv[:, :, 1], GN_EPS, None, add).then_inc(y_ve.sem, 1)
                    if i == 21:
                        dve.wait_ge(y_rs.sem, y_rs.at(h))
                        for t in range(3):
                            rows = QRY[t][1]
                            dve.tensor_scalar(y_n[0:rows, t, :], bank_r[t][0:rows, :], mv[0:rows, t, 0:1],
                                              rstd[0:rows, t:t + 1], ALU.subtract, ALU.mult).then_inc(y_nm.sem, 1)
                    if i in (23, 24):
                        for j in range(3) if i == 23 else (3,):
                            dve.wait_ge(yt_done.sem, yt_done.at(h, j + 1))
                            dve.wait_ge(p_act.sem, p_act.at(h, 5 + j))
                            if j >= 2:
                                dve.wait_ge(z_l.sem, z_l.at(h, j - 1))
                            TT(tmp[:, j % 2, 0:N], bank_r[j % 3][:, 0:N], gate[:, j, :], ALU.mult).then_inc(z_f.sem, 1)
                            dve.wait_ge(z_h.sem, z_h.at(h, j + 1))
                            TT(z_lo[:, j, :], tmp[:, j % 2, 0:N], f(z_hi[:, j, :]), ALU.subtract).then_inc(z_l.sem, 1)
                    if i >= 25:
                        out_read(i - 25)
                    for back, t in due(KV_AT, i - 1, first):
                        kv_update(h, t, back)

                for i in range(CPH):
                    if i == 24:
                        side(i)
                        rest_chunk(0, h, CPH, i)
                    else:
                        if i > 1 or i == 1 and not first:
                            rest_chunk(0, h, CPH, i)
                        side(i)
                    for t in QS_AT.get(i, ()):
                        s_rest(t)
                    if last and i >= 29:
                        centre_blocks(0, range(TURN * (i - 29), TURN * (i - 28)))
                if last:
                    centre_blocks(0, range(9, 14))
                else:
                    rest_chunk(0, h, CPH, CPH)
                out_read(7)

            head(0, True)
            with dve.Fori(1, HEADS - 1) as h:
                head(h, False)
            head(HEADS - 1, False, True)

            def norm(n):
                centre_blocks(n, (14, 15) if n == 0 else (15,))
                if n == 0:
                    for i in range(2):
                        rest_chunk(HEAD_CH, 0, CPE, i)
                v = [cols(ln_v[:, i], n) for i in range(3)]
                dve.wait_ge(n_m[n].sem, 1)
                TT(v[1], cols(ln_m, n), cols(ln_c, n), ALU.subtract).then_inc(n_f[n].sem, 1)
                dve.wait_ge(n_f[n].sem, 1)
                TT(v[0], v[1], v[1], ALU.mult).then_inc(n_f[n].sem, 1)
                dve.wait_ge(n_f[n].sem, 2)
                dve.wait_ge(n_qp[n].sem, KT - SQS[n])
                dve.scalar_tensor_tensor(v[0], bank_r[1][:, 2 * n:N], LN_EPS, v[0], add, ALU.subtract).then_inc(n_f[n].sem, 1)

                def less(ks):
                    for k in ks:
                        TT(blk(k, n), blk(k, n), cols(ln_m, n), ALU.subtract).then_inc(n_t2[n].sem, 1)

                less(range(LESS[n], min(LESS[n] + 2, KT)))
                dve.wait_ge(n_sd[n].sem, 1)
                dve.reciprocal(v[2], v[1]).then_inc(n_f[n].sem, 1)
                less(range(LESS[n] + 2, KT))
                dve.wait_ge(n_f[n].sem, 4)
                dve.wait_ge(ln_in.sem, 16)

                def rest(k):
                    dve.wait_ge(n_h[0].sem, k + 1)
                    dve.scalar_tensor_tensor(xl[:, k, CUT:T], blk(k), lnt[:, 1, 0, k:k + 1], f(xh[:, k, CUT:T]), add,
                                             ALU.subtract).then_inc(n_l[0].sem, 1)

                for k in range(KT):
                    if k < LESS[n]:
                        dve.wait_ge(n_t[n].sem, k + 1)
                    else:
                        dve.wait_ge(n_t2[n].sem, k - LESS[n] + 1)
                    dve.scalar_tensor_tensor(blk(k, n), blk(k, n), lnt[:, 0, n, k:k + 1], v[2], ALU.mult,
                                             ALU.mult).then_inc(n_s[n].sem, 1)
                    if n == 0 and k >= 1:
                        rest(k - 1)
                    if n == 0 and k in (11, 15):
                        rest_chunk(HEAD_CH, 0, CPE, k // 4)
                if n == 0:
                    rest(KT - 1)

            norm(0)
            dve.wait_ge(cw_in.sem, 32)

            def conv(j, done):
                for i in range(CPE):
                    if i > done:
                        rest_chunk(HEAD_CH, j, CPE, i)
                    if done:
                        for back, t in due(KV_AT, i - 1, last=True):
                            kv_update(HEADS, t, back)
                    if i == 0:
                        dve.tensor_copy(w_j[:, :], cwt[:, bass.ds(j, 1), :].rearrange("p a b -> p (a b)")).then_inc(c_w.sem, 1)
                        dve.tensor_copy(u_s[:, :, 0:2], csi[:, bass.ds(j, 1), :, :].rearrange("p a b c -> p (a b) c")).then_inc(c_st.sem, 1)
                    if i == 4:
                        dve.wait_ge(w_lu.sem, conv_done(j, 3))
                        dve.wait_ge(c_c.sem, c_c.at(j))
                        TT(u[:, 0:NP_], bank_p[1][:, 0:NP_], c_sb[:, 0:NP_], ALU.mult).then_inc(c_v.sem, 1)
                        bs = lambda ap: ap.rearrange("p (b r) -> p b r", r=DSEQ)
                        TT(u_s[:, :, 2:], bs(bank_p[1][:, NP_:N]), bs(c_sb[:, NP_:N]), ALU.mult).then_inc(c_v.sem, 1)
                        dve.wait_ge(c_v.sem, c_v.at(j, 2))
                        dve.wait_ge(c_w.sem, c_w.at(j))
                        dve.wait_ge(c_st.sem, c_st.at(j))
                        for n in range(WIDTH):
                            w0 = w_j[:, n:n + 1]
                            for s, (dst, src) in enumerate(((cv[:, 0:SEQ], u[:, n:n + SEQ]), (cv_s, u_s[:, :, n:n + DSEQ]))):
                                if n == 0:
                                    dve.tensor_scalar(dst, src, w0, None, ALU.mult).then_inc(c_x.sem, 1)
                                else:
                                    dve.wait_ge(c_x.sem, c_x.at(j, 2 * (n - 1) + s + 1))
                                    dve.scalar_tensor_tensor(dst, src, w0, dst, ALU.mult, add).then_inc(c_x.sem, 1)
                        dve.tensor_copy(cso[:, bass.ds(j, 1), 0, :].rearrange("p a c -> p (a c)"), u[:, NP_ - 2:NP_]).then_inc(cs_made.sem, 1)
                        dve.tensor_copy(cso[:, bass.ds(j, 1), 1:, :].rearrange("p a b c -> p (a b) c"), u_s[:, :, DSEQ:]).then_inc(cs_made.sem, 1)

            def conv_end(j):
                dve.wait_ge(w_lu.sem, conv_done(j, 7))
                dve.wait_ge(c_z.sem, c_z.at(j))
                TT(b_z[:, :], bank_p[1][:, 0:NOUT], z_sb[:, :], ALU.mult).then_inc(c_b.sem, 1)
                dve.wait_ge(c_b.sem, c_b.at(j))
                dve.wait_ge(c_x.sem, c_x.at(j, 6))
                TT(m_f[:, :], b_z[:, :], cv[:, :], ALU.mult).then_inc(c_m.sem, 1)

            def conv_rest(j):
                dve.wait_ge(c_mh.sem, c_mh.at(j))
                at = bass.ds(j, 1)
                sq = lambda ap: ap.rearrange("p a n -> p (a n)")
                TT(sq(m_lo[:, at, :]), m_f[:, :], f(sq(m_hi[:, at, :])), ALU.subtract).then_inc(c_ml.sem, 1)

            def conv_all(j, done):
                conv(j, done)
                rest_chunk(HEAD_CH, j, CPE, CPE)
                if done:
                    for back, t in due(KV_AT, CPE - 1, last=True):
                        kv_update(HEADS, t, back)
                conv_end(j)
                conv_rest(j)

            conv_all(0, 3)
            with dve.Fori(1, NE) as j:
                conv_all(j, 0)

            dve.wait_ge(n_o[0].sem, KT)

            def block_read(j, e):
                dve.wait_ge(w_lu.sem, out_done(j, 2 * e + 1))
                a = blk(2 * j + e, 1)
                dve.scalar_tensor_tensor(a, a, ALPHA, bank_p[e][:, 0:NOUT], ALU.mult, add).then_inc(o_read.sem, 1)

            def out_chunks(j):
                for i in range(1, 4 if isinstance(j, int) and j == OUT_CH // 4 - 1 else 5):
                    rest_chunk(HEAD_CH + CONV_CH, j, 4, i)
                    if i == 2:
                        block_read(j, 0)
                    if i == 3 and isinstance(j, int) and j == OUT_CH // 4 - 1:
                        centre_blocks(1, (14,))
                block_read(j, 1)

            for j in range(3):
                out_chunks(j)
            centre_blocks(1, range(3))
            with dve.Fori(3, OUT_CH // 4 - 2) as j:
                out_chunks(j)
                dve.wait_ge(o_read.sem, o_read.at(j, 2))
                for i in range(TURN):
                    centre(1, TURN * j + (i - 6), i, (n_qs[1].sem, n_qs[1].at(j, i - 8)))
            out_chunks(OUT_CH // 4 - 2)
            centre_blocks(1, (12, 13))
            out_chunks(OUT_CH // 4 - 1)
            norm(1)

        @block.tensor
        def _(pe):
            mm = pe.matmul

            def three(out, a_hi_, a_lo_, b_hi_, b_lo_, start, stop):
                mm(out, a_hi_, b_hi_, start=start, stop=False)
                mm(out, a_hi_, b_lo_, start=False, stop=False)
                return mm(out, a_lo_, b_hi_, start=False, stop=stop)

            def turn(out, src):
                n = src.shape[0]
                return pe.transpose(out, src if src.dtype == F32 else src.bitcast(F32), ident[0:n, 0:n])

            def proj(base, r, per, i, bank, n, rhs_h, rhs_l, first, last, by_block=None):
                wh, wl = w(w_hi, i % SPL), w(w_lo, i % SPL)
                pe.wait_ge(w_h.sem, r * per + (base + i + 1))
                for k in range(8):
                    if by_block:
                        by_block(k)
                    mm(bank[:, 0:n], wh[:, k, :], rhs_h(k), start=(first and k == 0), stop=False)
                    x = mm(bank[:, 0:n], wh[:, k, :], rhs_l(k), start=False, stop=False)
                x.then_inc(w_hu.sem, 1)
                pe.wait_ge(w_l.sem, r * per + (base + i + 1 + RAW))
                for k in range(8):
                    x = mm(bank[:, 0:n], wl[:, k, :], rhs_h(k), start=False, stop=(last and k == 7))
                x.then_inc(w_lu.sem, 1)

            pe.sem_inc(w_hu.sem, w_hu.credit)
            pe.sem_inc(w_lu.sem, w_lu.credit)
            pe.sem_inc(s_q.sem, s_q.credit)

            def kv_multiply(h, t, back):
                b = t // 2
                if t < 2:
                    pe.wait_ge(vs_made.sem, vs_made.at(h, t + 1))
                else:
                    pe.wait_ge(s_new.sem, s_new.at(h, t - 1, back))
                pe.wait_ge(kb_made.sem, kb_made.at(h, b + 1, back))
                mm(bank_r[3 + t % 2][:, :], k_b[:, b % 2, P * (t % 2):P * (t % 2) + P], v_st[:, b // 4, :],
                   start=True, stop=True).then_inc(kv_done.sem, 1)

            def first_mean(n):
                pe.wait_ge(n_su[n].sem, FIRST)
                mm(bank_q[:, 2 * n:N], ones, cols(ln_s4, n), start=True, stop=True).then_inc(n_first[n].sem, 1)

            def head(h, first, last=False):
                def y_turn(*js):
                    pe.wait_ge(y_nm.sem, y_nm.at(h, 3))
                    for j in js:
                        if j == 3:
                            pe.wait_ge(z_f.sem, z_f.at(h, 1))
                        for t, (c0, rows) in enumerate(QRY):
                            x = turn(bank_r[j % 3][:, c0:c0 + rows], y_n[0:rows, t, P * j:P * j + P])
                        x.then_inc(yt_done.sem, 1)

                def side(i):
                    if first and i == 5:
                        pe.wait_ge(zero_set.sem, 1)
                    if first and i == 10:
                        pe.wait_ge(con_in.sem, 16)
                        pe.wait_ge(fold_set.sem, 1)
                    if i == 10:
                        pe.wait_ge(k_d.sem, k_d.at(h))
                        pe.wait_ge(s_new.sem, s_new.at(h, 0))
                        for m, (t0, rows) in enumerate(KEY):
                            bank, c0 = (bank_r[3], 256 * m) if m < 2 else (bank_r[4], 0)
                            for d in range(DKB):
                                x = turn(bank[0:rows, c0 + P * d:c0 + P * d + P], k_dec[:, d, t0:t0 + rows])
                            x.then_inc(kt_done.sem, 1)
                        pe.wait_ge(sk_l.sem, sk_l.at(h, DKB))
                        for half in range(2):
                            for d in range(DKB):
                                x = turn(bank_r[0][:, 256 * half + P * d:256 * half + P * d + P],
                                         st_k[:, d, half].rearrange("p c n -> p (c n)"))
                        x.then_inc(ks_done.sem, 1)
                    if i in (11, 13):
                        pe.wait_ge(q_l.sem, q_l.at(h))
                        pe.wait_ge(k_l.sem, k_l.at(h))
                        if i == 13:
                            pe.wait_ge(ks_made.sem, ks_made.at(h))
                        for m in ((0, 1), (2,))[(i - 11) // 2]:
                            (t0, rows), (c0, n), bank = KEY[m], SC[m], bank_r[(1, 2, 0)[m]]
                            for d in range(DKB):
                                x = three(bank[0:rows, 0:n], kt_hi[:, d, t0:t0 + rows], kt_lo[:, d, t0:t0 + rows],
                                          q_hi[:, d, c0:c0 + n], q_lo[:, d, c0:c0 + n], d == 0, d == DKB - 1)
                            x.then_inc(sc_done.sem, 1)
                    if i == 16:
                        pe.wait_ge(p_act.sem, p_act.at(h, 4))
                        pe.wait_ge(a_f.sem, a_f.at(h, 3))
                        for m, (t0, rows) in enumerate(KEY):
                            for d in range(DVB):
                                x = turn(bank_r[m][0:rows, P * d:P * d + P], v_t[:, d, t0:t0 + rows])
                            x.then_inc(vt_done.sem, 1)
                    if i == 17:
                        pe.wait_ge(sv_l.sem, sv_l.at(h, DVB))
                        pe.wait_ge(kn_l.sem, kn_l.at(h, 3))
                        for half in range(2):
                            for d in range(DVB):
                                x = turn(bank_r[3 + half][:, P * d:P * d + P],
                                         st_v[:, d, half].rearrange("p c n -> p (c n)"))
                            x.then_inc(vs_done.sem, 1)
                    if i == 18:
                        pe.wait_ge(vn_l.sem, vn_l.at(h, 3))
                        pe.wait_ge(a_l.sem, a_l.at(h, 3))
                        for t in range(2):
                            rows = QRY[t][1]
                            for m in range(t + 1):
                                at = A_AT[m] + QRY[t][0] - SC[m][0]
                                x = three(bank_r[t][0:rows, :], a_hi[:, at:at + rows], a_lo[:, at:at + rows],
                                          v_hi[:, m, :], v_lo[:, m, :], m == 0, m == t)
                            x.then_inc(y_done.sem, 1)
                    if i == 23:
                        y_turn(3)
                    if i in (22, 23):
                        d = i - 22
                        if d:
                            pe.wait_ge(st_read.sem, st_read.at(h, 1))
                        for m in range(3):
                            rows = KEY[m][1]
                            c = slice(P * d, P * d + P)
                            x = three(bank_q[:, :], k_hi[0:rows, m, c], k_lo[0:rows, m, c],
                                      v_hi[0:rows, m, :], v_lo[0:rows, m, :], m == 0, m == 2)
                        x.then_inc(st_done.sem, 1)
                    for t in QS_AT.get(i, ()):
                        b, d = t // 2, t % 2
                        pe.wait_ge(s_l.sem, s_l.at(h, t + 1))
                        if t == 0:
                            pe.wait_ge(qz_l.sem, qz_l.at(h))
                            pe.wait_ge(st_read.sem, st_read.at(h, 0))
                        qb = qz[:, d, P * b:P * b + P]
                        mm(bank_q[:, :], qb, s_hi[:, t % 2, :], start=(t == 0), stop=False)
                        x = mm(bank_q[:, :], qb, s_lo[:, t % 2, :], start=False, stop=(t == 15))
                        x.then_inc(s_q.sem, 1)
                    if i == 19:
                        rows = QRY[2][1]
                        o = bank_r[2][0:rows, :]
                        pe.wait_ge(yf_l.sem, yf_l.at(h))
                        mm(o, fold[:, :], y_f[:, 0, :], start=True, stop=False)
                        mm(o, fold[:, :], y_f[:, 1, :], start=False, stop=False)
                        for m in range(3):
                            at = A_AT[m] + QRY[2][0] - SC[m][0]
                            kr = KEY[m][1]
                            x = three(o, a_hi[0:kr, at:at + rows], a_lo[0:kr, at:at + rows],
                                      v_hi[0:kr, m, :], v_lo[0:kr, m, :], False, m == 2)
                        x.then_inc(y_done.sem, 1)
                    for back, t in due(KV_AT, i, first):
                        kv_multiply(h, t, back)
                    if i == 22:
                        y_turn(0, 1, 2)

                def out(i):
                    c = i - 24
                    wh = w_hi[:, i % SPL, :].rearrange("p (k n) -> p k n", k=DVB)
                    wl = w_lo[:, i % SPL, :].rearrange("p (k n) -> p k n", k=DVB)
                    pe.wait_ge(w_h.sem, w_h.at(h, i + 1))
                    for e in range(2):
                        g = 12 + 2 * c + e
                        if g < 14:
                            pe.wait_ge(p_act.sem, p_act.at(h, g - 5))
                        else:
                            pe.wait_ge(p_dve.sem, p_dve.at(h, g - 9))
                        for k in range(DVB):
                            if c == 0 and e == 0:
                                pe.wait_ge(z_l.sem, z_l.at(h, k + 1))
                            x = mm(bank_p[e][:, 0:N], wh[:, k, P * e:P * e + P], z_hi[:, k, :], start=(k == 0), stop=False)
                            x = mm(bank_p[e][:, 0:N], wh[:, k, P * e:P * e + P], z_lo[:, k, :], start=False, stop=False)
                    x.then_inc(w_hu.sem, 1)
                    pe.wait_ge(w_l.sem, w_l.at(h, i + 1))
                    for e in range(2):
                        for k in range(DVB):
                            x = mm(bank_p[e][:, 0:N], wl[:, k, P * e:P * e + P], z_hi[:, k, :], start=False, stop=(k == DVB - 1))
                        x.then_inc((o_even if e == 0 else w_lu).sem, 1)

                for i in range(24):
                    g, kept = i // 2, i < 4 or i >= 16
                    if i % 2 == 0:
                        if g < 6:
                            pe.wait_ge(p_dve.sem, p_dve.at(h, g - 1))
                        else:
                            pe.wait_ge(p_act.sem, p_act.at(h, g - 5))
                    c0, k0 = (CUT if kept else 0), 8 * (i % 2)

                    def ready(k):
                        pe.wait_ge(x_l.sem, (k0 + k) * XC // KT + 1)

                    proj(0, h, CPH, i, bank_p[g % 2], T - c0, lambda k: xh[:, k0 + k, c0:T],
                         lambda k: xl[:, k0 + k, c0:T], i % 2 == 0, i % 2 == 1, ready if first and i < 2 else None)
                    side(i)
                for i in range(24, CPH):
                    out(i)
                    side(i)
                    if last and i == 28:
                        first_mean(0)

            head(0, True)
            with pe.Fori(1, HEADS - 1) as h:
                head(h, False)
            head(HEADS - 1, False, True)

            def norm(n, early=False):
                mean, sq = bank_r[0][:, 2 * n:N], bank_r[1][:, 2 * n:N]

                def squares(ks):
                    for k in ks:
                        pe.wait_ge(n_sq[n].sem, k + 1)
                        mm(sq, ones, cols(ln_x[:, k % TURN], n), start=False, stop=(k == KT - 1)).then_inc(n_qp[n].sem, 1)

                def means(ks):
                    for k in ks:
                        pe.wait_ge(*sums_read(n, k))
                        x = mm(mean, ones, blk(k, n), start=False, stop=(k == KT - 1))
                    return x

                def start():
                    pe.wait_ge(n_qs[n].sem, n_qs[n].at(0, SQS[n]))
                    mm(sq, ones, cols(ln_qs, n), start=True, stop=False)
                    squares(range(SQS[n], SUMS))
                    pe.wait_ge(n_su[n].sem, SUMS)
                    mm(mean, ones, cols(ln_su, n), start=True, stop=False)

                if n == 0:
                    start()
                    means(range(SUMS, KT)).then_inc(n_mean[n].sem, 1)
                    squares(range(SUMS, KT))
                elif early:
                    start()
                    means(range(SUMS, KT - 1))
                else:
                    squares(range(SUMS, KT - 1))
                    means((KT - 1,)).then_inc(n_mean[n].sem, 1)
                    squares((KT - 1,))

            norm(0)

            def conv(j, at, first):
                def group(i):
                    return (0, 1, 0, 1, 0, 0, 1, 1)[i], 8 * (0, 0, 1, 1, 0, 1, 0, 1)[i]

                for i in range(CPE):
                    bank, k0 = group(i)
                    bank, c0 = bank_p[bank], (CUT if i < 4 else META)
                    if i in (0, 1, 4, 6) and not (first and i < 4):
                        if i == 0:
                            pe.wait_ge(c_z.sem, c_z.at(j, 0))
                        if i == 1:
                            pe.wait_ge(c_b.sem, c_b.at(j, 0))
                        if i == 4:
                            pe.wait_ge(c_c.sem, c_c.at(j))
                        if i == 6:
                            pe.wait_ge(c_v.sem, c_v.at(j, 2))

                    def ready(k):
                        pe.wait_ge(n_l[0].sem, k0 + k + 1)

                    proj(HEAD_CH, at, CPE, i, bank, T - c0, lambda k: xh[:, k0 + k, c0:T],
                         lambda k: xl[:, k0 + k, c0:T], i in (0, 1, 4, 6), i in (2, 3, 5, 7),
                         ready if first and i in (0, 2) else None)
                    if first:
                        for back, t in due(KV_AT, i, last=True):
                            kv_multiply(HEADS, t, back)

            conv(0, 0, True)
            with pe.Fori(1, NE) as j:
                conv(j, j, False)

            def out_conv(j, first=False):
                for i in range(4):
                    g, k0 = i // 2, 8 * (i % 2)
                    if i % 2 == 0 and not first:
                        pe.wait_ge(o_read.sem, o_read.at(j, g - 1))

                    def ready(k):
                        pe.wait_ge(c_ml.sem, k0 + k + 1)

                    proj(HEAD_CH + CONV_CH, j, 4, i, bank_p[g % 2], NOUT, lambda k: m_hi[:, k0 + k, :],
                         lambda k: m_lo[:, k0 + k, :], i % 2 == 0, i % 2 == 1, ready if first and i < 2 else None)
                    if i == 0 and isinstance(j, int) and j == 2:
                        first_mean(1)
                    if i == 2 and isinstance(j, int) and j == OUT_CH // 4 - 1:
                        norm(1, True)

            pe.wait_ge(c_z.sem, c_z.at(NE - 1))
            pe.wait_ge(c_b.sem, c_b.at(NE - 1))
            out_conv(0, True)
            for j in range(1, 3):
                out_conv(j)
            with pe.Fori(3, OUT_CH // 4 - 1) as j:
                out_conv(j)
            out_conv(OUT_CH // 4 - 1)
            norm(1)


def head_tables():
    pos = np.concatenate([np.arange(PROMPT), np.tile(PAST + np.arange(DSEQ), NB)]).astype(np.float32)
    e = -np.arange(P, dtype=np.float32) * np.float32(2) / np.float32(DK)
    ang = (pos[None, :] * (10000.0 ** e.astype(np.float64)).astype(np.float32)[:, None]).astype(np.float64)
    trig = np.stack([np.cos(ang), np.sin(ang)], 1).astype(np.float32)
    lg = np.log1p(-np.exp2(-5.0 - np.arange(HEADS)))
    tok = np.arange(T)
    samp = np.where(tok < PROMPT, -1, (tok - PROMPT) // DSEQ)
    inner = np.where(tok < PROMPT, tok, (tok - PROMPT) % DSEQ)
    tables = np.zeros((HEADS, P, TAB + HEADS), np.float32)
    for h in range(HEADS):
        for m, (t0, rows) in enumerate(KEY):
            c0, n = SC[m]
            keys, qs = tok[t0:t0 + rows], tok[CUT + c0:CUT + c0 + n]
            diff = inner[qs][None, :] - inner[keys][:, None]
            ok = (samp[qs][None, :] == samp[keys][:, None]) & (diff >= 0)
            tables[h, 0:rows, M_AT[m]:M_AT[m] + n] = np.where(ok, np.exp(np.maximum(diff, 0) * lg[h]), 0) * DK ** -0.5
        tables[h, :, QD_AT:QD_AT + NSAMP] = np.exp((inner[PROMPT:] + 1) * lg[h]) * DK ** -0.5
        last = np.where(samp < 0, PROMPT - 1, DSEQ - 1)
        tables[h, :, KD_AT:KD_AT + T] = np.exp((last - inner) * lg[h])
        tables[:, :, TAB + h] = np.exp(DSEQ * lg[h])
    con = np.zeros((P, 3 * P + 8), np.float32)
    con[:, 0:P] = np.eye(P)
    con[:, P:2 * P] = 1.0 / D
    for j in range(NSAMP):
        con[[j, NSAMP + j], 2 * P + META + j] = 1.0
    con[0:META, 3 * P] = 1.0
    for b in range(4):
        con[:, 3 * P + 1 + b] = (np.arange(P) % 32) // DSEQ == b
    return tables, trig, con


def kernel(x_prompt, x_sample, state_ret, state_conv, meta, w_ret_in, w_ret_out,
           w_conv_in, conv_w, w_conv_out, ln_g, ln_b):
    import concourse.bacc as bacc
    from concourse.bass_utils import run_bass_kernel_spmd

    A = np.asarray
    tables, trig, con = head_tables()
    x = np.concatenate([A(meta), A(x_prompt)[0], A(x_sample).reshape(NSAMP, D)], 0)

    def blocks(wm, rows):
        k, c = wm.shape
        t = wm.reshape(k // (rows * P), rows, P, c // P, P)
        return t.transpose(3, 0, 2, 1, 4).reshape(c // P, k // (rows * P), P, rows * P)

    w_in = A(w_ret_in)[0]
    qk = HEADS * DK
    b = blocks(w_in, 8)
    nq, nv = qk // P, HEADS * DVB
    parts = []
    for at, n in ((0, DKB), (nq, DKB), (2 * nq, DVB), (2 * nq + nv, DVB)):
        parts.append(b[at:at + HEADS * n].reshape(HEADS, n * 2, P, HALF))
    wo = A(w_ret_out)[0].reshape(HEADS, DVB, P, KT // 2, 2 * P).transpose(0, 3, 2, 1, 4)
    parts.append(wo.reshape(HEADS, 8, P, HALF))
    w_head = np.concatenate(parts, 1)
    bc = blocks(A(w_conv_in)[0], 8).reshape(4, NE, 2, P, HALF)
    w_conv = np.stack([bc[1][:, 0], bc[2][:, 0], bc[1][:, 1], bc[2][:, 1],
                       bc[3][:, 0], bc[3][:, 1], bc[0][:, 0], bc[0][:, 1]], 1)
    w_cout = blocks(A(w_conv_out)[0], 8).reshape(OUT_CH // 4, 4, P, HALF)
    ins = {
        "x_t": x.reshape(T, KT, P).transpose(2, 1, 0),
        "w_head": w_head, "w_conv": w_conv, "w_cout": w_cout,
        "s_in": A(state_ret)[0].reshape(NB, HEADS, DKB, P, DV).transpose(0, 1, 3, 2, 4),
        "tables": tables, "trig": trig, "consts": con,
        "lnp": np.stack([A(ln_g), A(ln_b)]).reshape(2, 2, KT, P).transpose(3, 0, 1, 2),
        "cw": A(conv_w)[0].reshape(WIDTH, NE, P).transpose(2, 1, 0),
        "cs_in": A(state_conv)[0].reshape(NB, 2, NE, P).transpose(3, 2, 0, 1),
    }
    outs = {
        "y_t": [P, KT, NOUT], "s_prompt": [HEADS, P, DKB, DV], "s_out": [NB, HEADS, P, DKB, DV],
        "cs_out": [P, NE, 1 + NB, 2],
    }
    nc = bacc.Bacc("TRN2", target_bir_lowering=False, num_devices=1)
    ins = {k: np.ascontiguousarray(v) for k, v in ins.items()}
    aps = {k: nc.dram_tensor(k, v.shape, F32, kind="ExternalInput").ap() for k, v in ins.items()}
    aps |= {k: nc.dram_tensor(k, s, F32, kind="ExternalOutput").ap() for k, s in outs.items()}
    hybrid_step(nc, **aps)
    r = run_bass_kernel_spmd(nc, [ins], core_ids=[0]).results[0]
    y = r["y_t"].transpose(2, 1, 0).reshape(NOUT, D)
    sp = r["s_prompt"].transpose(0, 2, 1, 3).reshape(1, 1, HEADS, DK, DV)
    ss = r["s_out"].transpose(0, 1, 3, 2, 4).reshape(1, NB, HEADS, DK, DV)
    cs = r["cs_out"].transpose(2, 3, 1, 0).reshape(1 + NB, 2, D)
    return (y[:SEQ].reshape(1, SEQ, D), y[SEQ:].reshape(NB, DSEQ, D), sp, ss, cs[None, 0:1], cs[None, 1:])
```
